# Optimizing a Trainium2 kernel written in Bass

```python
import jax, jax.numpy as jnp
from jax import lax
import numpy as np

D_MODEL = 2048
BATCH = 1
SEQ = 256
DEPTH = 1

CTX_LEN = 256
GRID_W = 64

MLA_HEADS = 8
QK_NOPE_DIM = 128
QK_ROPE_DIM = 64
V_HEAD_DIM = 128
Q_LORA_RANK = 512
KV_LORA_RANK = 256
MLA_WIDTH = MLA_HEADS * V_HEAD_DIM
ATTN_SCALE = (QK_NOPE_DIM + QK_ROPE_DIM) ** -0.5
ROPE_BASE = 10000.0
Q_BLOCK = 128

CONV_WIDTH = D_MODEL - MLA_WIDTH
CONV_K = 3

Q_END = Q_LORA_RANK
KV_END = Q_END + KV_LORA_RANK
KR_END = KV_END + QK_ROPE_DIM
IN_COLS = KR_END + 3 * CONV_WIDTH

N_EXPERTS = 32
N_EXPERT_GROUPS = 4
TOPK_GROUPS = 2
TOP_K = 4
EXPERT_FF = 256
SHARED_FF = 512
ROUTED_SCALE = 2.5

N_MOD = 6
NORM_EPS = 1e-6

kernel_name = "hybrid_mla_shortconv_moe_dit_block"

def rmsnorm(x, g):
    xf = x.astype(jnp.float32)
    y = xf * lax.rsqrt(jnp.mean(xf * xf, axis=-1, keepdims=True) + NORM_EPS)
    return (y * g.astype(jnp.float32)).astype(x.dtype)

def modulated_norm(x, g, shift, scale):
    return rmsnorm(x, g) * (1 + scale) + shift

def axial_rope_tables(rows):
    row = jnp.repeat(jnp.arange(rows, dtype=jnp.float32), GRID_W)
    col = jnp.tile(jnp.arange(GRID_W, dtype=jnp.float32), rows)
    nf = QK_ROPE_DIM // 4
    inv = ROPE_BASE ** (-jnp.arange(nf, dtype=jnp.float32) / nf)
    ang = jnp.concatenate([row[:, None] * inv, col[:, None] * inv], axis=-1)
    return jnp.cos(ang), jnp.sin(ang)

def apply_axial_rope(x, cos, sin):
    bshape = (cos.shape[0],) + (1,) * (x.ndim - 3) + (cos.shape[-1],)
    cos = cos.reshape(bshape).astype(x.dtype)
    sin = sin.reshape(bshape).astype(x.dtype)
    nf = QK_ROPE_DIM // 4
    half = QK_ROPE_DIM // 2

    def rot(v, cs, sn):
        v1, v2 = v[..., :nf], v[..., nf:]
        return jnp.concatenate([v1 * cs - v2 * sn, v2 * cs + v1 * sn], axis=-1)

    return jnp.concatenate([rot(x[..., :half], cos[..., :nf], sin[..., :nf]),
                            rot(x[..., half:], cos[..., nf:], sin[..., nf:])], axis=-1)

def mla_query(q_a, p, rope):
    q = rmsnorm(q_a, p["q_a_norm"]) @ p["w_q_b"]
    q = q.reshape(q.shape[:-1] + (MLA_HEADS, QK_NOPE_DIM + QK_ROPE_DIM))
    qn, qr = q[..., :QK_NOPE_DIM], q[..., QK_NOPE_DIM:]
    if rope is not None:
        qr = apply_axial_rope(qr, *rope)
    return qn, qr

def mla_kv(kv_a, k_rope, p, rope):
    kv = rmsnorm(kv_a, p["kv_a_norm"]) @ p["w_kv_b"]
    kv = kv.reshape(kv.shape[:-1] + (MLA_HEADS, QK_NOPE_DIM + V_HEAD_DIM))
    kn, v = kv[..., :QK_NOPE_DIM], kv[..., QK_NOPE_DIM:]
    kr = apply_axial_rope(k_rope, *rope) if rope is not None else k_rope
    return kn, kr, v

def mla_attention(qn, qr, kn, kr, v):
    b, n = qn.shape[0], qn.shape[1]
    nb = n // Q_BLOCK

    def block(q):
        qn_b, qr_b = q
        s = (jnp.einsum("bqhd,bkhd->bhqk", qn_b, kn)
             + jnp.einsum("bqhr,bkr->bhqk", qr_b, kr)) * ATTN_SCALE
        pr = jax.nn.softmax(s.astype(jnp.float32), axis=-1).astype(v.dtype)
        return jnp.einsum("bhqk,bkhd->bqhd", pr, v)

    qn_blocks = qn.reshape(b, nb, Q_BLOCK, MLA_HEADS, QK_NOPE_DIM).swapaxes(0, 1)
    qr_blocks = qr.reshape(b, nb, Q_BLOCK, MLA_HEADS, QK_ROPE_DIM).swapaxes(0, 1)
    o = lax.map(block, (qn_blocks, qr_blocks))
    return o.swapaxes(0, 1).reshape(b, n, MLA_WIDTH)

def gated_short_conv(g_b, g_c, h, w_conv):
    u = g_c * h
    y = lax.conv_general_dilated(u, w_conv[:, None, :], window_strides=(1,),
                                 padding=((CONV_K // 2, CONV_K // 2),),
                                 dimension_numbers=("NWC", "WIO", "NWC"),
                                 feature_group_count=CONV_WIDTH)
    return g_b * y

def merge_head_groups(o_mla, o_conv, p):
    o = jnp.concatenate([rmsnorm(o_mla, p["o_norm_mla"]), rmsnorm(o_conv, p["o_norm_conv"])], axis=-1)
    return o @ p["w_out"]

def route(xf, w_router, bias):
    t = xf.shape[0]
    s = jax.nn.sigmoid((xf @ w_router).astype(jnp.float32))
    sel = s + bias.astype(jnp.float32)
    grp = sel.reshape(t, N_EXPERT_GROUPS, N_EXPERTS // N_EXPERT_GROUPS)
    gscore = lax.top_k(grp, 2)[0].sum(-1)
    _, gidx = lax.top_k(gscore, TOPK_GROUPS)
    gmask = jax.nn.one_hot(gidx, N_EXPERT_GROUPS, dtype=jnp.float32).sum(-2) > 0
    emask = jnp.repeat(gmask, N_EXPERTS // N_EXPERT_GROUPS, axis=-1)
    _, idx = lax.top_k(jnp.where(emask, sel, -jnp.inf), TOP_K)
    w = jnp.take_along_axis(s, idx, axis=-1)
    w = w / jnp.sum(w, axis=-1, keepdims=True) * ROUTED_SCALE
    return idx, w

def moe_ffn(h, p):
    shp = h.shape
    xf = h.reshape(-1, shp[-1])
    idx, w = route(xf, p["w_router"], p["router_bias"])
    comb = jnp.sum(jax.nn.one_hot(idx, N_EXPERTS, dtype=jnp.float32) * w[..., None], axis=1)
    g = jnp.einsum("td,edf->tef", xf, p["w_exp_gate"])
    u = jnp.einsum("td,edf->tef", xf, p["w_exp_up"])
    a = jax.nn.silu(g) * u * comb[..., None].astype(xf.dtype)
    routed = jnp.einsum("tef,efd->td", a, p["w_exp_down"])
    shared = (jax.nn.silu(xf @ p["w_sh_gate"]) * (xf @ p["w_sh_up"])) @ p["w_sh_down"]
    return (routed + shared).reshape(shp)

def context_update(h_c, nc, kn_c, kr_c, v_c, mods_c, p):
    _, _, ga_c, sf_c, scf_c, gf_c = mods_c
    w_in = p["w_in"]
    qn_c, qr_c = mla_query(nc @ w_in[:, :Q_END], p, None)
    o_mla = mla_attention(qn_c, qr_c, kn_c, kr_c, v_c)
    g_b, g_c, hh = jnp.split(nc @ w_in[:, KR_END:], 3, axis=-1)
    o_conv = gated_short_conv(g_b, g_c, hh, p["conv_w"])
    h_c = h_c + ga_c * merge_head_groups(o_mla, o_conv, p)
    return h_c + gf_c * moe_ffn(modulated_norm(h_c, p["ffn_norm"], sf_c, scf_c), p)

def setup_inputs(seed: int = 0) -> dict:
    key = jax.random.key(seed)
    ks = jax.random.split(key, 26)
    f32 = jnp.float32

    def nrm(k, shape, s):
        return jax.random.normal(k, shape, f32) * s

    def gain(k, shape):
        return 1.0 + 0.02 * jax.random.normal(k, shape, f32)

    d = D_MODEL
    return {
        "x": nrm(ks[0], (BATCH, SEQ, d), 1.0),
        "c": nrm(ks[1], (BATCH, d), 1.0),
        "ctx": nrm(ks[2], (BATCH, CTX_LEN, d), 1.0),
        "c_ctx": nrm(ks[3], (d,), 1.0),
        "w_mod": nrm(ks[4], (DEPTH, d, N_MOD * d), 0.5 * d ** -0.5),
        "b_mod": nrm(ks[5], (DEPTH, N_MOD * d), 0.02),
        "attn_norm": gain(ks[6], (DEPTH, d)),
        "w_in": nrm(ks[7], (DEPTH, d, IN_COLS), d ** -0.5),
        "q_a_norm": gain(ks[8], (DEPTH, Q_LORA_RANK)),
        "w_q_b": nrm(ks[9], (DEPTH, Q_LORA_RANK, MLA_HEADS * (QK_NOPE_DIM + QK_ROPE_DIM)), Q_LORA_RANK ** -0.5),
        "kv_a_norm": gain(ks[10], (DEPTH, KV_LORA_RANK)),
        "w_kv_b": nrm(ks[11], (DEPTH, KV_LORA_RANK, MLA_HEADS * (QK_NOPE_DIM + V_HEAD_DIM)), KV_LORA_RANK ** -0.5),
        "conv_w": nrm(ks[12], (DEPTH, CONV_K, CONV_WIDTH), CONV_K ** -0.5),
        "o_norm_mla": gain(ks[13], (DEPTH, MLA_WIDTH)),
        "o_norm_conv": gain(ks[14], (DEPTH, CONV_WIDTH)),
        "w_out": nrm(ks[15], (DEPTH, d, d), d ** -0.5),
        "ffn_norm": gain(ks[16], (DEPTH, d)),
        "w_router": nrm(ks[17], (DEPTH, d, N_EXPERTS), d ** -0.5),
        "router_bias": nrm(ks[18], (DEPTH, N_EXPERTS), 0.01),
        "w_exp_gate": nrm(ks[19], (DEPTH, N_EXPERTS, d, EXPERT_FF), d ** -0.5),
        "w_exp_up": nrm(ks[20], (DEPTH, N_EXPERTS, d, EXPERT_FF), d ** -0.5),
        "w_exp_down": nrm(ks[21], (DEPTH, N_EXPERTS, EXPERT_FF, d), EXPERT_FF ** -0.5),
        "w_sh_gate": nrm(ks[22], (DEPTH, d, SHARED_FF), d ** -0.5),
        "w_sh_up": nrm(ks[23], (DEPTH, d, SHARED_FF), d ** -0.5),
        "w_sh_down": nrm(ks[24], (DEPTH, SHARED_FF, d), SHARED_FF ** -0.5),
        "final_norm": gain(ks[25], (d,)),
    }

def reference(x, c, ctx, c_ctx, w_mod, b_mod, attn_norm, w_in, q_a_norm, w_q_b, kv_a_norm, w_kv_b,
              conv_w, o_norm_mla, o_norm_conv, w_out, ffn_norm, w_router, router_bias,
              w_exp_gate, w_exp_up, w_exp_down, w_sh_gate, w_sh_up, w_sh_down, final_norm):
    n_lat = x.shape[1]
    ROWS = n_lat // GRID_W
    rope = axial_rope_tables(ROWS)
    silu_c = jax.nn.silu(c)
    silu_cc = jax.nn.silu(c_ctx)[None, :]
    h_x, h_c = x, ctx
    for l in range(DEPTH):
        p = {"w_in": w_in[l], "q_a_norm": q_a_norm[l], "w_q_b": w_q_b[l], "kv_a_norm": kv_a_norm[l],
             "w_kv_b": w_kv_b[l], "conv_w": conv_w[l], "o_norm_mla": o_norm_mla[l],
             "o_norm_conv": o_norm_conv[l], "w_out": w_out[l], "ffn_norm": ffn_norm[l],
             "w_router": w_router[l], "router_bias": router_bias[l], "w_exp_gate": w_exp_gate[l],
             "w_exp_up": w_exp_up[l], "w_exp_down": w_exp_down[l], "w_sh_gate": w_sh_gate[l],
             "w_sh_up": w_sh_up[l], "w_sh_down": w_sh_down[l]}
        mods_x = jnp.split((silu_c @ w_mod[l] + b_mod[l])[:, None, :], N_MOD, axis=-1)
        mods_c = jnp.split((silu_cc @ w_mod[l] + b_mod[l])[:, None, :], N_MOD, axis=-1)
        sa_x, sca_x, ga_x, sf_x, scf_x, gf_x = mods_x

        nc = modulated_norm(h_c, attn_norm[l], mods_c[0], mods_c[1])
        pc = nc @ w_in[l][:, Q_END:KR_END]
        kn_c, kr_c, v_c = mla_kv(pc[..., :KV_LORA_RANK], pc[..., KV_LORA_RANK:], p, None)

        nx = modulated_norm(h_x, attn_norm[l], sa_x, sca_x)
        q_a, kv_a, k_rope, g_b, g_c, hh = jnp.split(
            nx @ w_in[l], [Q_END, KV_END, KR_END, KR_END + CONV_WIDTH, KR_END + 2 * CONV_WIDTH], axis=-1)
        qn, qr = mla_query(q_a, p, rope)
        kn_x, kr_x, v_x = mla_kv(kv_a, k_rope, p, rope)
        o_mla = mla_attention(qn, qr,
                              jnp.concatenate([kn_c, kn_x], axis=1),
                              jnp.concatenate([kr_c, kr_x], axis=1),
                              jnp.concatenate([v_c, v_x], axis=1))
        o_conv = gated_short_conv(g_b, g_c, hh, p["conv_w"])
        h_new = h_x + ga_x * merge_head_groups(o_mla, o_conv, p)
        h_new = h_new + gf_x * moe_ffn(modulated_norm(h_new, p["ffn_norm"], sf_x, scf_x), p)

        if l + 1 < DEPTH:
            h_c = context_update(h_c, nc, kn_c, kr_c, v_c, mods_c, p)
        h_x = h_new
    return rmsnorm(h_x, final_norm)


_drawn_inputs = setup_inputs


def setup_inputs(seed=0):
    import zlib

    import numpy as np

    out = dict(_drawn_inputs(seed))
    spreads = {}
    factors = {'attn_norm': 3.251,
     'q_a_norm': 7.341,
     'o_norm_mla': 3.425,
     'o_norm_conv': 3.056,
     'final_norm': 2.717}
    for name, (base, spread) in spreads.items():
        noise = np.random.default_rng([zlib.crc32(name.encode()), seed]).standard_normal(out[name].shape)
        drawn = base * np.exp(spread * noise) if base else spread * noise
        out[name] = __import__('jax').numpy.asarray(drawn.astype(out[name].dtype))
    for name, factor in factors.items():
        out[name] = (out[name] * factor).astype(out[name].dtype)
    return out
```

```python
from contextlib import ExitStack

import numpy as np

import concourse.bass as bass
from concourse import mybir
from concourse.alu_op_type import AluOpType as ALU

ACT = mybir.ActivationFunctionType
AX = mybir.AxisListType
F32 = mybir.dt.float32
BF16 = mybir.dt.bfloat16
I32 = mybir.dt.int32

P = 128
D = 2048
T = 256
KC = D // P
HEADS, NOPE, ROPE, VD = 8, 128, 64, 128
QL, KVL = 512, 256
CW = D - HEADS * VD
KR0 = QL + KVL
CONV0 = KR0 + ROPE
NE, NG, FF = 32, 4, 256
EPS = 1e-6
SCALE = float(NOPE + ROPE) ** -0.5
GRID_W = 64
ROUTED_SCALE = 2.5
TOP_K = 4
SLOTS = 64
PASSES = T // SLOTS
BIG = 1e30

C_ID, C_ONE, C_ROTQ, C_DUP, C_ROTK = 0, 128, 256, 384, 512
C_COS, C_SIN, C_SEL2, C_SUM4, C_TRI, C_IOTA, C_LOW, C_HALF = 640, 896, 1152, 1160, 1192, 1320, 1384, 1400
NCONST = 1401

V_AN, V_QN, V_KN, V_CW, V_OM, V_OC, V_FN = 0, 16, 20, 22, 46, 54, 62
NVEC = 78


def constants():
    c = np.zeros((P, NCONST), np.float32)
    c[:, C_ID:C_ID + P] = np.eye(P)
    c[:, C_ONE:C_ONE + P] = 1.0
    for j in range(P):
        w = j % 32
        source, sign = (j + 16, -1.0) if w < 16 else (j - 16, 1.0)
        c[source, C_ROTQ + j] = sign
        for half in range(2):
            c[64 * half + j % 64, C_DUP + j] = 1.0
            c[64 * half + source % 64, C_ROTK + j] = sign
    inv = (np.float32(10000.0) ** (-np.arange(16, dtype=np.float32) / np.float32(16))).astype(np.float32)
    token = np.arange(T)
    for j in range(P):
        place = (token // GRID_W if j % 64 < 32 else token % GRID_W).astype(np.float32)
        angle = (place * inv[j % 16]).astype(np.float32)
        c[j, C_COS:C_COS + T] = np.cos(angle)
        c[j, C_SIN:C_SIN + T] = np.sin(angle)
    for q in range(4):
        for v in range(2):
            c[32 * q + v, C_SEL2 + v] = 1.0
        for e in range(32):
            c[32 * q + e, C_SUM4 + e] = 1.0
    c[:, C_TRI:C_TRI + P] = np.triu(np.ones((P, P)), 1)
    c[:, C_IOTA:C_IOTA + SLOTS] = np.arange(SLOTS)
    c[:, C_LOW:C_LOW + NG * NG] = np.tril(np.ones((NG, NG)), -1).ravel()
    c[:, C_HALF] = -0.5
    return c


def block_kernel(nc, x, c, ctx_in, c_ctx, w_mod, b_mod, attn_norm, w_in, q_a_norm, w_q_b, kv_a_norm, w_kv_b,
                 conv_w, o_norm_mla, o_norm_conv, w_out, ffn_norm, w_router, router_bias,
                 w_exp_gate, w_exp_up, w_exp_down, w_sh_gate, w_sh_up, w_sh_down, final_norm, consts, out):
    with ExitStack() as stack:
        def sb(name, shape, dt=F32):
            return stack.enter_context(nc.sbuf_tensor(name, shape, dt))

        def sem(name):
            return stack.enter_context(nc.semaphore(name))

        xres = sb("xres", [P, 2, D])
        ring = sb("ring", [P, 6 * 4096])
        nreg = sb("nreg", [P, 8192])
        qkv = sb("qkv", [P, 2048])
        krT = sb("krT", [P, 2 * T])
        krs = sb("krs", [P, 2 * T])
        qnT = sb("qnT", [P, HEADS, T])
        part = sb("part", [P, 2, 512])
        modT = sb("modT", [P, 96, 2])
        csT = sb("csT", [P, KC, 32])
        cst = sb("cst", [P, NCONST])
        kq = sb("kq", [P, 2048])
        conv = sb("conv", [P, 1540])
        hb = sb("hb", [P, 2, D], BF16)
        vrow = sb("vrow", [P, P])
        brow = sb("brow", [P, P])
        crow = sb("crow", [32, P])
        csil = sb("csil", [32, P])
        vecT = sb("vecT", [P, NVEC])
        bT = sb("bT", [P, 96])
        amul = sb("amul", [P, KC, 2])
        amul2 = sb("amul2", [P, KC])
        stat = sb("stat", [P, 16])
        wr = sb("wr", [P, KC, NE])
        rb = sb("rb", [P, NE])
        sig = sb("sig", [P, 2, NE])
        sel = sb("sel", [P, 2, NE])
        mask = sb("mask", [P, 2, NE])
        scan = sb("scan", [P, 2, 2, NE])
        comb = sb("comb", [P, 2, NE])
        rank = sb("rank", [P, PASSES, 2, NE])
        top8 = sb("top8", [P, 10, 8])
        tiny = sb("tiny", [P, 160])
        more = sb("more", [P, NE // 2], I32)
        pick = sb("pick", [P, 2, 2 * SLOTS], BF16)

        slot = [ring[:, 4096 * s:4096 * (s + 1)] for s in range(6)]
        ctxs = slot[3].rearrange("p (t d) -> p t d", t=2)
        xs = slot[4].rearrange("p (t d) -> p t d", t=2)
        mslot = [ring[:, 3 * 4096 + 2048 * s:3 * 4096 + 2048 * (s + 1)].rearrange("p (k n) -> p k n", k=4)
                 for s in range(4)]
        oT = slot[5].rearrange("p (c t) -> p c t", c=KC)
        squ = slot[5][:, 0:2048]
        knT = slot[3].rearrange("p (h t) -> p h t", h=HEADS)
        vtok = slot[4].rearrange("p (k n) -> p k n", k=4)
        xh = slot[3].rearrange("p (t d) -> p t d", t=2)
        gu = ring[:, 0:16384].rearrange("p (q u g k n) -> p q u g k n", q=4, u=2, g=2, k=4)
        down = [slot[4 + u].rearrange("p (k n) -> p k n", k=2) for u in range(2)]

        wkr = kq[:, 0:1024].rearrange("p (k n) -> p k n", k=KC)
        rowq, rowkv = kq[:, 0:T], kq[:, T:3 * T]
        qrT = kq[:, 1024:2048].rearrange("p (h t) -> p h t", h=HEADS // 2)
        gcs = conv[:, 0:512].rearrange("p (m t) -> p m t", m=2)
        upad = conv[:, 512:1028].rearrange("p (m t) -> p m t", m=2)
        ycv = conv[:, 1028:1540].rearrange("p (m t) -> p m t", m=2)
        pickw = conv[:, 0:256].rearrange("p (t s) -> p t s", t=2)
        pickT = conv[:, 256:512]
        act = conv[:, 512:1024].rearrange("p (a f) -> p a f", a=2)
        actT = conv[:, 1024:1280].rearrange("p (k s) -> p k s", k=2)
        qaT = qkv[:, 0:1024].rearrange("p (c t) -> p c t", c=4)
        kvT = qkv[:, 1024:2048].rearrange("p (c t) -> p c t", c=2)
        gfB = qkv[:, :]
        nT = nreg[:, :].rearrange("p (c t) -> p c t", c=KC)
        prob = nreg[:, 0:1024].rearrange("p (b k) -> p b k", b=2)
        pT = nreg[:, 1024:3072].rearrange("p (b k q) -> p b k q", b=2, k=4)
        gaB = nreg[:, 3072:5120]
        sqr = nreg[:, 5120:6144].rearrange("p (b t) -> p b t", b=4)
        diag = nreg[:, 6144:7168].rearrange("p (b n) -> p b n", b=2)
        rconv = nreg[:, 7168:7424]
        rmla = nreg[:, 7424:7680]
        qraw = nreg[:, 7680:8192].rearrange("p (b t) -> p b t", b=2)
        hT = nreg[:, 0:4096].rearrange("p (c t) -> p c t", c=KC)
        yacc = nreg[:, 4096:8192].rearrange("p (t d) -> p t d", t=2)
        shT = krT[:, :].rearrange("p (k t) -> p k t", k=2)
        shS = krs[:, :].rearrange("p (k t) -> p k t", k=2)
        gainB = slot[0][:, 0:D]
        xg = nreg[:, 0:2048].rearrange("p (c s) -> p c s", c=KC)
        ye = nreg[:, 2048:4096]
        parts = [qnT[:, :, :].rearrange("p h t -> p (h t)").bitcast(BF16).rearrange("p (t d) -> p t d", t=2),
                 hb[:, :, :], kq[:, :].bitcast(BF16).rearrange("p (t d) -> p t d", t=2)]

        ident, ones = cst[:, C_ID:C_ID + P], cst[:, C_ONE:C_ONE + P]
        cosT, sinT = cst[:, C_COS:C_COS + T], cst[:, C_SIN:C_SIN + T]
        sel2, sum4 = cst[:, C_SEL2:C_SEL2 + 2], cst[:, C_SUM4:C_SUM4 + 32]
        before, iota = cst[:, C_TRI:C_TRI + P], cst[:, C_IOTA:C_IOTA + SLOTS]
        low = cst[:, C_LOW:C_LOW + NG * NG].rearrange("p (a b) -> p a b", a=NG)

        ps = stack.enter_context(nc.psum_tensor("ps", [P, 8, 512], F32))

        small_in, x_in, ctx_ld, wkr_in, router_in, gain_in = (sem("small_in"), sem("x_in"), sem("ctx_ld"), sem("wkr_in"),
                                                     sem("router_in"), sem("gain_in"))
        w_full = [sem(f"w_full{s}") for s in range(6)]
        m_full = [sem(f"m_full{s}") for s in range(4)]
        m_used = [sem(f"m_used{s}") for s in range(4)]
        half_used = sem("half_used")
        zeroed, silu_c, small_T, small_done = sem("zeroed"), sem("silu_c"), sem("small_T"), sem("small_done")
        mod_rows, part_full, mod_cols, modT_done = (sem("mod_rows"), sem("part_full"), sem("mod_cols"),
                                                    sem("modT_done"))
        squares, xs_ready, amul_ready, xT_full, nT_lat, nT_ctx = (sem("squares"), sem("xs_ready"), sem("amul_ready"),
                                                                  sem("xT_full"), sem("nT_lat"), sem("nT_ctx"))
        q_full, q_out, q_sq = sem("q_full"), sem("q_out"), sem("q_sq")
        kv_full, kv_out, kv_sq = sem("kv_full"), sem("kv_out"), sem("kv_sq")
        kr_full, kr_sum, kr_mm, kr_done = (sem("kr_full"), sem("kr_sum"), sem("kr_mm"),
                                                   sem("kr_done"))
        stat_q, stat_kv, q_ready, kv_ready = (sem("stat_q"), sem("stat_kv"),
                                                        sem("q_ready"), sem("kv_ready"))
        conv_full, gc_out, u_out, y_out = sem("conv_full"), sem("gc_out"), sem("u_out"), sem("y_out")
        mods_ready, diag_ready, diag_used, gate_done = (sem("mods_ready"), sem("diag_ready"), sem("diag_used"),
                                                        sem("gate_done"))
        proj_full, proj_act, proj_dve = sem("proj_full"), sem("proj_act"), sem("proj_dve")
        rot_full, qr_ready = sem("rot_full"), sem("qr_ready")
        csq, csq_used, msq, msq_used = sem("csq"), sem("csq_used"), sem("msq"), sem("msq_used")
        oc_ready, om_ready = sem("oc_ready"), sem("om_ready")
        score_full, neg_max, exp_done, p_ready = sem("score_full"), sem("neg_max"), sem("exp_done"), sem("p_ready")
        pT_full, pT_out, o_full, o_out = sem("pT_full"), sem("pT_out"), sem("o_full"), sem("o_out")
        wo_half, wo_full, h_part = sem("wo_half"), sem("wo_full"), sem("h_part")
        hsq, xh_ready, hT_full, hT_act, hT_dve = (sem("hsq"), sem("xh_ready"), sem("hT_full"), sem("hT_act"),
                                                  sem("hT_dve"))
        split_act, split_ready = sem("split_act"), sem("split_ready")
        rt_rows, rt_copied, rt_full, rt_sig, mask_ready, rank_full, rank_ready = (
            sem("rt_rows"), sem("rt_copied"), sem("rt_full"), sem("rt_sig"), sem("mask_ready"), sem("rank_full"),
            sem("rank_ready"))
        sh_gate, sh_up, sh_silu, sh_act, sh_down = (sem("sh_gate"), sem("sh_up"), sem("sh_silu"), sem("sh_act"),
                                                          sem("sh_down"))
        gu_in = [sem(f"gu_in{q}") for q in range(4)]
        gu_used = [sem(f"gu_used{q}") for q in range(4)]
        down_in, down_used = sem("down_in"), [sem(f"down_used{u}") for u in range(2)]
        pick_ready, pickw_ready, gx_full, gx_act, gx_dve, pickT_full, pickT_out = (
            sem("pick_ready"), sem("pickw_ready"), sem("gx_full"), sem("gx_act"), sem("gx_dve"), sem("pickT_full"),
            sem("pickT_out"))
        gu_full, silu_done, act_ready, actT_full, actT_out, dn_full, ye_out, sc_full, y_add = (
            sem("gu_full"), sem("silu_done"), sem("act_ready"), sem("actT_full"), sem("actT_out"), sem("dn_full"),
            sem("ye_out"), sem("sc_full"), sem("y_add"))
        mean_sq, root, mean_wide, root_wide = sem("mean_sq"), sem("root"), sem("mean_wide"), sem("root_wide")
        fin_h, fin_sq, fin_done, stored = sem("fin_h"), sem("fin_sq"), sem("fin_done"), sem("stored")
        v_step = sem("v_step")

        wm = w_mod[0].rearrange("(c p) n -> p c n", p=P)
        wi = w_in[0].rearrange("(c p) n -> p c n", p=P)
        wq = w_q_b[0].rearrange("(c p) n -> p c n", p=P)
        wkv = w_kv_b[0].rearrange("(c p) n -> p c n", p=P)
        wo = w_out[0].rearrange("(c p) n -> p c n", p=P)
        wg = w_exp_gate[0].rearrange("e (c p) n -> p e c n", p=P)
        wu = w_exp_up[0].rearrange("e (c p) n -> p e c n", p=P)
        wd = w_exp_down[0].rearrange("e (c p) n -> p e c n", p=P)
        sg = w_sh_gate[0].rearrange("(c p) n -> p c n", p=P)
        su = w_sh_up[0].rearrange("(c p) n -> p c n", p=P)
        sd = w_sh_down[0].rearrange("(c p) n -> p c n", p=P)

        def k_of(s, k):
            return slot[s].rearrange("p (k n) -> p k n", k=k)

        FIRST = 0
        MOD_SLOTS = [0, 1, 2, 5]
        W_OUT = [(n, half) for n in range(4) for half in (1, 0)]
        USES = 10
        WO_USE = [(j % 3, USES + j // 3 + 1) for j in range(len(W_OUT))]
        SH_USE = [14, 14, 13, 1, 1, 5]

        block = stack.enter_context(nc.Block())

        @block.sync
        def _(sp):
            sp.dma_start(crow[0:KC, :], c.rearrange("b (c p) -> (b c) p", p=P)).then_inc(small_in, 16)
            sp.dma_start(crow[KC:2 * KC, :], c_ctx.rearrange("(c p) -> c p", p=P)).then_inc(small_in, 16)
            sp.dma_start(cst[:, :], consts).then_inc(small_in, 16)
            for at, src in ((V_AN, attn_norm[0]), (V_QN, q_a_norm[0]), (V_KN, kv_a_norm[0]), (V_OM, o_norm_mla[0]),
                            (V_OC, o_norm_conv[0]), (V_FN, ffn_norm[0])):
                n = src.shape[0] // P
                sp.dma_start(vrow[at:at + n, :], src.rearrange("(c p) -> c p", p=P)).then_inc(small_in, 16)
            sp.dma_start(vrow[V_CW:V_CW + 24, :], conv_w[0].rearrange("k (c p) -> (k c) p", p=P)).then_inc(small_in, 16)
            sp.dma_start(brow[0:96, :], b_mod[0].rearrange("(c p) -> c p", p=P)).then_inc(small_in, 16)

            def load_mod(g, u):
                for half in range(2):
                    s = MOD_SLOTS[2 * u + half]
                    sp.dma_start(k_of(s, 8), wm[:, 8 * half:8 * half + 8, bass.ds(g * 512, 512)])\
                      .then_inc(w_full[s], 16)

            load_mod(0, 0)
            sp.dma_start(xres[:, :, :], x[0].rearrange("(t p) d -> p t d", p=P)).then_inc(x_in, 16)
            sp.dma_start(ctxs, ctx_in[0].rearrange("(t p) d -> p t d", p=P)).then_inc(ctx_ld, 16)
            load_mod(1, 1)
            with sp.Fori(1, 4) as i:
                for u in range(2):
                    sp.wait_ge(mod_rows, 2 * i + u - 1)
                    load_mod(2 * i + u, u)

            sp.wait_ge(mod_rows, 7)
            for s in range(2):
                sp.dma_start(k_of(s, KC), wi[:, :, 256 * s:256 * s + 256]).then_inc(w_full[s], 16)
            sp.wait_ge(mod_rows, 8)
            sp.dma_start(k_of(2, KC), wi[:, :, 512:768]).then_inc(w_full[2], 16)
            sp.dma_start(wkr[:, :, :], wi[:, :, KR0:CONV0]).then_inc(wkr_in, 16)

            def load_group(i, u):
                for q in range(4):
                    if q == 3:
                        sp.wait_ge(mod_rows, 4 * i + u + 8)
                    elif not (i is FIRST and u == 0):
                        sp.wait_ge(m_used[q], 4 * i + u)
                    sp.dma_start(mslot[q], wm[:, 4 * q:4 * q + 4, bass.ds((4 * i + u + 8) * 512, 512)])\
                      .then_inc(m_full[q], 16)

            def load_conv(i, s, col):
                sp.dma_start(k_of(s, KC), wi[:, :, bass.ds(col + i * 256, 256)]).then_inc(w_full[s], 16)

            sp.wait_ge(q_full, 2)
            load_conv(0, 0, CONV0 + CW)
            sp.wait_ge(q_full, 4)
            load_conv(0, 1, CONV0 + 2 * CW)
            sp.wait_ge(nT_lat, KC)
            sp.wait_ge(nT_ctx, KC)
            load_group(FIRST, 0)
            load_group(FIRST, 1)
            sp.wait_ge(kv_full, 2)
            load_conv(0, 2, CONV0)
            load_group(0, 2)
            load_group(0, 3)
            with sp.Fori(1, 4) as i:
                sp.wait_ge(conv_full, 6 * i - 4)
                load_conv(i, 0, CONV0 + CW)
                load_group(i, 0)
                sp.wait_ge(conv_full, 6 * i - 2)
                load_conv(i, 1, CONV0 + 2 * CW)
                load_group(i, 1)
                sp.wait_ge(conv_full, 6 * i)
                load_conv(i, 2, CONV0)
                load_group(i, 2)
                load_group(i, 3)

            for s in range(2):
                sp.wait_ge(conv_full, 20 + 2 * s)
                sp.dma_start(slot[s][:, 0:3072].rearrange("p (k n) -> p k n", k=4), wq[:, :, 768 * s:768 * s + 768])\
                  .then_inc(w_full[s], 16)
            sp.wait_ge(conv_full, 24)
            sp.dma_start(k_of(2, 2), wkv).then_inc(w_full[2], 16)
            sp.dma_start(wr[:, :, :], w_router[0].rearrange("(c p) n -> p c n", p=P)).then_inc(router_in, 16)
            sp.dma_start(rb[:, :], router_bias.to_broadcast([P, NE])).then_inc(router_in, 16)

            for j, ((n, half), (s, use)) in enumerate(zip(W_OUT, WO_USE)):
                if j < 3:
                    sp.wait_ge(proj_full, (6, 12, 28)[j])
                elif (j - 3) % 2 == 0:
                    sp.wait_ge(wo_half, (j - 3) // 2 + 1)
                else:
                    sp.wait_ge(wo_full, (j - 3) // 2 + 1)
                sp.dma_start(k_of(s, 8), wo[:, 8 * half:8 * half + 8, 512 * n:512 * n + 512]).then_inc(w_full[s], 16)

            sp.wait_ge(wo_half, 4)
            sp.wait_ge(wo_full, 3)
            sp.dma_start(k_of(2, KC), sg[:, :, FF:2 * FF]).then_inc(w_full[2], 16)
            sp.dma_start(k_of(0, KC), sg[:, :, 0:FF]).then_inc(w_full[0], 16)
            sp.wait_ge(wo_full, 4)
            sp.dma_start(k_of(1, KC), su[:, :, 0:FF]).then_inc(w_full[1], 16)
            sp.dma_start(k_of(5, 2), sd[:, 2:4, :]).then_inc(w_full[5], 16)
            sp.dma_start(k_of(4, 2), sd[:, 0:2, :]).then_inc(w_full[4], 16)
            sp.wait_ge(hT_full, 8)
            sp.wait_ge(split_ready, 2)
            sp.dma_start(k_of(3, KC), su[:, :, FF:2 * FF]).then_inc(w_full[3], 16)

            def load_quarter(i, q):
                for u in range(2):
                    for g, src in ((0, wg), (1, wu)):
                        sp.dma_start(gu[:, q, u, g, :, :].rearrange("p k n -> p (k n)").rearrange("p (k n) -> p k n", k=4),
                                     src[:, bass.ds(2 * i + u, 1), 4 * q:4 * q + 4, :]
                                     .rearrange("p a c n -> p (a c) n")).then_inc(gu_in[q], 16)

            def load_down(i):
                for u in range(2):
                    if i is not FIRST:
                        sp.wait_ge(down_used[u], i)
                    sp.dma_start(down[u], wd[:, bass.ds(2 * i + u, 1), :, :].rearrange("p a c n -> p (a c) n"))\
                      .then_inc(down_in, 16)

            sp.wait_ge(sh_gate, 2)
            load_quarter(0, 0)
            sp.wait_ge(sh_up, 2)
            load_quarter(0, 1)
            sp.wait_ge(sh_gate, 4)
            load_quarter(0, 2)
            sp.wait_ge(sh_up, 4)
            load_quarter(0, 3)
            sp.wait_ge(sh_down, 16)
            load_down(FIRST)
            with sp.Fori(1, NE // 2) as i:
                for q in range(4):
                    sp.wait_ge(gu_used[q], i)
                    load_quarter(i, q)
                load_down(i)

            sp.wait_ge(gu_used[0], NE // 2)
            sp.dma_start(gainB, final_norm.rearrange("(a d) -> a d", a=1).to_broadcast([P, D])).then_inc(gain_in, 16)

            for t in range(2):
                sp.wait_ge(fin_done, t + 1)
                sp.dma_start(out[0].rearrange("(t p) d -> p t d", p=P)[:, t, :], xres[:, t, :]).then_inc(stored, 16)
            sp.wait_ge(stored, 32)

        @block.gpsimd
        def _(pool):
            nc.gpsimd.memset(csT[:, :, :], 0.0).then_inc(zeroed, 1)
            nc.gpsimd.memset(upad[:, :, :], 0.0).then_inc(zeroed, 1)

            roots = [0]

            def power(v):
                roots[0] += 1
                pool.wait_ge(mean_sq, roots[0])
                nc.gpsimd.tensor_tensor(v, v, cst[:, C_HALF:C_HALF + 1].to_broadcast(list(v.shape)), ALU.pow)\
                    .then_inc(root, 1)

            power(tiny[:, 8:12])

            pool.wait_ge(mods_ready, 1)
            for m in range(8):
                if m >= 2:
                    pool.wait_ge(diag_used, m - 1)
                for j in range(4):
                    at = (2 if m < 4 else 5) * KC + 4 * (m % 4) + j
                    ins = nc.gpsimd.tensor_scalar(diag[:, m % 2, 128 * j:128 * j + 128], ident, modT[:, at, 0:1],
                                                  None, ALU.mult)
                ins.then_inc(diag_ready, 1)
            for at in (10, 11, 14, 15):
                power(stat[:, at:at + 1])

        @block.tensor
        def _(pe):
            def mm(o, l, r, start, stop):
                return nc.tensor.matmul(o, l, r, start=start, stop=stop)

            pe.wait_ge(silu_c, 1)
            nc.tensor.transpose(ps[:, 7, 0:32], csil[:, :], ident[0:32, 0:32])
            nc.tensor.transpose(ps[:, 7, 64:64 + NVEC], vrow[0:NVEC, :], ident[0:NVEC, 0:NVEC])
            nc.tensor.transpose(ps[:, 7, 256:352], brow[0:96, :], ident[0:96, 0:96]).then_inc(small_T, 1)
            pe.wait_ge(small_done, 1)

            def mod_cols_of(n, b):
                pe.wait_ge(part_full, n + 1)
                if n is not FIRST:
                    pe.wait_ge(modT_done, n)
                for j in range(4):
                    ins = mm(ps[:, 5, 8 * b + 2 * j:8 * b + 2 * j + 2], part[:, b, 128 * j:128 * j + 128], sel2,
                             True, True)
                ins.then_inc(mod_cols, 1)

            def first_groups(i, first):
                for u in range(2):
                    if not first:
                        pe.wait_ge(part_full, 2 * i + u - 1)
                    for half in range(2):
                        s = MOD_SLOTS[2 * u + half]
                        w = k_of(s, 8)
                        pe.wait_ge(w_full[s], 16 * i + 16)
                        for k in range(8):
                            q = k % 4
                            ins = mm(ps[32 * q:32 * q + 32, 6 + u, :], csT[:, 8 * half + k, :], w[:, k, :],
                                     half == 0 and k < 4, half == 1 and k >= 4)
                    ins.then_inc(mod_rows, 1)
                for u in range(2):
                    mod_cols_of(FIRST if first and u == 0 else 2 * i + u, u)

            first_groups(FIRST, True)
            with pe.Fori(1, 4) as i:
                first_groups(i, False)

            pe.wait_ge(xs_ready, 4)
            for k in range(KC):
                if k >= 2:
                    pe.wait_ge(nT_lat, k - 1)
                    pe.wait_ge(nT_ctx, k - 1)
                for t in range(4):
                    src = (xs if t < 2 else ctxs)[:, t % 2, 128 * k:128 * k + 128]
                    ins = nc.tensor.transpose(ps[:, 2 * (k % 2) + t // 2, 128 * (t % 2):128 * (t % 2) + 128], src, ident)
                ins.then_inc(xT_full, 1)

            pe.wait_ge(nT_lat, KC)
            pe.wait_ge(nT_ctx, KC)
            for m in range(4):
                w = k_of(m // 2, KC)
                pe.wait_ge(w_full[m // 2], 16 * 5)
                for k in range(KC):
                    ins = mm(ps[:, m, 0:T], w[:, k, 128 * (m % 2):128 * (m % 2) + 128], nT[:, k, 0:T], k == 0, k == KC - 1)
                ins.then_inc(q_full, 1)
            pe.wait_ge(w_full[2], 16 * 5)
            pe.wait_ge(modT_done, 8)
            pe.wait_ge(part_full, 8)
            w = k_of(2, KC)
            for m in range(2):
                for k in range(KC):
                    ins = mm(ps[:, 6 - m, :], w[:, k, 128 * m:128 * m + 128], nT[:, k, :], k == 0, k == KC - 1)
                ins.then_inc(kv_full, 1)
            pe.wait_ge(wkr_in, 16)
            for k in range(KC):
                r = 64 * (k % 2)
                ins = mm(ps[r:r + 64, 7, :], wkr[:, k, :], nT[:, k, :], k < 2, k >= 14)
            ins.then_inc(kr_full, 1)
            pe.wait_ge(q_sq, 4)
            pe.wait_ge(q_out, 4)
            for m in range(4):
                ins = mm(ps[:, 0, 0:T], ones, squ[:, T * m:T * m + T], m == 0, m == 3)
            ins.then_inc(stat_q, 1)
            pe.wait_ge(kv_sq, 2)
            for m in range(2):
                ins = mm(ps[:, 1, :], ones, squ[:, 1024 + 512 * m:1536 + 512 * m], m == 0, m == 1)
            ins.then_inc(stat_kv, 1)
            pe.wait_ge(kr_sum, 1)
            mm(ps[:, 2, :], cst[:, C_DUP:C_DUP + P], krs[:, :], True, True)
            mm(ps[:, 3, 0:T], cst[:, C_ROTK:C_ROTK + P], krs[:, 0:T], True, True).then_inc(kr_mm, 1)

            pe.wait_ge(mean_wide, 2)
            pe.wait_ge(kr_done, 1)
            pe.wait_ge(kv_out, 2)

            def conv_blocks(i, s, first_bank):
                pe.wait_ge(w_full[s], 16 * i + 16 * 6)
                w = k_of(s, KC)
                for m in range(2):
                    for k in range(KC):
                        ins = mm(ps[:, first_bank + m, 0:T], w[:, k, 128 * m:128 * m + 128], nT[:, k, 0:T],
                                 k == 0, k == KC - 1)
                    ins.then_inc(conv_full, 1)

            def group_rows(i, u):
                for k in range(KC):
                    q = k // 4
                    if k % 4 == 0:
                        pe.wait_ge(m_full[q], 16 * (4 * i + u) + 16)
                    ins = mm(ps[32 * (k % 4):32 * (k % 4) + 32, 6 + u % 2, :], csT[:, k, :], mslot[q][:, k % 4, :],
                             k < 4, k >= 12)
                    if k % 4 == 3:
                        ins.then_inc(m_used[q] if q < 3 else mod_rows, 1)

            with pe.Fori(0, 4) as i:
                conv_blocks(i, 0, 0)
                pe.wait_ge(part_full, 4 * i + 7)
                group_rows(i, 0)
                conv_blocks(i, 1, 2)
                pe.wait_ge(part_full, 4 * i + 8)
                group_rows(i, 1)
                mod_cols_of(4 * i + 8, 0)
                pe.wait_ge(gc_out, 2 * i + 2)
                conv_blocks(i, 2, 0)
                group_rows(i, 2)
                mod_cols_of(4 * i + 9, 1)
                group_rows(i, 3)
                mod_cols_of(4 * i + 10, 0)
                mod_cols_of(4 * i + 11, 1)
                pe.wait_ge(y_out, 2 * i + 2)
            pe.wait_ge(u_out, 8)

            def project(j, width, steps):
                if j >= 4:
                    pe.wait_ge(proj_dve if j % 2 else proj_act, (j - 4) // 2 + 1)
                for n, (ls, r) in enumerate(steps):
                    for u, l in enumerate(ls):
                        rows_ = slice(P // len(ls) * u, P // len(ls) * (u + 1))
                        ins = mm(ps[rows_, j % 4, 0:width], l, r, n == 0, n == len(steps) - 1)
                ins.then_inc(proj_full, 1)

            def rotate(p):
                pe.wait_ge(proj_act, 3 * (p // 2) + p % 2 + 1)
                if p >= 2:
                    pe.wait_ge(qr_ready, p - 1)
                mm(ps[:, 6 + p % 2, 0:T], cst[:, C_ROTQ:C_ROTQ + P], qraw[:, p % 2, :], True, True).then_inc(rot_full, 1)

            pe.wait_ge(q_ready, 1)
            for s in range(2):
                w = slot[s][:, 0:3072].rearrange("p (k h n) -> p k h n", k=4, h=4)
                pe.wait_ge(w_full[s], 16 * USES)
                for n, (rope, h) in enumerate(((True, 0), (False, 0), (True, 2), (False, 1), (False, 2), (False, 3))):
                    lhs = [[w[:, k, h + u, NOPE:NOPE + ROPE] for u in range(2)] if rope else [w[:, k, h, 0:NOPE]]
                           for k in range(4)]
                    project(6 * s + n, T, [(lhs[k], qaT[:, k, :]) for k in range(4)])
                    if n == 3:
                        rotate(2 * s)
                rotate(2 * s + 1)
            pe.wait_ge(kv_ready, 1)
            pe.wait_ge(w_full[2], 16 * USES)
            w = slot[2].rearrange("p (k h n) -> p k h n", k=2, h=HEADS)
            for h in range(HEADS):
                project(12 + h, 2 * T, [([w[:, k, h, 0:NOPE]], kvT[:, k, :]) for k in range(2)])
            for t in range(4):
                for n in range(2):
                    project(20 + 2 * t + n, 512, [([kvT[:, k, 128 * t:128 * t + 128]],
                                                   w[:, k, 4 * n:4 * n + 4, NOPE:NOPE + VD]) for k in range(2)])

            pe.wait_ge(modT_done, 24)
            for k in range(8):
                pe.wait_ge(csq, k + 1)
                mm(ps[:, 5, 0:T], ones, sqr[:, k % 4, :], k == 0, k == 7).then_inc(csq_used, 1)
            pe.wait_ge(qr_ready, 4)
            for m in range(8):
                pe.wait_ge(diag_ready, m + 1)
                if m >= 2:
                    pe.wait_ge(gate_done, m - 1)
                mm(ps[:, 6 + m % 2, :], ones, diag[:, m % 2, :], True, True).then_inc(diag_used, 1)

            pe.wait_ge(proj_act, 14)
            pe.wait_ge(proj_dve, 14)

            def scores(n):
                h, t = n // 2, n % 2
                r = 64 * (h % 2)
                if n >= 2:
                    pe.wait_ge(exp_done, n - 1)
                mm(ps[:, n % 2, :], qnT[:, h, 128 * t:128 * t + 128], knT[:, h, :], True, False)
                mm(ps[:, n % 2, :], qrT[r:r + 64, h // 2, 128 * t:128 * t + 128], krT[r:r + 64, :], False, True)\
                    .then_inc(score_full, 1)

            def head_square(h):
                if h == 0:
                    pe.wait_ge(gate_done, 8)
                pe.wait_ge(msq, h + 1)
                mm(ps[:, 7, 0:T], ones, sqr[:, h % 4, :], h == 0, h == 7).then_inc(msq_used, 1)

            scores(0)
            scores(1)
            for n in range(2 * HEADS):
                h = n // 2
                pe.wait_ge(p_ready, n + 1)
                if n >= 2:
                    pe.wait_ge(pT_out, n - 1)
                for k in range(4):
                    ins = nc.tensor.transpose(ps[:, 2 + n % 2, 128 * k:128 * k + 128],
                                              prob[:, n % 2, 128 * k:128 * k + 128], ident)
                ins.then_inc(pT_full, 1)
                if n + 2 < 2 * HEADS:
                    scores(n + 2)
                if n % 2:
                    pe.wait_ge(pT_out, n + 1)
                    if h >= 2:
                        pe.wait_ge(o_out, h - 1)
                    else:
                        pe.wait_ge(gate_done, 7)
                    for k in range(4):
                        ins = mm(ps[:, 4 + 2 * (h % 2), 0:T], vtok[:, k, 128 * h:128 * h + 128], pT[:, h % 2, k, :],
                                 k == 0, k == 3)
                    ins.then_inc(o_full, 1)
                    if h:
                        head_square(h - 1)
            head_square(HEADS - 1)

            pe.wait_ge(oc_ready, 8)
            for (n, half), (s, use) in zip(W_OUT, WO_USE):
                pe.wait_ge(w_full[s], 16 * use)
                if n >= 2 and half == 1:
                    pe.wait_ge(h_part, 2 * (n - 1))
                w = k_of(s, 8)
                for k in range(8):
                    if half == 0:
                        pe.wait_ge(om_ready, k + 1)
                    for t in range(2):
                        ins = mm(ps[:, 2 * (n % 2) + t, :], oT[:, 8 * half + k, 128 * t:128 * t + 128], w[:, k, :],
                                 half == 1 and k == 0, half == 0 and k == 7)
                ins.then_inc(wo_full if half == 0 else wo_half, 1)

            pe.wait_ge(xh_ready, 2)
            for b in range(8):
                if b >= 4:
                    pe.wait_ge(hT_dve if b % 2 else hT_act, (b - 4) // 2 + 1)
                for j in range(2):
                    for t in range(2):
                        k = 2 * b + j
                        ins = nc.tensor.transpose(ps[:, b % 4, 256 * j + 128 * t:256 * j + 128 * t + 128],
                                                  xh[:, t, 128 * k:128 * k + 128], ident)
                ins.then_inc(hT_full, 1)

            pe.wait_ge(router_in, 32)
            for k in range(KC):
                if k % 2 == 0:
                    pe.wait_ge(hT_dve if k % 4 else hT_act, k // 4 + 1)
                q = k % 4
                ins = mm(ps[32 * q:32 * q + 32, 4, 0:T], wr[:, k, :], hT[:, k, :], k < 4, k >= 12)
            ins.then_inc(rt_rows, 1)
            pe.wait_ge(rt_copied, 1)
            for t in range(2):
                ins = mm(ps[:, 5, 32 * t:32 * t + 32], part[:, 0, 128 * t:128 * t + 128], sum4, True, True)
            ins.then_inc(rt_full, 1)

            for u in range(2):
                if u:
                    pe.wait_ge(sh_act, 2)
                for s, base, full in ((2 * u, 0, sh_gate), (2 * u + 1, 2, sh_up)):
                    w = k_of(s, KC)
                    pe.wait_ge(w_full[s], 16 * SH_USE[s])
                    for m in range(2):
                        for k in range(KC):
                            ins = mm(ps[:, base + m, 0:T], w[:, k, 128 * m:128 * m + 128], hT[:, k, :],
                                     k == 0, k == KC - 1)
                        ins.then_inc(full, 1)
                if u == 0:
                    pe.wait_ge(mask_ready, 1)
                    mm(ps[:, 5, 0:32], before, mask[:, 0, :], True, True)
                    mm(ps[:, 5, 32:64], ones, mask[:, 0, :], True, False)
                    mm(ps[:, 5, 32:64], before, mask[:, 1, :], False, True)
                    mm(ps[:, 5, 64:96], ones, mask[:, 0, :], True, False)
                    mm(ps[:, 5, 64:96], ones, mask[:, 1, :], False, True).then_inc(rank_full, 1)
                    pe.wait_ge(rank_ready, 1)
                w = k_of(4 + u, 2)
                pe.wait_ge(w_full[4 + u], 16 * SH_USE[4 + u])
                pe.wait_ge(sh_act, 2 * u + 2)
                for j in range(8):
                    t, m = j // 4, j % 4
                    if 8 * u + j >= 4:
                        pe.wait_ge(y_add, 8 * u + j - 3)
                    for k in range(2):
                        ins = mm(ps[:, 4 + m, :], shT[:, k, 128 * t:128 * t + 128], w[:, k, 512 * m:512 * m + 512],
                                 k == 0, k == 1)
                    ins.then_inc(sh_down, 1)

            def pair_pass(i, t, last):
                pe.wait_ge(pick_ready, t + 1)
                for b in range(4):
                    if b >= 2:
                        pe.wait_ge((gx_act, gx_dve)[b % 2], 2 * t + 1)
                    for j in range(4):
                        k = 4 * b + j
                        for n in range(6):
                            ins = mm(ps[:, b % 2, 128 * j:128 * j + 128], parts[n % 3][:, n // 3, 128 * k:128 * k + 128],
                                     pick[:, n // 3, :], n == 0, n == 5)
                    ins.then_inc(gx_full, 1)
                pe.wait_ge(pickw_ready, t + 1)
                for j in range(2):
                    ins = nc.tensor.transpose(ps[:, 3, 128 * j:128 * j + 128], pickw[:, j, :], ident)
                ins.then_inc(pickT_full, 1)
                for q in range(4):
                    pe.wait_ge(gu_in[q], 64 * i + 64)
                    pe.wait_ge((gx_act, gx_dve)[q % 2], 2 * t + (q // 2 + 1))
                    for k in range(4):
                        for u in range(2):
                            ins = mm(ps[64 * u:64 * u + 64, 2, :], xg[:, 4 * q + k, 64 * u:64 * u + 64],
                                     gu[:, q, u, :, k, :], q == 0 and k == 0, q == 3 and k == 3)
                    if q == 3:
                        ins.then_inc(gu_full, 1)
                    elif last:
                        ins.then_inc(gu_used[q], 1)
                pe.wait_ge(act_ready, t + 1)
                for k in range(2):
                    ins = nc.tensor.transpose(ps[:, 3, 256 + 128 * k:384 + 128 * k], act[:, 1, 128 * k:128 * k + 128], ident)
                    if k == 0 and last:
                        ins.then_inc(gu_used[3], 1)
                ins.then_inc(actT_full, 1)
                pe.wait_ge(down_in, 32 * i + 32)
                pe.wait_ge(actT_out, t + 1)

                def scatter(n):
                    pe.wait_ge(ye_out, 4 * t + (n + 1))
                    for h in range(2):
                        m = 2 * n + h
                        pe.wait_ge(y_add, 8 * t + (16 + max(m - 1, 0)))
                        ins = mm(ps[:, 6 + h, :], pickT[:, 128 * h:128 * h + 128], ye[:, 512 * n:512 * n + 512], True, True)
                        if n == 2 and h == 0 and last:
                            ins.then_inc(down_used[1], 1)
                    ins.then_inc(sc_full, 1)

                for n in range(4):
                    if n >= 2:
                        pe.wait_ge(ye_out, 4 * t + (n - 1))
                    for k in range(2):
                        for u in range(2):
                            ins = mm(ps[64 * u:64 * u + 64, 4 + n % 2, :], actT[:, k, 64 * u:64 * u + 64],
                                     down[u][:, k, 512 * n:512 * n + 512], k == 0, k == 1)
                            if n == 3 and k == 1 and u == 0 and last:
                                ins.then_inc(down_used[0], 1)
                    ins.then_inc(dn_full, 1)
                    if n == 0:
                        pe.wait_ge(pickT_out, t + 1)
                    else:
                        scatter(n - 1)
                scatter(3)

            passes = pe.alloc_register("pe_passes")
            pe.reg_mov(passes, 0)
            pe.wait_ge(rank_ready, 1)
            pe.wait_ge(y_add, 16)
            with pe.Fori(0, NE // 2) as i:
                extra = pe.value_load(more[0:1, bass.ds(i, 1)], min_val=0, max_val=PASSES - 1)
                with pe.If(extra > 0):
                    with pe.Fori(1, extra + 1):
                        pair_pass(i, pe.snap(passes, min_val=0, max_val=64), False)
                        pe.reg_add(passes, passes, 1)
                pair_pass(i, pe.snap(passes, min_val=0, max_val=64), True)
                pe.reg_add(passes, passes, 1)

        @block.scalar
        def _(sc):
            def copy(o, i_):
                return nc.scalar.activation(o, i_, ACT.Copy)

            sc.wait_ge(small_in, 16 * 11)
            nc.scalar.activation(csil[:, :], crow[:, :], ACT.Silu).then_inc(silu_c, 1)

            sc.wait_ge(x_in, 16)
            for t in range(2):
                nc.scalar.activation(nreg[:, 2048 * t:2048 * t + 2048], xres[:, t, :], ACT.Square,
                                     accum_out=stat[:, t:t + 1]).then_inc(squares, 1)
            sc.wait_ge(ctx_ld, 16)
            for t in range(2):
                nc.scalar.activation(nreg[:, 2048 * t + 4096:2048 * t + 6144], ctxs[:, t, :], ACT.Square,
                                     accum_out=stat[:, t + 2:t + 3]).then_inc(squares, 1)

            def rows_out(n, bank, b, first):
                sc.wait_ge(mod_rows, n + 1)
                if not first:
                    sc.wait_ge(mod_cols, n - 1)
                copy(part[:, b, :], ps[:, bank, :]).then_inc(part_full, 1)

            rows_out(0, 6, 0, True)
            rows_out(1, 7, 1, True)
            with sc.Fori(1, 4) as i:
                rows_out(2 * i, 6, 0, False)
                rows_out(2 * i + 1, 7, 1, False)

            sc.wait_ge(amul_ready, 1)
            for k in range(KC):
                sc.wait_ge(xT_full, k + 1)
                nc.scalar.activation(nT[:, k, T:2 * T], ps[:, 2 * (k % 2) + 1, 0:T], ACT.Identity, bias=modT[:, k, 1:2],
                                     scale=amul[:, k, 1:2]).then_inc(nT_ctx, 1)

            for m in range(4):
                sc.wait_ge(q_full, m + 1)
                nc.scalar.activation(squ[:, T * m:T * m + T], ps[:, m, 0:T], ACT.Square).then_inc(q_sq, 1)
            for m in range(2):
                sc.wait_ge(kv_full, m + 1)
                nc.scalar.activation(squ[:, 1024 + 512 * m:1536 + 512 * m], ps[:, 6 - m, :], ACT.Square).then_inc(kv_sq, 1)
            sc.wait_ge(kr_full, 1)
            copy(krs[:, :], ps[:, 7, :]).then_inc(kr_sum, 1)

            wide = [0]

            def square_root(v):
                wide[0] += 1
                sc.wait_ge(mean_wide, wide[0])
                nc.scalar.activation(v, v, ACT.Sqrt).then_inc(root_wide, 1)

            square_root(rowq)
            square_root(rowkv)

            with sc.Fori(0, 4) as i:
                for m in range(2):
                    sc.wait_ge(conv_full, 6 * i + m + 1)
                    copy(gcs[:, m, :], ps[:, m, 0:T]).then_inc(gc_out, 1)
                for u in range(4):
                    rows_out(4 * i + u + 8, 6 + u % 2, u % 2, False)

            for j in range(0, 28, 2):
                sc.wait_ge(proj_full, j + 1)
                bank = ps[:, j % 4, :]
                if j < 12:
                    s, n = j // 6, j % 6
                    if n == 4:
                        dst, src = qnT[:, 4 * s + 2, :], bank[:, 0:T]
                    else:
                        p = 2 * s + n // 2
                        if p >= 2:
                            sc.wait_ge(qr_ready, p - 1)
                        dst, src = qraw[:, p % 2, :], bank[:, 0:T]
                elif j < 20:
                    dst, src = knT[:, j - 12, :], bank
                else:
                    t, n = (j - 20) // 2, j % 2
                    dst, src = vtok[:, t, 512 * n:512 * n + 512], bank
                copy(dst, src).then_inc(proj_act, 1)

            sc.wait_ge(y_out, 8)
            for k in range(8):
                if k >= 4:
                    sc.wait_ge(csq_used, k - 3)
                nc.scalar.activation(sqr[:, k % 4, :], oT[:, 8 + k, :], ACT.Square).then_inc(csq, 1)

            square_root(rconv)

            def exponentials(n):
                sc.wait_ge(neg_max, n + 1)
                if n >= 2:
                    sc.wait_ge(pT_full, n - 1)
                nc.scalar.activation(prob[:, n % 2, :], ps[:, n % 2, :], ACT.Exp, bias=stat[:, 4 + n % 2:5 + n % 2],
                                     scale=SCALE, accum_out=stat[:, 6 + n % 2:7 + n % 2]).then_inc(exp_done, 1)

            def head_square(h):
                sc.wait_ge(o_out, h + 1)
                if h >= 4:
                    sc.wait_ge(msq_used, h - 3)
                nc.scalar.activation(sqr[:, h % 4, :], oT[:, h, :], ACT.Square).then_inc(msq, 1)

            sc.wait_ge(csq_used, 8)
            exponentials(0)
            for n in range(2 * HEADS):
                h = n // 2
                if n + 1 < 2 * HEADS:
                    exponentials(n + 1)
                sc.wait_ge(pT_full, n + 1)
                if h >= 2:
                    sc.wait_ge(o_full, h - 1)
                copy(pT[:, h % 2, :, 128 * (n % 2):128 * (n % 2) + 128],
                     ps[:, 2 + n % 2, :].rearrange("p (k q) -> p k q", k=4)).then_inc(pT_out, 1)
                if n % 2 and h:
                    head_square(h - 1)
            head_square(HEADS - 1)
            square_root(rmla)

            for t in range(2):
                sc.wait_ge(h_part, 7 + t)
                nc.scalar.activation(xh[:, t, :], xres[:, t, :], ACT.Square, accum_out=stat[:, 8 + t:9 + t])\
                    .then_inc(hsq, 1)

            for b in range(0, 8, 2):
                sc.wait_ge(hT_full, b + 1)
                for k in (2 * b, 2 * b + 1):
                    ins = nc.scalar.activation(hT[:, k, :], ps[:, b % 4, T * (k % 2):T * (k % 2) + T], ACT.Identity,
                                               bias=modT[:, 3 * KC + k, 0:1], scale=amul2[:, k:k + 1])
                ins.then_inc(hT_act, 1)
            sc.wait_ge(hT_full, 8)
            sc.wait_ge(rt_rows, 1)
            copy(part[:, 0, 0:T], ps[:, 4, 0:T]).then_inc(rt_copied, 1)
            sc.wait_ge(rt_full, 1)
            nc.scalar.activation(sig[:, :, :], ps[:, 5, 0:64].rearrange("p (t e) -> p t e", t=2), ACT.Sigmoid)\
                .then_inc(rt_sig, 1)

            for t in range(2):
                copy(parts[0][:, t, :], xh[:, t, :]).then_inc(split_act, 1)

            for n in range(4):
                sc.wait_ge(sh_gate, n + 1)
                if n >= 2:
                    sc.wait_ge(sh_act, n - 1)
                nc.scalar.activation(shS[:, n % 2, :], ps[:, n % 2, 0:T], ACT.Silu).then_inc(sh_silu, 1)

            def pair_pass(t):
                for b in (0, 2):
                    sc.wait_ge(gx_full, 4 * t + (b + 1))
                    for j in range(4):
                        k = 4 * b + j
                        ins = nc.scalar.activation(xg[:, k, :], ps[:, b % 2, 128 * j:128 * j + 128], ACT.Identity,
                                                   bias=modT[:, 3 * KC + k, 0:1], scale=amul2[:, k:k + 1])
                    ins.then_inc(gx_act, 1)
                sc.wait_ge(pickT_full, t + 1)
                copy(pickT[:, :], ps[:, 3, 0:256]).then_inc(pickT_out, 1)
                sc.wait_ge(gu_full, t + 1)
                nc.scalar.activation(act[:, 0, :], ps[:, 2, 0:FF], ACT.Silu).then_inc(silu_done, 1)
                sc.wait_ge(actT_full, t + 1)
                copy(actT[:, :, :].rearrange("p k s -> p (k s)"), ps[:, 3, 256:512]).then_inc(actT_out, 1)
                for n in range(4):
                    sc.wait_ge(dn_full, 4 * t + (n + 1))
                    copy(ye[:, 512 * n:512 * n + 512], ps[:, 4 + n % 2, :]).then_inc(ye_out, 1)

            passes = sc.alloc_register("act_passes")
            sc.reg_mov(passes, 0)
            sc.wait_ge(rank_ready, 1)
            with sc.Fori(0, NE // 2) as i:
                extra = sc.value_load(more[0:1, bass.ds(i, 1)], min_val=0, max_val=PASSES - 1)
                with sc.If(extra > 0):
                    with sc.Fori(1, extra + 1):
                        pair_pass(sc.snap(passes, min_val=0, max_val=64))
                        sc.reg_add(passes, passes, 1)
                pair_pass(sc.snap(passes, min_val=0, max_val=64))
                sc.reg_add(passes, passes, 1)

            for t in range(2):
                sc.wait_ge(fin_h, t + 1)
                nc.scalar.activation(hT.rearrange("p c t -> p (c t)")[:, 2048 * t:2048 * t + 2048], xres[:, t, :],
                                     ACT.Square, accum_out=stat[:, 12 + t:13 + t]).then_inc(fin_sq, 1)

        @block.vector
        def _(ve):
            V = nc.vector
            steps = [0]

            def link(ins):
                steps[0] += 1
                ins.then_inc(v_step, 1)
                ve.wait_ge(v_step, steps[0])

            roots = [0]
            wide = [0]

            def rsqrt_wide(o, i_, n):
                V.tensor_scalar(o, i_, 1.0 / n, EPS, ALU.mult, ALU.add).then_inc(mean_wide, 1)
                wide[0] += 1
                ve.wait_ge(root_wide, wide[0])
                link(V.reciprocal(o, o))

            def rsqrt(o, i_, n):
                V.tensor_scalar(o, i_, 1.0 / n, EPS, ALU.mult, ALU.add).then_inc(mean_sq, 1)
                roots[0] += 1
                ve.wait_ge(root, roots[0])

            ve.wait_ge(zeroed, 2)
            ve.wait_ge(small_T, 1)
            for v in range(2):
                V.tensor_copy(csT[:, :, v:v + 1], ps[:, 7, 16 * v:16 * v + 16].rearrange("p (c a) -> p c a", a=1))
            V.tensor_copy(vecT[:, :], ps[:, 7, 64:64 + NVEC])
            V.tensor_copy(bT[:, :], ps[:, 7, 256:352]).then_inc(small_done, 1)
            ve.wait_ge(small_done, 1)

            ve.wait_ge(squares, 4)
            rsqrt(tiny[:, 8:12], stat[:, 0:4], D)
            for t in range(2):
                V.tensor_scalar(xs[:, t, :], xres[:, t, :], tiny[:, 8 + t:9 + t], None, ALU.mult).then_inc(xs_ready, 1)
            for t in range(2):
                V.tensor_scalar(ctxs[:, t, :], ctxs[:, t, :], tiny[:, 10 + t:11 + t], None, ALU.mult).then_inc(xs_ready, 1)

            def cols_out(n, b):
                ve.wait_ge(mod_cols, n + 1)
                V.tensor_copy(modT[:, bass.ds(4 * n, 4), :], ps[:, 5, 8 * b:8 * b + 8].rearrange("p (c v) -> p c v", v=2))\
                    .then_inc(modT_done, 1)

            with ve.Fori(0, 4) as i:
                cols_out(2 * i, 0)
                cols_out(2 * i + 1, 1)
            ve.wait_ge(modT_done, 8)
            link(V.tensor_tensor(modT[:, 0:32, :], modT[:, 0:32, :], bT[:, 0:32].unsqueeze(2).to_broadcast([P, 32, 2]),
                                 ALU.add))
            V.scalar_tensor_tensor(out=amul[:, :, :], in0=modT[:, 16:32, :], scalar=1.0,
                                   in1=vecT[:, V_AN:V_AN + KC].unsqueeze(2).to_broadcast([P, KC, 2]),
                                   op0=ALU.add, op1=ALU.mult).then_inc(amul_ready, 1)
            ve.wait_ge(amul_ready, 1)
            for k in range(KC):
                ve.wait_ge(xT_full, k + 1)
                V.tensor_scalar(nT[:, k, 0:T], ps[:, 2 * (k % 2), 0:T], amul[:, k, 0:1], modT[:, k, 0:1], ALU.mult, ALU.add)\
                    .then_inc(nT_lat, 1)

            for m in range(4):
                ve.wait_ge(q_sq, m + 1)
                V.tensor_scalar(qaT[:, m, :], ps[:, m, 0:T], vecT[:, V_QN + m:V_QN + m + 1], None, ALU.mult)\
                    .then_inc(q_out, 1)
            for m in range(2):
                ve.wait_ge(kv_sq, m + 1)
                V.tensor_scalar(kvT[:, m, :], ps[:, 6 - m, :], vecT[:, V_KN + m:V_KN + m + 1], None, ALU.mult)\
                    .then_inc(kv_out, 1)
            ve.wait_ge(stat_q, 1)
            rsqrt_wide(rowq, ps[:, 0, 0:T], QL)
            ve.wait_ge(stat_kv, 1)
            rsqrt_wide(rowkv, ps[:, 1, :], KVL)
            ve.wait_ge(kr_mm, 1)
            V.tensor_copy(krT[:, T:2 * T], ps[:, 2, T:2 * T])
            link(V.tensor_tensor(krT[:, 0:T], ps[:, 2, 0:T], cosT, ALU.mult))
            link(V.tensor_tensor(krs[:, 0:T], ps[:, 3, 0:T], sinT, ALU.mult))
            V.tensor_tensor(krT[:, 0:T], krT[:, 0:T], krs[:, 0:T], ALU.add).then_inc(kr_done, 1)
            ve.wait_ge(q_out, 4)
            ve.wait_ge(kv_out, 2)
            for m in range(4):
                ins = V.tensor_tensor(qaT[:, m, :], qaT[:, m, :], rowq, ALU.mult)
            ins.then_inc(q_ready, 1)
            for m in range(2):
                ins = V.tensor_tensor(kvT[:, m, :], kvT[:, m, :], rowkv, ALU.mult)
            ins.then_inc(kv_ready, 1)

            base, LINKS = steps[0], 3
            with ve.Fori(0, 4) as i:
                def tap(j, m):
                    return vecT[:, bass.ds(V_CW + 8 * j + m + 2 * i, 1)]

                for m in range(2):
                    ve.wait_ge(conv_full, 6 * i + 3 + m)
                    ve.wait_ge(gc_out, 2 * i + m + 1)
                    V.tensor_tensor(upad[:, m, 1:T + 1], ps[:, 2 + m, 0:T], gcs[:, m, :], ALU.mult).then_inc(u_out, 1)
                ve.wait_ge(u_out, 2 * i + 2)
                for m in range(2):
                    ins = V.tensor_scalar(ycv[:, m, :], upad[:, m, 1:T + 1], tap(1, m), None, ALU.mult)
                ins.then_inc(v_step, 1)
                ve.wait_ge(v_step, 3 * i + base + 1)
                for j in (0, 2):
                    for m in range(2):
                        ins = V.scalar_tensor_tensor(out=ycv[:, m, :], in0=upad[:, m, j:j + T], scalar=tap(j, m),
                                                     in1=ycv[:, m, :], op0=ALU.mult, op1=ALU.add)
                    ins.then_inc(v_step, 1)
                    ve.wait_ge(v_step, 3 * i + base + 2 + j // 2)
                for m in range(2):
                    ve.wait_ge(conv_full, 6 * i + 5 + m)
                    V.tensor_tensor(oT[:, bass.ds(8 + m + 2 * i, 1), :].rearrange("p a t -> p (a t)"), ps[:, m, 0:T],
                                    ycv[:, m, :], ALU.mult).then_inc(y_out, 1)
                for u in range(4):
                    cols_out(4 * i + u + 8, u % 2)
            steps[0] += 4 * LINKS

            ve.wait_ge(modT_done, 24)
            link(V.tensor_tensor(modT[:, 32:96, :], modT[:, 32:96, :], bT[:, 32:96].unsqueeze(2).to_broadcast([P, 64, 2]),
                                 ALU.add))
            V.scalar_tensor_tensor(out=amul2[:, :].rearrange("p (c a) -> p c a", a=1), in0=modT[:, 64:80, 0:1], scalar=1.0,
                                   in1=vecT[:, V_FN:V_FN + KC].rearrange("p (c a) -> p c a", a=1),
                                   op0=ALU.add, op1=ALU.mult).then_inc(mods_ready, 1)

            def rope(p):
                ve.wait_ge(rot_full, p + 1)
                ve.wait_ge(proj_act, 3 * (p // 2) + p % 2 + 1)
                link(V.tensor_tensor(ycv[:, p % 2, :], ps[:, 6 + p % 2, 0:T], sinT, ALU.mult))
                link(V.tensor_tensor(qrT[:, p, :], qraw[:, p % 2, :], cosT, ALU.mult))
                V.tensor_tensor(qrT[:, p, :], qrT[:, p, :], ycv[:, p % 2, :], ALU.add).then_inc(qr_ready, 1)

            for j in range(1, 28, 2):
                ve.wait_ge(proj_full, j + 1)
                bank = ps[:, j % 4, :]
                if j < 12:
                    s, n = j // 6, j % 6
                    dst, src = qnT[:, 4 * s + {1: 0, 3: 1, 5: 3}[n], :], bank[:, 0:T]
                elif j < 20:
                    dst, src = knT[:, j - 12, :], bank
                else:
                    dst, src = vtok[:, (j - 20) // 2, 512:1024], bank
                V.tensor_copy(dst, src).then_inc(proj_dve, 1)
                if j in (5, 7, 11, 13):
                    rope({5: 0, 7: 1, 11: 2, 13: 3}[j])

            ve.wait_ge(csq_used, 8)
            rsqrt_wide(rconv, ps[:, 5, 0:T], CW)
            for k in range(8):
                V.scalar_tensor_tensor(out=oT[:, 8 + k, :], in0=oT[:, 8 + k, :], scalar=vecT[:, V_OC + k:V_OC + k + 1],
                                       in1=rconv, op0=ALU.mult, op1=ALU.mult).then_inc(oc_ready, 1)
            for m in range(8):
                ve.wait_ge(diag_used, m + 1)
                V.tensor_copy((gaB if m < 4 else gfB)[:, 512 * (m % 4):512 * (m % 4) + 512], ps[:, 6 + m % 2, :])\
                    .then_inc(gate_done, 1)

            def maximum(n):
                ve.wait_ge(score_full, n + 1)
                link(V.tensor_reduce(tiny[:, 16 + n % 2:17 + n % 2], ps[:, n % 2, :], AX.X, ALU.max))
                V.tensor_scalar(stat[:, 4 + n % 2:5 + n % 2], tiny[:, 16 + n % 2:17 + n % 2], -SCALE, None, ALU.mult)\
                    .then_inc(neg_max, 1)

            def head_out(h):
                ve.wait_ge(o_full, h + 1)
                V.tensor_copy(oT[:, h, :], ps[:, 4 + 2 * (h % 2), 0:T]).then_inc(o_out, 1)

            maximum(0)
            for n in range(2 * HEADS):
                if n + 1 < 2 * HEADS:
                    maximum(n + 1)
                ve.wait_ge(exp_done, n + 1)
                if n >= 2:
                    ve.wait_ge(p_ready, n - 1)
                inverse = tiny[:, 20 + n % 2:21 + n % 2]
                link(V.reciprocal(inverse, stat[:, 6 + n % 2:7 + n % 2]))
                V.tensor_scalar(prob[:, n % 2, :], prob[:, n % 2, :], inverse, None, ALU.mult).then_inc(p_ready, 1)
                if n % 2 and n > 1:
                    head_out(n // 2 - 1)
            head_out(HEADS - 1)

            ve.wait_ge(msq_used, 8)
            rsqrt_wide(rmla, ps[:, 7, 0:T], HEADS * VD)
            for k in range(8):
                V.scalar_tensor_tensor(out=oT[:, k, :], in0=oT[:, k, :], scalar=vecT[:, V_OM + k:V_OM + k + 1],
                                       in1=rmla, op0=ALU.mult, op1=ALU.mult).then_inc(om_ready, 1)

            ve.wait_ge(gate_done, 8)
            for n in range(4):
                ve.wait_ge(wo_full, n + 1)
                for t in range(2):
                    tmp = nreg[:, 512 * t:512 * t + 512]
                    link(V.tensor_tensor(tmp, ps[:, 2 * (n % 2) + t, :], gaB[:, 512 * n:512 * n + 512], ALU.mult))
                    V.tensor_tensor(xres[:, t, 512 * n:512 * n + 512], xres[:, t, 512 * n:512 * n + 512], tmp, ALU.add)\
                        .then_inc(h_part, 1)

            for t in range(2):
                ve.wait_ge(hsq, t + 1)
                rsqrt(stat[:, 10 + t:11 + t], stat[:, 8 + t:9 + t], D)
                V.tensor_scalar(xh[:, t, :], xres[:, t, :], stat[:, 10 + t:11 + t], None, ALU.mult).then_inc(xh_ready, 1)
            for b in range(1, 8, 2):
                ve.wait_ge(hT_full, b + 1)
                for k in (2 * b, 2 * b + 1):
                    ins = V.tensor_scalar(hT[:, k, :], ps[:, b % 4, T * (k % 2):T * (k % 2) + T], amul2[:, k:k + 1],
                                          modT[:, 3 * KC + k, 0:1], ALU.mult, ALU.add)
                ins.then_inc(hT_dve, 1)

            ve.wait_ge(rt_sig, 1)
            link(V.tensor_tensor(sel[:, :, :], sig[:, :, :], rb[:, :].unsqueeze(1).to_broadcast([P, 2, NE]), ALU.add))
            for t in range(2):
                for g in range(NG):
                    ins = V.max(top8[:, 4 * t + g, :], sel[:, t, 8 * g:8 * g + 8])
            link(ins)
            gs = tiny[:, 32:40].rearrange("p (t g) -> p t g", t=2)
            link(V.tensor_tensor(gs.unsqueeze(3), top8[:, 0:8, 0:1].rearrange("p (t g) a -> p t g a", t=2),
                                 top8[:, 0:8, 1:2].rearrange("p (t g) a -> p t g a", t=2), ALU.add))
            above = tiny[:, 40:72].rearrange("p (t g a) -> p t g a", t=2, g=NG)
            same = tiny[:, 72:104].rearrange("p (t g a) -> p t g a", t=2, g=NG)
            other = gs.unsqueeze(2).to_broadcast([P, 2, NG, NG])
            own = gs.unsqueeze(3).to_broadcast([P, 2, NG, NG])
            V.tensor_tensor(above, other, own, ALU.is_gt)
            link(V.tensor_tensor(same, other, own, ALU.is_equal))
            link(V.tensor_tensor(same, same, low.unsqueeze(1).to_broadcast([P, 2, NG, NG]), ALU.mult))
            link(V.tensor_tensor(above, above, same, ALU.add))
            link(V.tensor_reduce(tiny[:, 104:112].rearrange("p (t g) -> p t g", t=2), above, AX.X, ALU.add))
            link(V.tensor_scalar(tiny[:, 112:120], tiny[:, 104:112], 1.5, -BIG, ALU.is_gt, ALU.mult))
            gm = tiny[:, 104:112]
            link(V.tensor_scalar(gm, tiny[:, 104:112], 1.5, None, ALU.is_lt))
            link(V.tensor_tensor(sel[:, :, :].rearrange("p t (g e) -> p t g e", g=NG),
                                 sel[:, :, :].rearrange("p t (g e) -> p t g e", g=NG),
                                 gm.rearrange("p (t g) -> p t g", t=2).unsqueeze(3).to_broadcast([P, 2, NG, 8]), ALU.mult))
            link(V.tensor_tensor(sel[:, :, :].rearrange("p t (g e) -> p t g e", g=NG),
                                 sel[:, :, :].rearrange("p t (g e) -> p t g e", g=NG),
                                 tiny[:, 112:120].rearrange("p (t g) -> p t g", t=2).unsqueeze(3)
                                 .to_broadcast([P, 2, NG, 8]), ALU.add))
            for t in range(2):
                ins = V.max(top8[:, 8 + t, :], sel[:, t, :])
            link(ins)
            for t in range(2):
                last_ = top8[:, 8 + t, TOP_K - 1:TOP_K]
                V.tensor_scalar(mask[:, t, :], sel[:, t, :], last_, None, ALU.is_gt)
                ins = V.tensor_scalar(scan[:, 0, t, :], sel[:, t, :], last_, None, ALU.is_equal)
            link(ins)
            V.tensor_copy(sel[:, :, :], scan[:, 0, :, :])
            link(V.tensor_reduce(tiny[:, 120:122], mask[:, :, :], AX.X, ALU.add))
            for n, d in enumerate((1, 2, 4, 8, 16)):
                a, b = scan[:, n % 2, :, :], scan[:, (n + 1) % 2, :, :]
                V.tensor_copy(b[:, :, 0:d], a[:, :, 0:d])
                link(V.tensor_tensor(b[:, :, d:NE], a[:, :, d:NE], a[:, :, 0:NE - d], ALU.add))
            link(V.tensor_tensor(scan[:, 1, :, :], scan[:, 1, :, :], tiny[:, 120:122].unsqueeze(2).to_broadcast([P, 2, NE]),
                                 ALU.add))
            link(V.tensor_scalar(scan[:, 1, :, :], scan[:, 1, :, :], TOP_K + 0.5, None, ALU.is_lt))
            link(V.tensor_tensor(sel[:, :, :], sel[:, :, :], scan[:, 1, :, :], ALU.mult))
            V.tensor_tensor(mask[:, :, :], mask[:, :, :], sel[:, :, :], ALU.add).then_inc(mask_ready, 1)
            ve.wait_ge(mask_ready, 1)
            link(V.tensor_tensor(comb[:, :, :], sig[:, :, :], mask[:, :, :], ALU.mult))
            link(V.tensor_reduce(tiny[:, 124:126], comb[:, :, :], AX.X, ALU.add))
            link(V.reciprocal(tiny[:, 126:128], tiny[:, 124:126]))
            for t in range(2):
                ins = V.tensor_scalar(comb[:, t, :], comb[:, t, :], tiny[:, 126 + t:127 + t], ROUTED_SCALE, ALU.mult, ALU.mult)
            link(ins)
            for t in range(2):
                ve.wait_ge(split_act, t + 1)
                link(V.tensor_tensor(xh[:, t, :], xh[:, t, :], parts[0][:, t, :], ALU.subtract))
                link(V.tensor_copy(parts[1][:, t, :], xh[:, t, :]))
                V.tensor_tensor(parts[2][:, t, :], xh[:, t, :], parts[1][:, t, :], ALU.subtract).then_inc(split_ready, 1)

            ve.wait_ge(rank_full, 1)
            cnt = scan[:, 0, 0, :]
            V.tensor_copy(cnt, ps[:, 5, 64:96])
            link(V.scalar_tensor_tensor(out=rank[:, 0, :, :], in0=ps[:, 5, 0:64].rearrange("p (t e) -> p t e", t=2),
                                        scalar=1.0, in1=mask[:, :, :], op0=ALU.add, op1=ALU.mult))
            link(V.tensor_scalar(rank[:, 0, :, :], rank[:, 0, :, :], -1.0, None, ALU.add))
            for n in range(1, PASSES):
                V.tensor_scalar(rank[:, n, :, :], rank[:, 0, :, :], -float(SLOTS * n), None, ALU.add)
            pairs = cnt.rearrange("p (i u) -> p i u", u=2)
            big = scan[:, 0, 1, 0:16]
            link(V.tensor_tensor(big.unsqueeze(2), pairs[:, :, 0:1], pairs[:, :, 1:2], ALU.max))
            acc, one = scan[:, 1, 0, 0:16], scan[:, 1, 1, 0:16]
            link(V.tensor_scalar(acc, big, SLOTS + 0.5, None, ALU.is_gt))
            for n in range(2, PASSES):
                link(V.tensor_scalar(one, big, SLOTS * n + 0.5, None, ALU.is_gt))
                link(V.tensor_tensor(acc, acc, one, ALU.add))
            V.tensor_copy(more[:, :], acc).then_inc(rank_ready, 1)

            for u in range(2):
                for m in range(2):
                    n = 2 * u + m
                    ve.wait_ge(sh_up, n + 1)
                    ve.wait_ge(sh_silu, n + 1)
                    if u:
                        ve.wait_ge(sh_down, 8)
                    V.tensor_tensor(shT[:, m, :], ps[:, 2 + m, 0:T], shS[:, m, :], ALU.mult).then_inc(sh_act, 1)
                for j in range(8):
                    t, m = j // 4, j % 4
                    ve.wait_ge(sh_down, 8 * u + j + 1)
                    y = yacc[:, t, 512 * m:512 * m + 512]
                    if u == 0:
                        V.tensor_copy(y, ps[:, 4 + m, :]).then_inc(y_add, 1)
                    else:
                        ve.wait_ge(y_add, j + 1)
                        V.tensor_tensor(y, y, ps[:, 4 + m, :], ALU.add).then_inc(y_add, 1)

            def pair_pass(i, t, n):
                for j in range(2):
                    for u in range(2):
                        ins = V.tensor_scalar(pick[:, j, 64 * u:64 * u + 64], iota,
                                              slots[:, bass.ds(n * (2 * NE) + j * NE + 2 * i + u, 1)], None, ALU.is_equal)
                ins.then_inc(pick_ready, 1)
                for j in range(2):
                    for u in range(2):
                        ins = V.tensor_scalar(pickw[:, j, 64 * u:64 * u + 64], iota,
                                              slots[:, bass.ds(n * (2 * NE) + j * NE + 2 * i + u, 1)],
                                              weights[:, bass.ds(j * NE + 2 * i + u, 1)], ALU.is_equal, ALU.mult)
                ins.then_inc(pickw_ready, 1)
                for b in (1, 3):
                    ve.wait_ge(gx_full, 4 * t + (b + 1))
                    for j in range(4):
                        k = 4 * b + j
                        ins = V.tensor_scalar(xg[:, k, :], ps[:, b % 2, 128 * j:128 * j + 128], amul2[:, k:k + 1],
                                              modT[:, 3 * KC + k, 0:1], ALU.mult, ALU.add)
                    ins.then_inc(gx_dve, 1)
                ve.wait_ge(silu_done, t + 1)
                V.tensor_tensor(act[:, 1, :], ps[:, 2, FF:2 * FF], act[:, 0, :], ALU.mult).then_inc(act_ready, 1)
                for m in range(8):
                    h, q = m % 2, m // 2
                    if h == 0:
                        ve.wait_ge(sc_full, 4 * t + (q + 1))
                    y = yacc[:, h, 512 * q:512 * q + 512]
                    V.tensor_tensor(y, y, ps[:, 6 + h, :], ALU.add).then_inc(y_add, 1)
                ve.wait_ge(y_add, 8 * t + 24)

            slots = rank[:, :, :, :].rearrange("p n t e -> p (n t e)")
            weights = comb[:, :, :].rearrange("p t e -> p (t e)")
            passes = ve.alloc_register("dve_passes")
            ve.reg_mov(passes, 0)
            ve.wait_ge(y_add, 16)
            ve.wait_ge(rank_ready, 1)
            with ve.Fori(0, NE // 2) as i:
                extra = ve.value_load(more[0:1, bass.ds(i, 1)], min_val=0, max_val=PASSES - 1)
                with ve.If(extra > 0):
                    with ve.Fori(1, extra + 1) as n:
                        pair_pass(i, ve.snap(passes, min_val=0, max_val=64), n)
                        ve.reg_add(passes, passes, 1)
                pair_pass(i, ve.snap(passes, min_val=0, max_val=64), 0)
                ve.reg_add(passes, passes, 1)

            for t in range(2):
                link(V.tensor_tensor(yacc[:, t, :], yacc[:, t, :], gfB, ALU.mult))
                V.tensor_tensor(xres[:, t, :], xres[:, t, :], yacc[:, t, :], ALU.add).then_inc(fin_h, 1)
            ve.wait_ge(gain_in, 16)
            for t in range(2):
                ve.wait_ge(fin_sq, t + 1)
                rsqrt(stat[:, 14 + t:15 + t], stat[:, 12 + t:13 + t], D)
                V.scalar_tensor_tensor(out=xres[:, t, :], in0=xres[:, t, :], scalar=stat[:, 14 + t:15 + t],
                                       in1=gainB, op0=ALU.mult, op1=ALU.mult).then_inc(fin_done, 1)


_INS = ["x", "c", "ctx", "c_ctx", "w_mod", "b_mod", "attn_norm", "w_in", "q_a_norm", "w_q_b", "kv_a_norm", "w_kv_b",
        "conv_w", "o_norm_mla", "o_norm_conv", "w_out", "ffn_norm", "w_router", "router_bias",
        "w_exp_gate", "w_exp_up", "w_exp_down", "w_sh_gate", "w_sh_up", "w_sh_down", "final_norm"]


def kernel(**inputs):
    import concourse.bacc as _bacc
    from concourse.bass_utils import run_bass_kernel_spmd as _run

    nc = _bacc.Bacc("TRN2", target_bir_lowering=False, num_devices=1)
    arrays = {f"in_{name}": np.ascontiguousarray(inputs[name]) for name in _INS}
    arrays["in_consts"] = constants()
    args = [nc.dram_tensor(name, a.shape, F32, kind="ExternalInput").ap() for name, a in arrays.items()]
    args.append(nc.dram_tensor("out", (1, T, D), F32, kind="ExternalOutput").ap())
    block_kernel(nc, *args)
    r = _run(nc, [arrays], core_ids=[0])
    return r.results[0]["out"]
```

```python
from contextlib import ExitStack

import numpy as np

import concourse.bass as bass
from concourse import mybir
from concourse.alu_op_type import AluOpType as ALU

ACT = mybir.ActivationFunctionType
AX = mybir.AxisListType
F32 = mybir.dt.float32
BF16 = mybir.dt.bfloat16
I32 = mybir.dt.int32

P = 128
D = 2048
T = 256
KC = D // P
HEADS, NOPE, ROPE, VD = 8, 128, 64, 128
QL, KVL = 512, 256
CW = D - HEADS * VD
KR0 = QL + KVL
CONV0 = KR0 + ROPE
NE, NG, FF = 32, 4, 256
EPS = 1e-6
SCALE = float(NOPE + ROPE) ** -0.5
GRID_W = 64
ROUTED_SCALE = 2.5
TOP_K = 4
SLOTS = 64
PASSES = T // SLOTS
BIG = 1e30

C_ID, C_ONE, C_ROTQ, C_DUP, C_ROTK = 0, 128, 256, 384, 512
C_COS, C_SIN, C_SEL2, C_SUM4, C_TRI, C_IOTA, C_LOW, C_HALF = 640, 896, 1152, 1160, 1192, 1320, 1384, 1400
NCONST = 1401

V_AN, V_QN, V_KN, V_CW, V_OM, V_OC, V_FN = 0, 16, 20, 22, 46, 54, 62
NVEC = 78


def constants():
    c = np.zeros((P, NCONST), np.float32)
    c[:, C_ID:C_ID + P] = np.eye(P)
    c[:, C_ONE:C_ONE + P] = 1.0
    for j in range(P):
        w = j % 32
        source, sign = (j + 16, -1.0) if w < 16 else (j - 16, 1.0)
        c[source, C_ROTQ + j] = sign
        for half in range(2):
            c[64 * half + j % 64, C_DUP + j] = 1.0
            c[64 * half + source % 64, C_ROTK + j] = sign
    inv = (np.float32(10000.0) ** (-np.arange(16, dtype=np.float32) / np.float32(16))).astype(np.float32)
    token = np.arange(T)
    for j in range(P):
        place = (token // GRID_W if j % 64 < 32 else token % GRID_W).astype(np.float32)
        angle = (place * inv[j % 16]).astype(np.float32)
        c[j, C_COS:C_COS + T] = np.cos(angle)
        c[j, C_SIN:C_SIN + T] = np.sin(angle)
    for q in range(4):
        for v in range(2):
            c[32 * q + v, C_SEL2 + v] = 1.0
        for e in range(32):
            c[32 * q + e, C_SUM4 + e] = 1.0
    c[:, C_TRI:C_TRI + P] = np.triu(np.ones((P, P)), 1)
    c[:, C_IOTA:C_IOTA + SLOTS] = np.arange(SLOTS)
    c[:, C_LOW:C_LOW + NG * NG] = np.tril(np.ones((NG, NG)), -1).ravel()
    c[:, C_HALF] = -0.5
    return c


def block_kernel(nc, x, c, ctx_in, c_ctx, w_mod, b_mod, attn_norm, w_in, q_a_norm, w_q_b, kv_a_norm, w_kv_b,
                 conv_w, o_norm_mla, o_norm_conv, w_out, ffn_norm, w_router, router_bias,
                 w_exp_gate, w_exp_up, w_exp_down, w_sh_gate, w_sh_up, w_sh_down, final_norm, consts, out):
    with ExitStack() as stack:
        def sb(name, shape, dt=F32):
            return stack.enter_context(nc.sbuf_tensor(name, shape, dt))

        def sem(name):
            return stack.enter_context(nc.semaphore(name))

        xres = sb("xres", [P, 2, D])
        ring = sb("ring", [P, 6 * 4096])
        nreg = sb("nreg", [P, 8192])
        qkv = sb("qkv", [P, 2048])
        krT = sb("krT", [P, 2 * T])
        krs = sb("krs", [P, 2 * T])
        qnT = sb("qnT", [P, HEADS, T])
        part = sb("part", [P, 2, 512])
        modT = sb("modT", [P, 96, 2])
        csT = sb("csT", [P, KC, 32])
        cst = sb("cst", [P, NCONST])
        kq = sb("kq", [P, 2048])
        conv = sb("conv", [P, 1540])
        hb = sb("hb", [P, 2, D], BF16)
        vrow = sb("vrow", [P, P])
        brow = sb("brow", [P, P])
        crow = sb("crow", [32, P])
        csil = sb("csil", [32, P])
        vecT = sb("vecT", [P, NVEC])
        bT = sb("bT", [P, 96])
        amul = sb("amul", [P, KC, 2])
        amul2 = sb("amul2", [P, KC])
        stat = sb("stat", [P, 16])
        wr = sb("wr", [P, KC, NE])
        rb = sb("rb", [P, NE])
        sig = sb("sig", [P, 2, NE])
        sel = sb("sel", [P, 2, NE])
        mask = sb("mask", [P, 2, NE])
        scan = sb("scan", [P, 2, 2, NE])
        comb = sb("comb", [P, 2, NE])
        rank = sb("rank", [P, PASSES, 2, NE])
        top8 = sb("top8", [P, 10, 8])
        tiny = sb("tiny", [P, 160])
        more = sb("more", [P, NE // 2], I32)
        pick = sb("pick", [P, 2, 2 * SLOTS], BF16)

        slot = [ring[:, 4096 * s:4096 * (s + 1)] for s in range(6)]
        ctxs = slot[3].rearrange("p (t d) -> p t d", t=2)
        xs = slot[4].rearrange("p (t d) -> p t d", t=2)
        mslot = [ring[:, 3 * 4096 + 2048 * s:3 * 4096 + 2048 * (s + 1)].rearrange("p (k n) -> p k n", k=4)
                 for s in range(4)]
        aslot = [ring[:, 2048 * s:2048 * (s + 1)].rearrange("p (k n) -> p k n", k=4) for s in range(4)]
        oT = slot[5].rearrange("p (c t) -> p c t", c=KC)
        squ = slot[5][:, 0:2048]
        knT = slot[3].rearrange("p (h t) -> p h t", h=HEADS)
        vtok = slot[4].rearrange("p (k n) -> p k n", k=4)
        xh = slot[3].rearrange("p (t d) -> p t d", t=2)
        gu = ring[:, 0:16384].rearrange("p (q u g k n) -> p q u g k n", q=4, u=2, g=2, k=4)
        down = [slot[4 + u].rearrange("p (k n) -> p k n", k=2) for u in range(2)]

        wkr = kq[:, 0:1024].rearrange("p (k n) -> p k n", k=KC)
        rowq, rowkv = kq[:, 0:T], kq[:, T:3 * T]
        qrT = kq[:, 1024:2048].rearrange("p (h t) -> p h t", h=HEADS // 2)
        gcs = conv[:, 0:512].rearrange("p (m t) -> p m t", m=2)
        upad = conv[:, 512:1028].rearrange("p (m t) -> p m t", m=2)
        ycv = conv[:, 1028:1540].rearrange("p (m t) -> p m t", m=2)
        pickw = conv[:, 0:256].rearrange("p (t s) -> p t s", t=2)
        pickT = conv[:, 256:512]
        act = conv[:, 512:1024].rearrange("p (a f) -> p a f", a=2)
        actT = conv[:, 1024:1280].rearrange("p (k s) -> p k s", k=2)
        qaT = qkv[:, 0:1024].rearrange("p (c t) -> p c t", c=4)
        kvT = qkv[:, 1024:2048].rearrange("p (c t) -> p c t", c=2)
        gfB = qkv[:, :]
        nT = nreg[:, :].rearrange("p (c t) -> p c t", c=KC)
        prob = [nreg[:, 0:512], nreg[:, 512:1024], nreg[:, 7680:8192]]
        pT = nreg[:, 1024:3072].rearrange("p (b k q) -> p b k q", b=2, k=4)
        gaB = nreg[:, 3072:5120]
        sqr = nreg[:, 5120:6144].rearrange("p (b t) -> p b t", b=4)
        diag = nreg[:, 6144:7168].rearrange("p (b n) -> p b n", b=2)
        rconv = nreg[:, 7168:7424]
        rmla = nreg[:, 7424:7680]
        qraw = nreg[:, 7680:8192].rearrange("p (b t) -> p b t", b=2)
        hT = nreg[:, 0:4096].rearrange("p (c t) -> p c t", c=KC)
        yacc = nreg[:, 4096:8192].rearrange("p (t d) -> p t d", t=2)
        shT = krT[:, :].rearrange("p (k t) -> p k t", k=2)
        shS = krs[:, :].rearrange("p (k t) -> p k t", k=2)
        gainB = slot[0][:, 0:D]
        xg = nreg[:, 0:2048].rearrange("p (c s) -> p c s", c=KC)
        ye = nreg[:, 2048:4096]
        parts = [qnT[:, :, :].rearrange("p h t -> p (h t)").bitcast(BF16).rearrange("p (t d) -> p t d", t=2),
                 hb[:, :, :], kq[:, :].bitcast(BF16).rearrange("p (t d) -> p t d", t=2)]

        ident, ones = cst[:, C_ID:C_ID + P], cst[:, C_ONE:C_ONE + P]
        cosT, sinT = cst[:, C_COS:C_COS + T], cst[:, C_SIN:C_SIN + T]
        sel2, sum4 = cst[:, C_SEL2:C_SEL2 + 2], cst[:, C_SUM4:C_SUM4 + 32]
        before, iota = cst[:, C_TRI:C_TRI + P], cst[:, C_IOTA:C_IOTA + SLOTS]
        low = cst[:, C_LOW:C_LOW + NG * NG].rearrange("p (a b) -> p a b", a=NG)

        ps = stack.enter_context(nc.psum_tensor("ps", [P, 8, 512], F32))

        SCORE_BANK = (0, 1, 6)
        hsum = tiny[:, 140:148].rearrange("p (t n) -> p t n", t=2)
        finsum = tiny[:, 148:156].rearrange("p (t n) -> p t n", t=2)
        negmax, rowsum, rowmax, inverse = (tiny[:, 128:131], tiny[:, 131:134], tiny[:, 134:137], tiny[:, 137:140])

        small_in, x_in, ctx_ld, wkr_in, router_in, gain_in = (sem("small_in"), sem("x_in"), sem("ctx_ld"), sem("wkr_in"),
                                                     sem("router_in"), sem("gain_in"))
        w_full = [sem(f"w_full{s}") for s in range(6)]
        m_full = [sem(f"m_full{s}") for s in range(4)]
        m_used = [sem(f"m_used{s}") for s in range(4)]
        half_used = sem("half_used")
        zeroed, silu_c, small_T, small_done = sem("zeroed"), sem("silu_c"), sem("small_T"), sem("small_done")
        mod_rows, part_full, mod_cols, modT_done = (sem("mod_rows"), sem("part_full"), sem("mod_cols"),
                                                    sem("modT_done"))
        squares, xs_ready, amul_ready, xT_full, nT_lat, nT_ctx = (sem("squares"), sem("xs_ready"), sem("amul_ready"),
                                                                  sem("xT_full"), sem("nT_lat"), sem("nT_ctx"))
        q_full, q_out, q_sq = sem("q_full"), sem("q_out"), sem("q_sq")
        kv_full, kv_out, kv_sq = sem("kv_full"), sem("kv_out"), sem("kv_sq")
        kr_full, kr_sum, kr_mm, kr_done = (sem("kr_full"), sem("kr_sum"), sem("kr_mm"),
                                                   sem("kr_done"))
        stat_q, stat_kv, q_ready, kv_ready = (sem("stat_q"), sem("stat_kv"),
                                                        sem("q_ready"), sem("kv_ready"))
        conv_full, gc_out, u_out, y_out = sem("conv_full"), sem("gc_out"), sem("u_out"), sem("y_out")
        mods_ready, diag_ready, diag_used, gate_done = (sem("mods_ready"), sem("diag_ready"), sem("diag_used"),
                                                        sem("gate_done"))
        proj_full, proj_act, proj_dve = sem("proj_full"), sem("proj_act"), sem("proj_dve")
        rot_full, qr_ready = sem("rot_full"), sem("qr_ready")
        csq, csq_used, msq, msq_used = sem("csq"), sem("csq_used"), sem("msq"), sem("msq_used")
        oc_ready, om_ready = sem("oc_ready"), sem("om_ready")
        score_full, neg_max, exp_done, p_ready = sem("score_full"), sem("neg_max"), sem("exp_done"), sem("p_ready")
        pT_full, pT_out, o_full, o_out = sem("pT_full"), sem("pT_out"), sem("o_full"), sem("o_out")
        wo_half, wo_full, h_part = sem("wo_half"), sem("wo_full"), sem("h_part")
        hsq, xh_ready, xh_act, hT_full, hT_act, hT_dve = (sem("hsq"), sem("xh_ready"), sem("xh_act"), sem("hT_full"), sem("hT_act"),
                                                  sem("hT_dve"))
        split_act, split_ready = sem("split_act"), sem("split_ready")
        rt_rows, rt_copied, rt_full, rt_sig, mask_ready, rank_full, rank_ready = (
            sem("rt_rows"), sem("rt_copied"), sem("rt_full"), sem("rt_sig"), sem("mask_ready"), sem("rank_full"),
            sem("rank_ready"))
        sh_gate, sh_up, sh_silu, sh_act, sh_down = (sem("sh_gate"), sem("sh_up"), sem("sh_silu"), sem("sh_act"),
                                                          sem("sh_down"))
        gu_in = [sem(f"gu_in{q}") for q in range(4)]
        gu_used = [sem(f"gu_used{q}") for q in range(4)]
        down_in = [sem(f"down_in{n}") for n in range(4)]
        down_used = [sem(f"down_used{n}") for n in range(4)]
        pick_ready, pickw_ready, gx_full, gx_act, gx_dve, pickT_full, pickT_out = (
            sem("pick_ready"), sem("pickw_ready"), sem("gx_full"), sem("gx_act"), sem("gx_dve"), sem("pickT_full"),
            sem("pickT_out"))
        gu_full, silu_done, act_ready, actT_full, actT_out, dn_full, ye_out, sc_full, y_add = (
            sem("gu_full"), sem("silu_done"), sem("act_ready"), sem("actT_full"), sem("actT_out"), sem("dn_full"),
            sem("ye_out"), sem("sc_full"), sem("y_add"))
        mean_sq, root, mean_wide, root_wide = sem("mean_sq"), sem("root"), sem("mean_wide"), sem("root_wide")
        fin_h, fin_sq, fin_gain, fin_dve, fin_act, stored = (sem("fin_h"), sem("fin_sq"), sem("fin_gain"),
                                                             sem("fin_dve"), sem("fin_act"), sem("stored"))
        v_step = sem("v_step")

        wm = w_mod[0].rearrange("(c p) n -> p c n", p=P)
        wi = w_in[0].rearrange("(c p) n -> p c n", p=P)
        wq = w_q_b[0].rearrange("(c p) n -> p c n", p=P)
        wkv = w_kv_b[0].rearrange("(c p) n -> p c n", p=P)
        wo = w_out[0].rearrange("(c p) n -> p c n", p=P)
        wg = w_exp_gate[0].rearrange("e (c p) n -> p e c n", p=P)
        wu = w_exp_up[0].rearrange("e (c p) n -> p e c n", p=P)
        wd = w_exp_down[0].rearrange("e (c p) n -> p e c n", p=P)
        sg = w_sh_gate[0].rearrange("(c p) n -> p c n", p=P)
        su = w_sh_up[0].rearrange("(c p) n -> p c n", p=P)
        sd = w_sh_down[0].rearrange("(c p) n -> p c n", p=P)

        def k_of(s, k):
            return slot[s].rearrange("p (k n) -> p k n", k=k)

        FIRST = 0
        MOD_SLOTS = [0, 1, 2, 5]
        W_OUT = [(n, half) for n in range(4) for half in (1, 0)]
        USES = 10
        WO_USE = [((2, 0, 1)[j % 3], USES + j // 3 + 1) for j in range(len(W_OUT))]
        ATT_GROUP, OUT_GROUP = 16, 20

        def group_at(n, lag):
            at = n - 2 - lag
            return ATT_GROUP + 1 + at // 5 if at >= 0 and at % 5 == 0 else None

        SH_SLOT = (0, 1, 2, 0, 4, 5)
        SH_USE = (14, 13, 14, 15, 1, 5)

        block = stack.enter_context(nc.Block())

        @block.sync
        def _(sp):
            sp.dma_start(crow[0:KC, :], c.rearrange("b (c p) -> (b c) p", p=P)).then_inc(small_in, 16)
            sp.dma_start(crow[KC:2 * KC, :], c_ctx.rearrange("(c p) -> c p", p=P)).then_inc(small_in, 16)
            sp.dma_start(cst[:, :], consts).then_inc(small_in, 16)
            for at, src in ((V_AN, attn_norm[0]), (V_QN, q_a_norm[0]), (V_KN, kv_a_norm[0]), (V_OM, o_norm_mla[0]),
                            (V_OC, o_norm_conv[0]), (V_FN, ffn_norm[0])):
                n = src.shape[0] // P
                sp.dma_start(vrow[at:at + n, :], src.rearrange("(c p) -> c p", p=P)).then_inc(small_in, 16)
            sp.dma_start(vrow[V_CW:V_CW + 24, :], conv_w[0].rearrange("k (c p) -> (k c) p", p=P)).then_inc(small_in, 16)
            sp.dma_start(brow[0:96, :], b_mod[0].rearrange("(c p) -> c p", p=P)).then_inc(small_in, 16)

            def load_mod(g, u):
                for half in range(2):
                    s = MOD_SLOTS[2 * u + half]
                    sp.dma_start(k_of(s, 8), wm[:, 8 * half:8 * half + 8, bass.ds(g * 512, 512)])\
                      .then_inc(w_full[s], 16)

            load_mod(0, 0)
            sp.dma_start(xres[:, :, :], x[0].rearrange("(t p) d -> p t d", p=P)).then_inc(x_in, 16)
            sp.dma_start(ctxs, ctx_in[0].rearrange("(t p) d -> p t d", p=P)).then_inc(ctx_ld, 16)
            load_mod(1, 1)
            with sp.Fori(1, 4) as i:
                for u in range(2):
                    sp.wait_ge(mod_rows, 2 * i + u - 1)
                    load_mod(2 * i + u, u)

            sp.wait_ge(mod_rows, 7)
            for s in range(2):
                sp.dma_start(k_of(s, KC), wi[:, :, 256 * s:256 * s + 256]).then_inc(w_full[s], 16)
            sp.wait_ge(mod_rows, 8)
            sp.dma_start(k_of(2, KC), wi[:, :, 512:768]).then_inc(w_full[2], 16)
            sp.dma_start(wkr[:, :, :], wi[:, :, KR0:CONV0]).then_inc(wkr_in, 16)

            def load_group(i, u, slots_=mslot):
                for q in range(4):
                    if q == 3:
                        sp.wait_ge(mod_rows, 2 * i + u + 8)
                    elif not (i is FIRST and u == 0):
                        sp.wait_ge(m_used[q], 2 * i + u)
                    sp.dma_start(slots_[q], wm[:, 4 * q:4 * q + 4, bass.ds((2 * i + u + 8) * 512, 512)])\
                      .then_inc(m_full[q], 16)

            def load_conv(i, s, col):
                sp.dma_start(k_of(s, KC), wi[:, :, bass.ds(col + i * 256, 256)]).then_inc(w_full[s], 16)

            sp.wait_ge(nT_lat, KC)
            sp.wait_ge(nT_ctx, KC)
            load_group(FIRST, 0)
            sp.wait_ge(q_full, 2)
            load_conv(0, 0, CONV0 + CW)
            sp.wait_ge(q_full, 4)
            load_conv(0, 1, CONV0 + 2 * CW)
            sp.wait_ge(kv_full, 2)
            load_conv(0, 2, CONV0)
            load_group(FIRST, 1)
            with sp.Fori(1, 4) as i:
                sp.wait_ge(conv_full, 6 * i - 4)
                load_conv(i, 0, CONV0 + CW)
                load_group(i, 0)
                sp.wait_ge(conv_full, 6 * i - 2)
                load_conv(i, 1, CONV0 + 2 * CW)
                load_group(i, 1)
                sp.wait_ge(conv_full, 6 * i)
                load_conv(i, 2, CONV0)

            for s in range(2):
                sp.wait_ge(conv_full, 20 + 2 * s)
                sp.dma_start(slot[s][:, 0:3072].rearrange("p (k n) -> p k n", k=4), wq[:, :, 768 * s:768 * s + 768])\
                  .then_inc(w_full[s], 16)
            sp.wait_ge(conv_full, 24)
            sp.dma_start(k_of(2, 2), wkv).then_inc(w_full[2], 16)
            sp.dma_start(wr[:, :, :], w_router[0].rearrange("(c p) n -> p c n", p=P)).then_inc(router_in, 16)
            sp.dma_start(rb[:, :], router_bias.to_broadcast([P, NE])).then_inc(router_in, 16)

            def load_out(j):
                (n, half), (s, use) = W_OUT[j], WO_USE[j]
                if j >= 3:
                    sp.wait_ge(wo_full if j % 2 == 0 else wo_half, (j - 3) // 2 + 1)
                sp.dma_start(k_of(s, 8), wo[:, 8 * half:8 * half + 8, 512 * n:512 * n + 512]).then_inc(w_full[s], 16)

            def load_late(g, slots_):
                load_group(0, g - 8, slots_)

            sp.wait_ge(proj_full, 12)
            load_late(16, aslot)
            sp.wait_ge(proj_full, 28)
            load_out(0)
            for g in (17, 18, 19):
                load_late(g, aslot)
            for q in range(3):
                sp.wait_ge(m_used[q], 12)
            sp.wait_ge(mod_rows, 20)
            load_out(1)
            load_out(2)
            sp.wait_ge(score_full, 2 * HEADS)
            sp.wait_ge(o_full, HEADS)
            load_late(20, mslot)
            load_out(3)
            load_late(21, mslot)
            load_out(4)
            load_out(5)
            load_late(22, mslot)
            load_out(6)
            load_out(7)
            load_late(23, mslot)

            sp.wait_ge(wo_full, 3)
            sp.dma_start(k_of(1, KC), su[:, :, 0:FF]).then_inc(w_full[1], 16)
            sp.wait_ge(wo_half, 4)
            sp.dma_start(k_of(2, KC), sg[:, :, FF:2 * FF]).then_inc(w_full[2], 16)
            sp.wait_ge(m_used[2], 16)
            sp.wait_ge(mod_rows, 24)
            sp.dma_start(k_of(4, 2), sd[:, 0:2, :]).then_inc(w_full[4], 16)
            sp.wait_ge(wo_full, 4)
            sp.dma_start(k_of(0, KC), sg[:, :, 0:FF]).then_inc(w_full[0], 16)
            sp.dma_start(k_of(5, 2), sd[:, 2:4, :]).then_inc(w_full[5], 16)
            sp.wait_ge(sh_gate, 2)
            sp.dma_start(k_of(0, KC), su[:, :, FF:2 * FF]).then_inc(w_full[0], 16)

            def load_quarter(i, q):
                for u in range(2):
                    for g, src in ((0, wg), (1, wu)):
                        sp.dma_start(gu[:, q, u, g, :, :].rearrange("p k n -> p (k n)").rearrange("p (k n) -> p k n", k=4),
                                     src[:, bass.ds(2 * i + u, 1), 4 * q:4 * q + 4, :]
                                     .rearrange("p a c n -> p (a c) n")).then_inc(gu_in[q], 16)

            def load_down(i, n, u):
                sp.dma_start(down[u][:, :, 512 * n:512 * n + 512],
                             wd[:, bass.ds(2 * i + u, 1), :, 512 * n:512 * n + 512]
                             .rearrange("p a c n -> p (a c) n")).then_inc(down_in[n], 16)

            sp.wait_ge(sh_up, 2)
            load_quarter(0, 1)
            sp.wait_ge(hT_full, 8)
            sp.wait_ge(split_ready, 2)
            load_quarter(0, 3)
            sp.wait_ge(sh_gate, 4)
            load_quarter(0, 2)
            sp.wait_ge(sh_down, 8)
            for n in range(4):
                load_down(0, n, 0)
            sp.wait_ge(sh_up, 4)
            load_quarter(0, 0)
            sp.wait_ge(sh_down, 16)
            for n in range(4):
                load_down(0, n, 1)
            with sp.Fori(1, NE // 2) as i:
                for q in range(4):
                    sp.wait_ge(gu_used[q], i)
                    load_quarter(i, q)
                for n in range(4):
                    sp.wait_ge(down_used[n], i)
                    for u in range(2):
                        load_down(i, n, u)

            sp.wait_ge(gu_used[0], NE // 2)
            sp.dma_start(gainB, final_norm.rearrange("(a d) -> a d", a=1).to_broadcast([P, D])).then_inc(gain_in, 16)

            for half in range(2):
                for t, done in ((0, fin_dve), (1, fin_act)):
                    sp.wait_ge(done, 2 * half + 2)
                    cols = slice(1024 * half, 1024 * half + 1024)
                    sp.dma_start(out[0].rearrange("(t p) d -> p t d", p=P)[:, t, cols], xres[:, t, cols])\
                      .then_inc(stored, 16)
            sp.wait_ge(stored, 64)

        @block.gpsimd
        def _(pool):
            nc.gpsimd.memset(csT[:, :, :], 0.0).then_inc(zeroed, 1)
            nc.gpsimd.memset(upad[:, :, :], 0.0).then_inc(zeroed, 1)

            roots = [0]

            def power(v):
                roots[0] += 1
                pool.wait_ge(mean_sq, roots[0])
                nc.gpsimd.tensor_tensor(v, v, cst[:, C_HALF:C_HALF + 1].to_broadcast(list(v.shape)), ALU.pow)\
                    .then_inc(root, 1)

            power(tiny[:, 8:12])

            for m in range(8):
                if m % 4 == 0:
                    pool.wait_ge(mods_ready, m // 4 + 1)
                if m >= 2:
                    pool.wait_ge(diag_used, m - 1)
                for j in range(4):
                    at = (2 if m < 4 else 5) * KC + 4 * (m % 4) + j
                    ins = nc.gpsimd.tensor_scalar(diag[:, m % 2, 128 * j:128 * j + 128], ident, modT[:, at, 0:1],
                                                  None, ALU.mult)
                ins.then_inc(diag_ready, 1)
                if m == 3:
                    power(stat[:, 10:12])
            pool.wait_ge(gain_in, 16)
            for n in range(4):
                pool.wait_ge(fin_h, 2 * n + 2)
                nc.gpsimd.tensor_tensor(yacc[:, 1, 512 * n:512 * n + 512], xres[:, 1, 512 * n:512 * n + 512],
                                        gainB[:, 512 * n:512 * n + 512], ALU.mult).then_inc(fin_gain, 1)
            power(stat[:, 14:16])

        @block.tensor
        def _(pe):
            def mm(o, l, r, start, stop):
                return nc.tensor.matmul(o, l, r, start=start, stop=stop)

            pe.wait_ge(silu_c, 1)
            nc.tensor.transpose(ps[:, 7, 0:32], csil[:, :], ident[0:32, 0:32])
            nc.tensor.transpose(ps[:, 7, 64:64 + NVEC], vrow[0:NVEC, :], ident[0:NVEC, 0:NVEC])
            nc.tensor.transpose(ps[:, 7, 256:352], brow[0:96, :], ident[0:96, 0:96]).then_inc(small_T, 1)
            pe.wait_ge(small_done, 1)

            def mod_cols_of(n, b):
                pe.wait_ge(part_full, n + 1)
                if n is not FIRST:
                    pe.wait_ge(modT_done, n)
                for j in range(4):
                    ins = nc.tensor.transpose(ps[:, 5, 128 * j:128 * j + 128], part[:, b, 128 * j:128 * j + 128], ident)
                ins.then_inc(mod_cols, 1)

            def first_groups(i, first):
                for u in range(2):
                    if not first:
                        pe.wait_ge(part_full, 2 * i + u - 1)
                    for half in range(2):
                        s = MOD_SLOTS[2 * u + half]
                        w = k_of(s, 8)
                        pe.wait_ge(w_full[s], 16 * i + 16)
                        for k in range(8):
                            q = k % 4
                            ins = mm(ps[32 * q:32 * q + 32, 6 + u, :], csT[:, 8 * half + k, :], w[:, k, :],
                                     half == 0 and k < 4, half == 1 and k >= 4)
                    ins.then_inc(mod_rows, 1)
                for u in range(2):
                    mod_cols_of(FIRST if first and u == 0 else 2 * i + u, u)

            first_groups(FIRST, True)
            with pe.Fori(1, 4) as i:
                first_groups(i, False)

            pe.wait_ge(xs_ready, 4)
            for k in range(KC):
                if k >= 2:
                    pe.wait_ge(nT_lat, k - 1)
                    pe.wait_ge(nT_ctx, k - 1)
                for t in range(4):
                    src = (xs if t < 2 else ctxs)[:, t % 2, 128 * k:128 * k + 128]
                    ins = nc.tensor.transpose(ps[:, 2 * (k % 2) + t // 2, 128 * (t % 2):128 * (t % 2) + 128], src, ident)
                ins.then_inc(xT_full, 1)

            pe.wait_ge(nT_lat, KC)
            pe.wait_ge(nT_ctx, KC)
            for m in range(4):
                w = k_of(m // 2, KC)
                pe.wait_ge(w_full[m // 2], 16 * 5)
                for k in range(KC):
                    ins = mm(ps[:, m, 0:T], w[:, k, 128 * (m % 2):128 * (m % 2) + 128], nT[:, k, 0:T], k == 0, k == KC - 1)
                ins.then_inc(q_full, 1)
            pe.wait_ge(w_full[2], 16 * 5)
            pe.wait_ge(modT_done, 8)
            pe.wait_ge(part_full, 8)
            w = k_of(2, KC)
            for m in range(2):
                for k in range(KC):
                    ins = mm(ps[:, 6 - m, :], w[:, k, 128 * m:128 * m + 128], nT[:, k, :], k == 0, k == KC - 1)
                ins.then_inc(kv_full, 1)
            pe.wait_ge(wkr_in, 16)
            for k in range(KC):
                r = 64 * (k % 2)
                ins = mm(ps[r:r + 64, 7, :], wkr[:, k, :], nT[:, k, :], k < 2, k >= 14)
            ins.then_inc(kr_full, 1)
            pe.wait_ge(q_sq, 4)
            pe.wait_ge(q_out, 4)
            for m in range(4):
                ins = mm(ps[:, 0, 0:T], ones, squ[:, T * m:T * m + T], m == 0, m == 3)
            ins.then_inc(stat_q, 1)
            pe.wait_ge(kv_sq, 2)
            for m in range(2):
                ins = mm(ps[:, 1, :], ones, squ[:, 1024 + 512 * m:1536 + 512 * m], m == 0, m == 1)
            ins.then_inc(stat_kv, 1)
            pe.wait_ge(kr_sum, 1)
            mm(ps[:, 2, :], cst[:, C_DUP:C_DUP + P], krs[:, :], True, True)
            mm(ps[:, 3, 0:T], cst[:, C_ROTK:C_ROTK + P], krs[:, 0:T], True, True).then_inc(kr_mm, 1)

            pe.wait_ge(mean_wide, 2)
            pe.wait_ge(kr_done, 1)
            pe.wait_ge(kv_out, 2)

            def conv_blocks(i, s, first_bank):
                pe.wait_ge(w_full[s], 16 * i + 16 * 6)
                w = k_of(s, KC)
                for m in range(2):
                    for k in range(KC):
                        ins = mm(ps[:, first_bank + m, 0:T], w[:, k, 128 * m:128 * m + 128], nT[:, k, 0:T],
                                 k == 0, k == KC - 1)
                    ins.then_inc(conv_full, 1)

            def group_rows(i, u, slots_, bank):
                for k in range(KC):
                    q = k // 4
                    if k % 4 == 0:
                        pe.wait_ge(m_full[q], 16 * (2 * i + u) + 16)
                    ins = mm(ps[32 * (k % 4):32 * (k % 4) + 32, bank, :], csT[:, k, :], slots_[q][:, k % 4, :],
                             k < 4, k >= 12)
                    if k % 4 == 3:
                        ins.then_inc(m_used[q] if q < 3 else mod_rows, 1)

            with pe.Fori(0, 4) as i:
                conv_blocks(i, 0, 0)
                pe.wait_ge(part_full, 2 * i + 7)
                group_rows(i, 0, mslot, 6)
                conv_blocks(i, 1, 2)
                pe.wait_ge(part_full, 2 * i + 8)
                group_rows(i, 1, mslot, 7)
                mod_cols_of(2 * i + 8, 0)
                pe.wait_ge(gc_out, 2 * i + 2)
                conv_blocks(i, 2, 0)
                mod_cols_of(2 * i + 9, 1)
                pe.wait_ge(y_out, 2 * i + 2)
            pe.wait_ge(u_out, 8)

            def project(j, width, steps):
                if j >= 4:
                    pe.wait_ge(proj_dve if j % 2 else proj_act, (j - 4) // 2 + 1)
                for n, (ls, r) in enumerate(steps):
                    for u, l in enumerate(ls):
                        rows_ = slice(P // len(ls) * u, P // len(ls) * (u + 1))
                        ins = mm(ps[rows_, j % 4, 0:width], l, r, n == 0, n == len(steps) - 1)
                ins.then_inc(proj_full, 1)

            def rotate(p):
                pe.wait_ge(proj_act, 3 * (p // 2) + p % 2 + 1)
                if p >= 2:
                    pe.wait_ge(qr_ready, p - 1)
                mm(ps[:, 6 + p % 2, 0:T], cst[:, C_ROTQ:C_ROTQ + P], qraw[:, p % 2, :], True, True).then_inc(rot_full, 1)

            pe.wait_ge(q_ready, 1)
            for s in range(2):
                w = slot[s][:, 0:3072].rearrange("p (k h n) -> p k h n", k=4, h=4)
                pe.wait_ge(w_full[s], 16 * USES)
                for n, (rope, h) in enumerate(((True, 0), (False, 0), (True, 2), (False, 1), (False, 2), (False, 3))):
                    lhs = [[w[:, k, h + u, NOPE:NOPE + ROPE] for u in range(2)] if rope else [w[:, k, h, 0:NOPE]]
                           for k in range(4)]
                    project(6 * s + n, T, [(lhs[k], qaT[:, k, :]) for k in range(4)])
                    if n == 3:
                        rotate(2 * s)
                rotate(2 * s + 1)
            def gates(ms):
                for m in ms:
                    pe.wait_ge(diag_ready, m + 1)
                    if m >= 2:
                        pe.wait_ge(gate_done, m - 1)
                    mm(ps[:, 6 + m % 2, :], ones, diag[:, m % 2, :], True, True).then_inc(diag_used, 1)

            def conv_square(k):
                pe.wait_ge(csq, k + 1)
                mm(ps[:, 5, 0:T], ones, sqr[:, k % 4, :], k == 0, k == 7).then_inc(csq_used, 1)

            pe.wait_ge(kv_ready, 1)
            pe.wait_ge(w_full[2], 16 * USES)
            pe.wait_ge(modT_done, 16)
            w = slot[2].rearrange("p (k h n) -> p k h n", k=2, h=HEADS)
            for h in range(HEADS):
                project(12 + h, 2 * T, [([w[:, k, h, 0:NOPE]], kvT[:, k, :]) for k in range(2)])
                if h >= 2:
                    conv_square(h - 2)
            pe.wait_ge(qr_ready, 4)
            for t in range(4):
                for n in range(2):
                    project(20 + 2 * t + n, 512, [([kvT[:, k, 128 * t:128 * t + 128]],
                                                   w[:, k, 4 * n:4 * n + 4, NOPE:NOPE + VD]) for k in range(2)])
                if t < 2:
                    conv_square(6 + t)
                gates((t,))

            def late_rows(g, slots_):
                pe.wait_ge(modT_done, g)
                group_rows(0, g - 8, slots_, 5)

            pe.wait_ge(mean_wide, 3)
            late_rows(ATT_GROUP, aslot)

            pe.wait_ge(proj_act, 14)
            pe.wait_ge(proj_dve, 14)

            def scores(n):
                h, t = n // 2, n % 2
                r = 64 * (h % 2)
                if n >= 3:
                    pe.wait_ge(exp_done, n - 2)
                elif n == 2:
                    pe.wait_ge(gate_done, 3)
                bank = SCORE_BANK[n % 3]
                mm(ps[:, bank, :], qnT[:, h, 128 * t:128 * t + 128], knT[:, h, :], True, False)
                mm(ps[:, bank, :], qrT[r:r + 64, h // 2, 128 * t:128 * t + 128], krT[r:r + 64, :], False, True)\
                    .then_inc(score_full, 1)

            def head_square(h):
                if h == 0:
                    pe.wait_ge(gate_done, 4)
                pe.wait_ge(msq, h + 1)
                mm(ps[:, 7, 0:T], ones, sqr[:, h % 4, :], h == 0, h == 7).then_inc(msq_used, 1)

            scores(0)
            scores(1)
            scores(2)
            mod_cols_of(ATT_GROUP, 0)
            for n in range(2 * HEADS):
                h = n // 2
                pe.wait_ge(p_ready, n + 1)
                if n >= 2:
                    pe.wait_ge(pT_out, n - 1)
                for k in range(4):
                    ins = nc.tensor.transpose(ps[:, 2 + n % 2, 128 * k:128 * k + 128],
                                              prob[n % 3][:, 128 * k:128 * k + 128], ident)
                ins.then_inc(pT_full, 1)
                if n + 3 < 2 * HEADS:
                    scores(n + 3)
                if group_at(n, 0):
                    late_rows(group_at(n, 0), aslot)
                if group_at(n, 2):
                    mod_cols_of(group_at(n, 2), group_at(n, 2) % 2)
                if n % 2:
                    pe.wait_ge(pT_out, n + 1)
                    if h:
                        pe.wait_ge(o_out, h)
                    for k in range(4):
                        ins = mm(ps[:, 4, 0:T], vtok[:, k, 128 * h:128 * h + 128], pT[:, h % 2, k, :],
                                 k == 0, k == 3)
                    ins.then_inc(o_full, 1)
                    if h:
                        head_square(h - 1)
            head_square(HEADS - 1)

            pe.wait_ge(oc_ready, 8)
            for (n, half), (s, use) in zip(W_OUT, WO_USE):
                pe.wait_ge(w_full[s], 16 * use)
                if n >= 2 and half == 1:
                    pe.wait_ge(h_part, 2 * (n - 1))
                w = k_of(s, 8)
                for k in range(8):
                    if half == 0:
                        pe.wait_ge(om_ready, k + 1)
                    for t in range(2):
                        ins = mm(ps[:, 2 * (n % 2) + t, :], oT[:, 8 * half + k, 128 * t:128 * t + 128], w[:, k, :],
                                 half == 1 and k == 0, half == 0 and k == 7)
                ins.then_inc(wo_full if half == 0 else wo_half, 1)
                if half == 1:
                    late_rows(OUT_GROUP + n, mslot)
                else:
                    mod_cols_of(OUT_GROUP + n, n % 2)

            for b in range(8):
                if b % 2 == 0:
                    pe.wait_ge(xh_ready, b // 2 + 1)
                    pe.wait_ge(xh_act, b // 2 + 1)
                if b >= 4:
                    pe.wait_ge(hT_dve if b % 2 else hT_act, (b - 4) // 2 + 1)
                for j in range(2):
                    for t in range(2):
                        k = 2 * b + j
                        ins = nc.tensor.transpose(ps[:, b % 4, 256 * j + 128 * t:256 * j + 128 * t + 128],
                                                  xh[:, t, 128 * k:128 * k + 128], ident)
                ins.then_inc(hT_full, 1)

            pe.wait_ge(router_in, 32)
            for k in range(KC):
                if k % 2 == 0:
                    pe.wait_ge(hT_dve if k % 4 else hT_act, k // 4 + 1)
                q = k % 4
                ins = mm(ps[32 * q:32 * q + 32, 4, 0:T], wr[:, k, :], hT[:, k, :], k < 4, k >= 12)
            ins.then_inc(rt_rows, 1)
            pe.wait_ge(rt_copied, 1)
            for t in range(2):
                ins = mm(ps[:, 5, 32 * t:32 * t + 32], part[:, 0, 128 * t:128 * t + 128], sum4, True, True)
            ins.then_inc(rt_full, 1)
            def gather(t, banks, last=False):
                for b in banks:
                    if b == 0:
                        pe.wait_ge(pick_ready, t + 1)
                    if b >= 2:
                        pe.wait_ge((gx_act, gx_dve)[b % 2], 2 * t + 1)
                    for j in range(4):
                        k = 4 * b + j
                        for n in range(6):
                            ins = mm(ps[:, b % 2, 128 * j:128 * j + 128], parts[n % 3][:, n // 3, 128 * k:128 * k + 128],
                                     pick[:, n // 3, :], n == 0, n == 5)
                            if last and b == j == n == 0:
                                ins.then_inc(gu_used[3], 1)
                    ins.then_inc(gx_full, 1)

            for u in range(2):
                if u:
                    pe.wait_ge(sh_act, 2)
                for i, base, full in ((2 * u, 0, sh_gate), (2 * u + 1, 2, sh_up)):
                    s = SH_SLOT[i]
                    w = k_of(s, KC)
                    pe.wait_ge(w_full[s], 16 * SH_USE[i])
                    for m in range(2):
                        for k in range(KC):
                            ins = mm(ps[:, base + m, 0:T], w[:, k, 128 * m:128 * m + 128], hT[:, k, :],
                                     k == 0, k == KC - 1)
                        ins.then_inc(full, 1)
                    if u == 0:
                        gates((4, 5) if full is sh_gate else (6, 7))
                w = k_of(4 + u, 2)
                pe.wait_ge(w_full[4 + u], 16 * SH_USE[4 + u])
                pe.wait_ge(sh_act, 2 * u + 2)
                if u == 1:
                    gather(0, (0, 1))
                    pe.wait_ge(rank_ready, 1)
                for j in range(8):
                    t, m = j // 4, j % 4
                    if 8 * u + j >= 4:
                        pe.wait_ge(y_add, 8 * u + j - 3)
                    elif m >= 2:
                        pe.wait_ge(gate_done, m + 5)
                    for k in range(2):
                        ins = mm(ps[:, 4 + m, :], shT[:, k, 128 * t:128 * t + 128], w[:, k, 512 * m:512 * m + 512],
                                 k == 0, k == 1)
                    ins.then_inc(sh_down, 1)
                if u == 0:
                    pe.wait_ge(mask_ready, 1)
                    pe.wait_ge(y_add, 6)
                    mm(ps[:, 5, 0:32], before, mask[:, 0, :], True, True)
                    mm(ps[:, 5, 32:64], ones, mask[:, 0, :], True, False)
                    mm(ps[:, 5, 32:64], before, mask[:, 1, :], False, True)
                    mm(ps[:, 5, 64:96], ones, mask[:, 0, :], True, False)
                    mm(ps[:, 5, 64:96], ones, mask[:, 1, :], False, True).then_inc(rank_full, 1)
            gather(0, (2, 3))

            def pair_pass(i, t, last, ahead=True):
                pe.wait_ge(pickw_ready, t + 1)
                for j in range(2):
                    ins = nc.tensor.transpose(ps[:, 3, 128 * j:128 * j + 128], pickw[:, j, :], ident)
                ins.then_inc(pickT_full, 1)
                for q in range(4):
                    pe.wait_ge(gu_in[q], 64 * i + 64)
                    pe.wait_ge((gx_act, gx_dve)[q % 2], 2 * t + (q // 2 + 1))
                    for k in range(4):
                        for u in range(2):
                            ins = mm(ps[64 * u:64 * u + 64, 2, :], xg[:, 4 * q + k, 64 * u:64 * u + 64],
                                     gu[:, q, u, :, k, :], q == 0 and k == 0, q == 3 and k == 3)
                    if q == 3:
                        ins.then_inc(gu_full, 1)
                    elif last:
                        ins.then_inc(gu_used[q], 1)
                if ahead:
                    gather(t + 1, (0, 1), last)
                pe.wait_ge(act_ready, t + 1)
                for k in range(2):
                    ins = nc.tensor.transpose(ps[:, 3, 256 + 128 * k:384 + 128 * k], act[:, 1, 128 * k:128 * k + 128], ident)
                ins.then_inc(actT_full, 1)
                if ahead:
                    gather(t + 1, (2, 3))
                pe.wait_ge(actT_out, t + 1)

                def scatter(n):
                    pe.wait_ge(ye_out, 4 * t + (n + 1))
                    for h in range(2):
                        m = 2 * n + h
                        pe.wait_ge(y_add, 8 * t + (16 + max(m - 1, 0)))
                        ins = mm(ps[:, 6 + h, :], pickT[:, 128 * h:128 * h + 128], ye[:, 512 * n:512 * n + 512], True, True)
                        if n < 3 and h == 0 and last:
                            ins.then_inc(down_used[n + 1], 1)
                    ins.then_inc(sc_full, 1)

                for n in range(4):
                    pe.wait_ge(down_in[n], 32 * i + 32)
                    if n >= 2:
                        pe.wait_ge(ye_out, 4 * t + (n - 1))
                    for k in range(2):
                        for u in range(2):
                            ins = mm(ps[64 * u:64 * u + 64, 4 + n % 2, :], actT[:, k, 64 * u:64 * u + 64],
                                     down[u][:, k, 512 * n:512 * n + 512], k == 0, k == 1)
                            if n == 1 and k == u == 0 and last:
                                ins.then_inc(down_used[0], 1)
                    ins.then_inc(dn_full, 1)
                    if n == 0:
                        pe.wait_ge(pickT_out, t + 1)
                    else:
                        scatter(n - 1)
                scatter(3)

            passes = pe.alloc_register("pe_passes")
            pe.reg_mov(passes, 0)
            pe.wait_ge(rank_ready, 1)
            pe.wait_ge(y_add, 16)

            def extra_passes(i):
                extra = pe.value_load(more[0:1, bass.ds(i, 1)], min_val=0, max_val=PASSES - 1)
                with pe.If(extra > 0):
                    with pe.Fori(0, extra):
                        pair_pass(i, pe.snap(passes, min_val=0, max_val=64), False)
                        pe.reg_add(passes, passes, 1)

            with pe.Fori(0, NE // 2 - 1) as i:
                extra_passes(i)
                pair_pass(i, pe.snap(passes, min_val=0, max_val=64), True)
                pe.reg_add(passes, passes, 1)
            extra_passes(NE // 2 - 1)
            pair_pass(NE // 2 - 1, pe.snap(passes, min_val=0, max_val=64), True, ahead=False)

        @block.scalar
        def _(sc):
            def copy(o, i_):
                return nc.scalar.activation(o, i_, ACT.Copy)

            sc.wait_ge(small_in, 16 * 11)
            nc.scalar.activation(csil[:, :], crow[:, :], ACT.Silu).then_inc(silu_c, 1)

            sc.wait_ge(x_in, 16)
            for t in range(2):
                nc.scalar.activation(nreg[:, 2048 * t:2048 * t + 2048], xres[:, t, :], ACT.Square,
                                     accum_out=stat[:, t:t + 1]).then_inc(squares, 1)
            sc.wait_ge(ctx_ld, 16)
            for t in range(2):
                nc.scalar.activation(nreg[:, 2048 * t + 4096:2048 * t + 6144], ctxs[:, t, :], ACT.Square,
                                     accum_out=stat[:, t + 2:t + 3]).then_inc(squares, 1)

            def rows_out(n, bank, b, first):
                sc.wait_ge(mod_rows, n + 1)
                if not first:
                    sc.wait_ge(mod_cols, n - 1)
                copy(part[:, b, :], ps[:, bank, :]).then_inc(part_full, 1)

            rows_out(0, 6, 0, True)
            rows_out(1, 7, 1, True)
            with sc.Fori(1, 4) as i:
                rows_out(2 * i, 6, 0, False)
                rows_out(2 * i + 1, 7, 1, False)

            sc.wait_ge(amul_ready, 1)
            for k in range(KC):
                sc.wait_ge(xT_full, k + 1)
                nc.scalar.activation(nT[:, k, T:2 * T], ps[:, 2 * (k % 2) + 1, 0:T], ACT.Identity, bias=modT[:, k, 1:2],
                                     scale=amul[:, k, 1:2]).then_inc(nT_ctx, 1)

            for m in range(4):
                sc.wait_ge(q_full, m + 1)
                nc.scalar.activation(squ[:, T * m:T * m + T], ps[:, m, 0:T], ACT.Square).then_inc(q_sq, 1)
            for m in range(2):
                sc.wait_ge(kv_full, m + 1)
                nc.scalar.activation(squ[:, 1024 + 512 * m:1536 + 512 * m], ps[:, 6 - m, :], ACT.Square).then_inc(kv_sq, 1)
            sc.wait_ge(kr_full, 1)
            copy(krs[:, :], ps[:, 7, :]).then_inc(kr_sum, 1)

            wide = [0]

            def square_root(v):
                wide[0] += 1
                sc.wait_ge(mean_wide, wide[0])
                nc.scalar.activation(v, v, ACT.Sqrt).then_inc(root_wide, 1)

            square_root(rowq)
            square_root(rowkv)

            with sc.Fori(0, 4) as i:
                for m in range(2):
                    sc.wait_ge(conv_full, 6 * i + m + 1)
                    copy(gcs[:, m, :], ps[:, m, 0:T]).then_inc(gc_out, 1)
                for u in range(2):
                    rows_out(2 * i + u + 8, 6 + u, u, False)

            for j in range(0, 28, 2):
                sc.wait_ge(proj_full, j + 1)
                bank = ps[:, j % 4, :]
                if j < 12:
                    s, n = j // 6, j % 6
                    if n == 4:
                        dst, src = qnT[:, 4 * s + 2, :], bank[:, 0:T]
                    else:
                        p = 2 * s + n // 2
                        if p >= 2:
                            sc.wait_ge(qr_ready, p - 1)
                        dst, src = qraw[:, p % 2, :], bank[:, 0:T]
                elif j < 20:
                    dst, src = knT[:, j - 12, :], bank
                else:
                    t, n = (j - 20) // 2, j % 2
                    dst, src = vtok[:, t, 512 * n:512 * n + 512], bank
                copy(dst, src).then_inc(proj_act, 1)
                for k in {10: (0, 1), 12: (2, 3), 14: (4,), 16: (5,), 18: (6, 7)}.get(j, ()):
                    if k == 0:
                        sc.wait_ge(y_out, 8)
                    if k >= 4:
                        sc.wait_ge(csq_used, k - 3)
                    nc.scalar.activation(sqr[:, k % 4, :], oT[:, 8 + k, :], ACT.Square).then_inc(csq, 1)
                if j == 26:
                    square_root(rconv)

            rows_out(ATT_GROUP, 5, 0, False)

            def exponentials(n):
                sc.wait_ge(neg_max, n + 1)
                b = n % 3
                if n >= 3:
                    sc.wait_ge(pT_full, n - 2)
                nc.scalar.activation(prob[b], ps[:, SCORE_BANK[b], :], ACT.Exp, bias=negmax[:, b:b + 1],
                                     scale=SCALE, accum_out=rowsum[:, b:b + 1]).then_inc(exp_done, 1)

            def head_square(h):
                sc.wait_ge(o_out, h + 1)
                if h >= 4:
                    sc.wait_ge(msq_used, h - 3)
                nc.scalar.activation(sqr[:, h % 4, :], oT[:, h, :], ACT.Square).then_inc(msq, 1)

            sc.wait_ge(csq_used, 8)
            exponentials(0)
            exponentials(1)
            for n in range(2 * HEADS):
                h = n // 2
                if n + 2 < 2 * HEADS:
                    exponentials(n + 2)
                sc.wait_ge(pT_full, n + 1)
                if h >= 2:
                    sc.wait_ge(o_full, h - 1)
                copy(pT[:, h % 2, :, 128 * (n % 2):128 * (n % 2) + 128],
                     ps[:, 2 + n % 2, :].rearrange("p (k q) -> p k q", k=4)).then_inc(pT_out, 1)
                if n % 2 and h:
                    head_square(h - 1)
                if group_at(n, 1):
                    rows_out(group_at(n, 1), 5, group_at(n, 1) % 2, False)
            head_square(HEADS - 1)
            square_root(rmla)
            for n in range(4):
                rows_out(OUT_GROUP + n, 5, n % 2, False)
                for t in range(2):
                    sc.wait_ge(h_part, 2 * n + t + 1)
                    if n:
                        sc.wait_ge(hsq, 2 * n + t - 1)
                    nc.scalar.activation(nreg[:, 1024 + 512 * t:1536 + 512 * t], xres[:, t, 512 * n:512 * n + 512],
                                         ACT.Square, accum_out=hsum[:, t, n:n + 1]).then_inc(hsq, 1)

            sc.wait_ge(root, 2)
            sc.wait_ge(mods_ready, 2)
            for n in range(4):
                nc.scalar.activation(xh[:, 1, 512 * n:512 * n + 512], xres[:, 1, 512 * n:512 * n + 512], ACT.Identity,
                                     scale=stat[:, 11:12]).then_inc(xh_act, 1)

            for b in range(0, 8, 2):
                sc.wait_ge(hT_full, b + 1)
                for k in (2 * b, 2 * b + 1):
                    ins = nc.scalar.activation(hT[:, k, :], ps[:, b % 4, T * (k % 2):T * (k % 2) + T], ACT.Identity,
                                               bias=modT[:, 3 * KC + k, 0:1], scale=amul2[:, k:k + 1])
                ins.then_inc(hT_act, 1)
            sc.wait_ge(hT_full, 8)
            sc.wait_ge(rt_rows, 1)
            copy(part[:, 0, 0:T], ps[:, 4, 0:T]).then_inc(rt_copied, 1)
            sc.wait_ge(rt_full, 1)
            nc.scalar.activation(sig[:, :, :], ps[:, 5, 0:64].rearrange("p (t e) -> p t e", t=2), ACT.Sigmoid)\
                .then_inc(rt_sig, 1)

            for t in range(2):
                copy(parts[0][:, t, :], xh[:, t, :]).then_inc(split_act, 1)

            for n in range(4):
                sc.wait_ge(sh_gate, n + 1)
                if n >= 2:
                    sc.wait_ge(sh_act, n - 1)
                nc.scalar.activation(shS[:, n % 2, :], ps[:, n % 2, 0:T], ACT.Silu).then_inc(sh_silu, 1)
                if n == 1:
                    for m in range(4, 8):
                        sc.wait_ge(diag_used, m + 1)
                        copy(gfB[:, 512 * (m - 4):512 * (m - 4) + 512], ps[:, 6 + m % 2, :]).then_inc(gate_done, 1)

            def tokens_out(t, b):
                sc.wait_ge(gx_full, 4 * t + (b + 1))
                for j in range(4):
                    k = 4 * b + j
                    ins = nc.scalar.activation(xg[:, k, :], ps[:, b % 2, 128 * j:128 * j + 128], ACT.Identity,
                                               bias=modT[:, 3 * KC + k, 0:1], scale=amul2[:, k:k + 1])
                ins.then_inc(gx_act, 1)

            def pair_pass(t, ahead=True):
                sc.wait_ge(pickT_full, t + 1)
                copy(pickT[:, :], ps[:, 3, 0:256]).then_inc(pickT_out, 1)
                sc.wait_ge(gu_full, t + 1)
                nc.scalar.activation(act[:, 0, :], ps[:, 2, 0:FF], ACT.Silu).then_inc(silu_done, 1)
                if ahead:
                    tokens_out(t + 1, 0)
                sc.wait_ge(actT_full, t + 1)
                copy(actT[:, :, :].rearrange("p k s -> p (k s)"), ps[:, 3, 256:512]).then_inc(actT_out, 1)
                if ahead:
                    tokens_out(t + 1, 2)
                for n in range(4):
                    sc.wait_ge(dn_full, 4 * t + (n + 1))
                    copy(ye[:, 512 * n:512 * n + 512], ps[:, 4 + n % 2, :]).then_inc(ye_out, 1)
                    if not ahead and n == 2:
                        final_squares(0)

            def final_squares(n):
                for t in range(2):
                    m = 2 * n + t
                    sc.wait_ge(fin_h, m + 1)
                    if m >= 4:
                        sc.wait_ge(fin_sq, m - 3)
                    nc.scalar.activation(nreg[:, 512 * (m % 4):512 * (m % 4) + 512], xres[:, t, 512 * n:512 * n + 512],
                                         ACT.Square, accum_out=finsum[:, t, n:n + 1]).then_inc(fin_sq, 1)

            passes = sc.alloc_register("act_passes")
            sc.reg_mov(passes, 0)
            sc.wait_ge(rank_ready, 1)
            tokens_out(0, 0)
            tokens_out(0, 2)

            def extra_passes(i):
                extra = sc.value_load(more[0:1, bass.ds(i, 1)], min_val=0, max_val=PASSES - 1)
                with sc.If(extra > 0):
                    with sc.Fori(0, extra):
                        pair_pass(sc.snap(passes, min_val=0, max_val=64))
                        sc.reg_add(passes, passes, 1)

            with sc.Fori(0, NE // 2 - 1) as i:
                extra_passes(i)
                pair_pass(sc.snap(passes, min_val=0, max_val=64))
                sc.reg_add(passes, passes, 1)
            extra_passes(NE // 2 - 1)
            pair_pass(sc.snap(passes, min_val=0, max_val=64), ahead=False)

            for n in range(1, 4):
                final_squares(n)
            sc.wait_ge(root, 3)
            for n in range(4):
                sc.wait_ge(fin_gain, n + 1)
                nc.scalar.activation(xres[:, 1, 512 * n:512 * n + 512], yacc[:, 1, 512 * n:512 * n + 512], ACT.Identity,
                                     scale=stat[:, 15:16]).then_inc(fin_act, 1)

        @block.vector
        def _(ve):
            V = nc.vector
            steps = [0]

            def link(ins):
                steps[0] += 1
                ins.then_inc(v_step, 1)
                ve.wait_ge(v_step, steps[0])

            roots = [0]
            wide = [0]

            def mean_square_wide(o, i_, n):
                V.tensor_scalar(o, i_, 1.0 / n, EPS, ALU.mult, ALU.add).then_inc(mean_wide, 1)
                wide[0] += 1

            def root_inverse_wide(o):
                ve.wait_ge(root_wide, wide[0])
                link(V.reciprocal(o, o))

            def rsqrt_wide(o, i_, n):
                mean_square_wide(o, i_, n)
                root_inverse_wide(o)

            def rsqrt(o, i_, n):
                V.tensor_scalar(o, i_, 1.0 / n, EPS, ALU.mult, ALU.add).then_inc(mean_sq, 1)
                roots[0] += 1
                ve.wait_ge(root, roots[0])

            ve.wait_ge(zeroed, 2)
            ve.wait_ge(small_T, 1)
            for v in range(2):
                V.tensor_copy(csT[:, :, v:v + 1], ps[:, 7, 16 * v:16 * v + 16].rearrange("p (c a) -> p c a", a=1))
            V.tensor_copy(vecT[:, :], ps[:, 7, 64:64 + NVEC])
            V.tensor_copy(bT[:, :], ps[:, 7, 256:352]).then_inc(small_done, 1)
            ve.wait_ge(small_done, 1)

            ve.wait_ge(squares, 4)
            rsqrt(tiny[:, 8:12], stat[:, 0:4], D)
            for t in range(2):
                V.tensor_scalar(xs[:, t, :], xres[:, t, :], tiny[:, 8 + t:9 + t], None, ALU.mult).then_inc(xs_ready, 1)
            for t in range(2):
                V.tensor_scalar(ctxs[:, t, :], ctxs[:, t, :], tiny[:, 10 + t:11 + t], None, ALU.mult).then_inc(xs_ready, 1)

            def cols_out(n):
                ve.wait_ge(mod_cols, n + 1)
                V.tensor_reduce(modT[:, bass.ds(4 * n, 4), :],
                                ps[:, 5, :].rearrange("p (c q r) -> p c r q", c=4, q=4)[:, :, 0:2, :], AX.X, ALU.add)\
                    .then_inc(modT_done, 1)

            with ve.Fori(0, 4) as i:
                cols_out(2 * i)
                cols_out(2 * i + 1)
            ve.wait_ge(modT_done, 8)
            link(V.tensor_tensor(modT[:, 0:32, :], modT[:, 0:32, :], bT[:, 0:32].unsqueeze(2).to_broadcast([P, 32, 2]),
                                 ALU.add))
            V.scalar_tensor_tensor(out=amul[:, :, :], in0=modT[:, 16:32, :], scalar=1.0,
                                   in1=vecT[:, V_AN:V_AN + KC].unsqueeze(2).to_broadcast([P, KC, 2]),
                                   op0=ALU.add, op1=ALU.mult).then_inc(amul_ready, 1)
            ve.wait_ge(amul_ready, 1)
            for k in range(KC):
                ve.wait_ge(xT_full, k + 1)
                V.tensor_scalar(nT[:, k, 0:T], ps[:, 2 * (k % 2), 0:T], amul[:, k, 0:1], modT[:, k, 0:1], ALU.mult, ALU.add)\
                    .then_inc(nT_lat, 1)

            for m in range(4):
                ve.wait_ge(q_sq, m + 1)
                V.tensor_scalar(qaT[:, m, :], ps[:, m, 0:T], vecT[:, V_QN + m:V_QN + m + 1], None, ALU.mult)\
                    .then_inc(q_out, 1)
            for m in range(2):
                ve.wait_ge(kv_sq, m + 1)
                V.tensor_scalar(kvT[:, m, :], ps[:, 6 - m, :], vecT[:, V_KN + m:V_KN + m + 1], None, ALU.mult)\
                    .then_inc(kv_out, 1)
            ve.wait_ge(stat_q, 1)
            rsqrt_wide(rowq, ps[:, 0, 0:T], QL)
            ve.wait_ge(stat_kv, 1)
            rsqrt_wide(rowkv, ps[:, 1, :], KVL)
            ve.wait_ge(kr_mm, 1)
            V.tensor_copy(krT[:, T:2 * T], ps[:, 2, T:2 * T])
            link(V.tensor_tensor(krT[:, 0:T], ps[:, 2, 0:T], cosT, ALU.mult))
            link(V.tensor_tensor(krs[:, 0:T], ps[:, 3, 0:T], sinT, ALU.mult))
            V.tensor_tensor(krT[:, 0:T], krT[:, 0:T], krs[:, 0:T], ALU.add).then_inc(kr_done, 1)
            ve.wait_ge(q_out, 4)
            ve.wait_ge(kv_out, 2)
            for m in range(4):
                ins = V.tensor_tensor(qaT[:, m, :], qaT[:, m, :], rowq, ALU.mult)
            ins.then_inc(q_ready, 1)
            for m in range(2):
                ins = V.tensor_tensor(kvT[:, m, :], kvT[:, m, :], rowkv, ALU.mult)
            ins.then_inc(kv_ready, 1)

            base, LINKS = steps[0], 3
            with ve.Fori(0, 4) as i:
                def tap(j, m):
                    return vecT[:, bass.ds(V_CW + 8 * j + m + 2 * i, 1)]

                for m in range(2):
                    ve.wait_ge(conv_full, 6 * i + 3 + m)
                    ve.wait_ge(gc_out, 2 * i + m + 1)
                    V.tensor_tensor(upad[:, m, 1:T + 1], ps[:, 2 + m, 0:T], gcs[:, m, :], ALU.mult).then_inc(u_out, 1)
                ve.wait_ge(u_out, 2 * i + 2)
                for m in range(2):
                    ins = V.tensor_scalar(ycv[:, m, :], upad[:, m, 1:T + 1], tap(1, m), None, ALU.mult)
                ins.then_inc(v_step, 1)
                ve.wait_ge(v_step, 3 * i + base + 1)
                for j in (0, 2):
                    for m in range(2):
                        ins = V.scalar_tensor_tensor(out=ycv[:, m, :], in0=upad[:, m, j:j + T], scalar=tap(j, m),
                                                     in1=ycv[:, m, :], op0=ALU.mult, op1=ALU.add)
                    ins.then_inc(v_step, 1)
                    ve.wait_ge(v_step, 3 * i + base + 2 + j // 2)
                for m in range(2):
                    ve.wait_ge(conv_full, 6 * i + 5 + m)
                    V.tensor_tensor(oT[:, bass.ds(8 + m + 2 * i, 1), :].rearrange("p a t -> p (a t)"), ps[:, m, 0:T],
                                    ycv[:, m, :], ALU.mult).then_inc(y_out, 1)
                for u in range(2):
                    cols_out(2 * i + u + 8)
            steps[0] += 4 * LINKS

            ve.wait_ge(modT_done, 16)
            V.tensor_tensor(modT[:, 32:64, :], modT[:, 32:64, :], bT[:, 32:64].unsqueeze(2).to_broadcast([P, 32, 2]),
                            ALU.add).then_inc(mods_ready, 1)

            def gate_out(m):
                ve.wait_ge(diag_used, m + 1)
                V.tensor_copy(gaB[:, 512 * m:512 * m + 512], ps[:, 6 + m % 2, :]).then_inc(gate_done, 1)

            def rope(p):
                ve.wait_ge(rot_full, p + 1)
                ve.wait_ge(proj_act, 3 * (p // 2) + p % 2 + 1)
                link(V.tensor_tensor(ycv[:, p % 2, :], ps[:, 6 + p % 2, 0:T], sinT, ALU.mult))
                link(V.tensor_tensor(qrT[:, p, :], qraw[:, p % 2, :], cosT, ALU.mult))
                V.tensor_tensor(qrT[:, p, :], qrT[:, p, :], ycv[:, p % 2, :], ALU.add).then_inc(qr_ready, 1)

            for j in range(1, 28, 2):
                ve.wait_ge(proj_full, j + 1)
                bank = ps[:, j % 4, :]
                if j < 12:
                    s, n = j // 6, j % 6
                    dst, src = qnT[:, 4 * s + {1: 0, 3: 1, 5: 3}[n], :], bank[:, 0:T]
                elif j < 20:
                    dst, src = knT[:, j - 12, :], bank
                else:
                    dst, src = vtok[:, (j - 20) // 2, 512:1024], bank
                V.tensor_copy(dst, src).then_inc(proj_dve, 1)
                if j in (5, 7, 11, 13):
                    rope({5: 0, 7: 1, 11: 2, 13: 3}[j])
                if j == 25:
                    ve.wait_ge(csq_used, 8)
                    mean_square_wide(rconv, ps[:, 5, 0:T], CW)
                if j >= 21:
                    gate_out((j - 21) // 2)

            root_inverse_wide(rconv)
            for k in range(8):
                V.scalar_tensor_tensor(out=oT[:, 8 + k, :], in0=oT[:, 8 + k, :], scalar=vecT[:, V_OC + k:V_OC + k + 1],
                                       in1=rconv, op0=ALU.mult, op1=ALU.mult).then_inc(oc_ready, 1)
            def maximum(n):
                ve.wait_ge(score_full, n + 1)
                b = n % 3
                link(V.tensor_reduce(rowmax[:, b:b + 1], ps[:, SCORE_BANK[b], :], AX.X, ALU.max))
                V.tensor_scalar(negmax[:, b:b + 1], rowmax[:, b:b + 1], -SCALE, None, ALU.mult).then_inc(neg_max, 1)

            def head_out(h):
                ve.wait_ge(o_full, h + 1)
                V.tensor_copy(oT[:, h, :], ps[:, 4, 0:T]).then_inc(o_out, 1)

            maximum(0)
            maximum(1)
            cols_out(ATT_GROUP)
            for n in range(2 * HEADS):
                b = n % 3
                ve.wait_ge(exp_done, n + 1)
                if n >= 3:
                    ve.wait_ge(p_ready, n - 2)
                link(V.reciprocal(inverse[:, b:b + 1], rowsum[:, b:b + 1]))
                V.tensor_scalar(prob[b], prob[b], inverse[:, b:b + 1], None, ALU.mult).then_inc(p_ready, 1)
                if n + 2 < 2 * HEADS:
                    maximum(n + 2)
                if n % 2 and n > 1:
                    head_out(n // 2 - 1)
                if group_at(n, 3):
                    cols_out(group_at(n, 3))
            head_out(HEADS - 1)

            ve.wait_ge(msq_used, 8)
            rsqrt_wide(rmla, ps[:, 7, 0:T], HEADS * VD)
            for k in range(8):
                V.scalar_tensor_tensor(out=oT[:, k, :], in0=oT[:, k, :], scalar=vecT[:, V_OM + k:V_OM + k + 1],
                                       in1=rmla, op0=ALU.mult, op1=ALU.mult).then_inc(om_ready, 1)

            ve.wait_ge(gate_done, 4)
            for n in range(4):
                ve.wait_ge(wo_full, n + 1)
                for t in range(2):
                    tmp = nreg[:, 512 * t:512 * t + 512]
                    link(V.tensor_tensor(tmp, ps[:, 2 * (n % 2) + t, :], gaB[:, 512 * n:512 * n + 512], ALU.mult))
                    V.tensor_tensor(xres[:, t, 512 * n:512 * n + 512], xres[:, t, 512 * n:512 * n + 512], tmp, ALU.add)\
                        .then_inc(h_part, 1)
                cols_out(OUT_GROUP + n)

            ve.wait_ge(hsq, 8)
            link(V.tensor_reduce(stat[:, 8:10], hsum, AX.X, ALU.add))
            V.tensor_scalar(stat[:, 10:12], stat[:, 8:10], 1.0 / D, EPS, ALU.mult, ALU.add).then_inc(mean_sq, 1)
            ve.wait_ge(modT_done, 24)
            link(V.tensor_tensor(modT[:, 64:96, :], modT[:, 64:96, :], bT[:, 64:96].unsqueeze(2).to_broadcast([P, 32, 2]),
                                 ALU.add))
            V.scalar_tensor_tensor(out=amul2[:, :].rearrange("p (c a) -> p c a", a=1), in0=modT[:, 64:80, 0:1], scalar=1.0,
                                   in1=vecT[:, V_FN:V_FN + KC].rearrange("p (c a) -> p c a", a=1),
                                   op0=ALU.add, op1=ALU.mult).then_inc(mods_ready, 1)
            roots[0] += 1
            ve.wait_ge(root, roots[0])
            ve.wait_ge(mods_ready, 2)
            for n in range(4):
                V.tensor_scalar(xh[:, 0, 512 * n:512 * n + 512], xres[:, 0, 512 * n:512 * n + 512], stat[:, 10:11], None,
                                ALU.mult).then_inc(xh_ready, 1)
            for b in range(1, 8, 2):
                ve.wait_ge(hT_full, b + 1)
                for k in (2 * b, 2 * b + 1):
                    ins = V.tensor_scalar(hT[:, k, :], ps[:, b % 4, T * (k % 2):T * (k % 2) + T], amul2[:, k:k + 1],
                                          modT[:, 3 * KC + k, 0:1], ALU.mult, ALU.add)
                ins.then_inc(hT_dve, 1)

            ve.wait_ge(rt_sig, 1)
            link(V.tensor_tensor(sel[:, :, :], sig[:, :, :], rb[:, :].unsqueeze(1).to_broadcast([P, 2, NE]), ALU.add))
            for t in range(2):
                for g in range(NG):
                    ins = V.max(top8[:, 4 * t + g, :], sel[:, t, 8 * g:8 * g + 8])
            link(ins)
            gs = tiny[:, 32:40].rearrange("p (t g) -> p t g", t=2)
            link(V.tensor_tensor(gs.unsqueeze(3), top8[:, 0:8, 0:1].rearrange("p (t g) a -> p t g a", t=2),
                                 top8[:, 0:8, 1:2].rearrange("p (t g) a -> p t g a", t=2), ALU.add))
            above = tiny[:, 40:72].rearrange("p (t g a) -> p t g a", t=2, g=NG)
            same = tiny[:, 72:104].rearrange("p (t g a) -> p t g a", t=2, g=NG)
            other = gs.unsqueeze(2).to_broadcast([P, 2, NG, NG])
            own = gs.unsqueeze(3).to_broadcast([P, 2, NG, NG])
            V.tensor_tensor(above, other, own, ALU.is_gt)
            link(V.tensor_tensor(same, other, own, ALU.is_equal))
            link(V.tensor_tensor(same, same, low.unsqueeze(1).to_broadcast([P, 2, NG, NG]), ALU.mult))
            link(V.tensor_tensor(above, above, same, ALU.add))
            link(V.tensor_reduce(tiny[:, 104:112].rearrange("p (t g) -> p t g", t=2), above, AX.X, ALU.add))
            link(V.tensor_scalar(tiny[:, 112:120], tiny[:, 104:112], 1.5, -BIG, ALU.is_gt, ALU.mult))
            gm = tiny[:, 104:112]
            link(V.tensor_scalar(gm, tiny[:, 104:112], 1.5, None, ALU.is_lt))
            link(V.tensor_tensor(sel[:, :, :].rearrange("p t (g e) -> p t g e", g=NG),
                                 sel[:, :, :].rearrange("p t (g e) -> p t g e", g=NG),
                                 gm.rearrange("p (t g) -> p t g", t=2).unsqueeze(3).to_broadcast([P, 2, NG, 8]), ALU.mult))
            link(V.tensor_tensor(sel[:, :, :].rearrange("p t (g e) -> p t g e", g=NG),
                                 sel[:, :, :].rearrange("p t (g e) -> p t g e", g=NG),
                                 tiny[:, 112:120].rearrange("p (t g) -> p t g", t=2).unsqueeze(3)
                                 .to_broadcast([P, 2, NG, 8]), ALU.add))
            for t in range(2):
                ins = V.max(top8[:, 8 + t, :], sel[:, t, :])
            link(ins)
            for t in range(2):
                last_ = top8[:, 8 + t, TOP_K - 1:TOP_K]
                V.tensor_scalar(mask[:, t, :], sel[:, t, :], last_, None, ALU.is_gt)
                ins = V.tensor_scalar(scan[:, 0, t, :], sel[:, t, :], last_, None, ALU.is_equal)
            link(ins)
            V.tensor_copy(sel[:, :, :], scan[:, 0, :, :])
            link(V.tensor_reduce(tiny[:, 120:122], mask[:, :, :], AX.X, ALU.add))
            for n, d in enumerate((1, 2, 4, 8, 16)):
                a, b = scan[:, n % 2, :, :], scan[:, (n + 1) % 2, :, :]
                V.tensor_copy(b[:, :, 0:d], a[:, :, 0:d])
                link(V.tensor_tensor(b[:, :, d:NE], a[:, :, d:NE], a[:, :, 0:NE - d], ALU.add))
            link(V.tensor_tensor(scan[:, 1, :, :], scan[:, 1, :, :], tiny[:, 120:122].unsqueeze(2).to_broadcast([P, 2, NE]),
                                 ALU.add))
            link(V.tensor_scalar(scan[:, 1, :, :], scan[:, 1, :, :], TOP_K + 0.5, None, ALU.is_lt))
            link(V.tensor_tensor(sel[:, :, :], sel[:, :, :], scan[:, 1, :, :], ALU.mult))
            V.tensor_tensor(mask[:, :, :], mask[:, :, :], sel[:, :, :], ALU.add).then_inc(mask_ready, 1)
            ve.wait_ge(mask_ready, 1)
            link(V.tensor_tensor(comb[:, :, :], sig[:, :, :], mask[:, :, :], ALU.mult))
            link(V.tensor_reduce(tiny[:, 124:126], comb[:, :, :], AX.X, ALU.add))
            link(V.reciprocal(tiny[:, 126:128], tiny[:, 124:126]))
            for t in range(2):
                ins = V.tensor_scalar(comb[:, t, :], comb[:, t, :], tiny[:, 126 + t:127 + t], ROUTED_SCALE, ALU.mult, ALU.mult)
            link(ins)
            def shared_act(u):
                for m in range(2):
                    n = 2 * u + m
                    ve.wait_ge(sh_up, n + 1)
                    ve.wait_ge(sh_silu, n + 1)
                    if u:
                        ve.wait_ge(sh_down, 8)
                    V.tensor_tensor(shT[:, m, :], ps[:, 2 + m, 0:T], shS[:, m, :], ALU.mult).then_inc(sh_act, 1)

            def shared_out(u):
                for j in range(8):
                    t, m = j // 4, j % 4
                    ve.wait_ge(sh_down, 8 * u + j + 1)
                    y = yacc[:, t, 512 * m:512 * m + 512]
                    if u == 0:
                        V.tensor_copy(y, ps[:, 4 + m, :]).then_inc(y_add, 1)
                    else:
                        ve.wait_ge(y_add, j + 1)
                        V.tensor_tensor(y, y, ps[:, 4 + m, :], ALU.add).then_inc(y_add, 1)

            shared_act(0)
            shared_out(0)

            for t in range(2):
                ve.wait_ge(split_act, t + 1)
                link(V.tensor_tensor(xh[:, t, :], xh[:, t, :], parts[0][:, t, :], ALU.subtract))
                link(V.tensor_copy(parts[1][:, t, :], xh[:, t, :]))
                V.tensor_tensor(parts[2][:, t, :], xh[:, t, :], parts[1][:, t, :], ALU.subtract).then_inc(split_ready, 1)

            ve.wait_ge(rank_full, 1)
            cnt = scan[:, 0, 0, :]
            V.tensor_copy(cnt, ps[:, 5, 64:96])
            link(V.scalar_tensor_tensor(out=rank[:, 0, :, :], in0=ps[:, 5, 0:64].rearrange("p (t e) -> p t e", t=2),
                                        scalar=1.0, in1=mask[:, :, :], op0=ALU.add, op1=ALU.mult))
            link(V.tensor_scalar(rank[:, 0, :, :], rank[:, 0, :, :], -1.0, None, ALU.add))
            for n in range(1, PASSES):
                V.tensor_scalar(rank[:, n, :, :], rank[:, 0, :, :], -float(SLOTS * n), None, ALU.add)
            pairs = cnt.rearrange("p (i u) -> p i u", u=2)
            big = scan[:, 0, 1, 0:16]
            link(V.tensor_tensor(big.unsqueeze(2), pairs[:, :, 0:1], pairs[:, :, 1:2], ALU.max))
            acc, one = scan[:, 1, 0, 0:16], scan[:, 1, 1, 0:16]
            link(V.tensor_scalar(acc, big, SLOTS + 0.5, None, ALU.is_gt))
            for n in range(2, PASSES):
                link(V.tensor_scalar(one, big, SLOTS * n + 0.5, None, ALU.is_gt))
                link(V.tensor_tensor(acc, acc, one, ALU.add))
            V.tensor_copy(more[:, :], acc).then_inc(rank_ready, 1)

            slots = rank[:, :, :, :].rearrange("p n t e -> p (n t e)")
            weights = comb[:, :, :].rearrange("p t e -> p (t e)")

            def picks(i, n):
                for j in range(2):
                    for u in range(2):
                        ins = V.tensor_scalar(pick[:, j, 64 * u:64 * u + 64], iota,
                                              slots[:, bass.ds(n * (2 * NE) + j * NE + 2 * i + u, 1)], None, ALU.is_equal)
                ins.then_inc(pick_ready, 1)

            def weighted_picks(i, n):
                for j in range(2):
                    for u in range(2):
                        ins = V.tensor_scalar(pickw[:, j, 64 * u:64 * u + 64], iota,
                                              slots[:, bass.ds(n * (2 * NE) + j * NE + 2 * i + u, 1)],
                                              weights[:, bass.ds(j * NE + 2 * i + u, 1)], ALU.is_equal, ALU.mult)
                ins.then_inc(pickw_ready, 1)

            def tokens_out(t, b):
                ve.wait_ge(gx_full, 4 * t + (b + 1))
                for j in range(4):
                    k = 4 * b + j
                    ins = V.tensor_scalar(xg[:, k, :], ps[:, b % 2, 128 * j:128 * j + 128], amul2[:, k:k + 1],
                                          modT[:, 3 * KC + k, 0:1], ALU.mult, ALU.add)
                ins.then_inc(gx_dve, 1)

            def pair_pass(t, ahead):
                if ahead:
                    picks(*ahead)
                    ve.wait_ge(pickT_full, t + 1)
                    weighted_picks(*ahead)
                ve.wait_ge(silu_done, t + 1)
                V.tensor_tensor(act[:, 1, :], ps[:, 2, FF:2 * FF], act[:, 0, :], ALU.mult).then_inc(act_ready, 1)
                if ahead:
                    tokens_out(t + 1, 1)
                    tokens_out(t + 1, 3)
                for q in range(4):
                    cols = slice(512 * q, 512 * q + 512)
                    ve.wait_ge(sc_full, 4 * t + (q + 1))
                    for h in range(2):
                        V.tensor_tensor(yacc[:, h, cols], yacc[:, h, cols], ps[:, 6 + h, :], ALU.add).then_inc(y_add, 1)
                    if not ahead:
                        ve.wait_ge(y_add, 8 * t + (2 * q + 18))
                        for h in range(2):
                            ins = V.tensor_tensor(yacc[:, h, cols], yacc[:, h, cols], gfB[:, cols], ALU.mult)
                        link(ins)
                        for h in range(2):
                            V.tensor_tensor(xres[:, h, cols], xres[:, h, cols], yacc[:, h, cols], ALU.add)\
                                .then_inc(fin_h, 1)
                ve.wait_ge(y_add, 8 * t + 24)

            passes = ve.alloc_register("dve_passes")
            ve.reg_mov(passes, 0)
            left = ve.alloc_register("dve_left")
            ve.wait_ge(rank_ready, 1)

            def extra_of(i):
                return ve.value_load(more[0:1, bass.ds(i, 1)], min_val=0, max_val=PASSES - 1)

            first = extra_of(0)
            picks(0, first)
            weighted_picks(0, first)
            shared_act(1)
            tokens_out(0, 1)
            shared_out(1)
            tokens_out(0, 3)
            ve.wait_ge(y_add, 16)

            def extra_passes(i):
                extra = extra_of(i)
                with ve.If(extra > 0):
                    ve.reg_mov(left, extra)
                    with ve.Fori(0, extra):
                        ve.reg_add(left, left, -1)
                        pair_pass(ve.snap(passes, min_val=0, max_val=64), (i, ve.snap(left, min_val=0, max_val=PASSES - 2)))
                        ve.reg_add(passes, passes, 1)

            with ve.Fori(0, NE // 2 - 1) as i:
                extra_passes(i)
                pair_pass(ve.snap(passes, min_val=0, max_val=64), (i + 1, extra_of(i + 1)))
                ve.reg_add(passes, passes, 1)
            extra_passes(NE // 2 - 1)
            ve.wait_ge(gate_done, 8)
            pair_pass(ve.snap(passes, min_val=0, max_val=64), None)

            ve.wait_ge(fin_sq, 8)
            link(V.tensor_reduce(stat[:, 12:14], finsum, AX.X, ALU.add))
            rsqrt(stat[:, 14:16], stat[:, 12:14], D)
            ve.wait_ge(gain_in, 16)
            for n in range(4):
                cols = slice(512 * n, 512 * n + 512)
                V.scalar_tensor_tensor(out=xres[:, 0, cols], in0=xres[:, 0, cols], scalar=stat[:, 14:15],
                                       in1=gainB[:, cols], op0=ALU.mult, op1=ALU.mult).then_inc(fin_dve, 1)


_INS = ["x", "c", "ctx", "c_ctx", "w_mod", "b_mod", "attn_norm", "w_in", "q_a_norm", "w_q_b", "kv_a_norm", "w_kv_b",
        "conv_w", "o_norm_mla", "o_norm_conv", "w_out", "ffn_norm", "w_router", "router_bias",
        "w_exp_gate", "w_exp_up", "w_exp_down", "w_sh_gate", "w_sh_up", "w_sh_down", "final_norm"]


def kernel(**inputs):
    import concourse.bacc as _bacc
    from concourse.bass_utils import run_bass_kernel_spmd as _run

    nc = _bacc.Bacc("TRN2", target_bir_lowering=False, num_devices=1)
    arrays = {f"in_{name}": np.ascontiguousarray(inputs[name]) for name in _INS}
    arrays["in_consts"] = constants()
    args = [nc.dram_tensor(name, a.shape, F32, kind="ExternalInput").ap() for name, a in arrays.items()]
    args.append(nc.dram_tensor("out", (1, T, D), F32, kind="ExternalOutput").ap())
    block_kernel(nc, *args)
    r = _run(nc, [arrays], core_ids=[0])
    return r.results[0]["out"]
```

```python
from contextlib import ExitStack

import numpy as np

import concourse.bass as bass
from concourse import mybir
from concourse.alu_op_type import AluOpType as ALU

ACT = mybir.ActivationFunctionType
AX = mybir.AxisListType
F32 = mybir.dt.float32
BF16 = mybir.dt.bfloat16
I32 = mybir.dt.int32

P = 128
D = 2048
T = 256
KC = D // P
HEADS, NOPE, ROPE, VD = 8, 128, 64, 128
QL, KVL = 512, 256
CW = D - HEADS * VD
KR0 = QL + KVL
CONV0 = KR0 + ROPE
NE, NG, FF = 32, 4, 256
EPS = 1e-6
SCALE = float(NOPE + ROPE) ** -0.5
GRID_W = 64
ROUTED_SCALE = 2.5
TOP_K = 4
SLOTS = 64
PASSES = T // SLOTS
BIG = 1e30

C_ID, C_ONE, C_ROTQ, C_DUP, C_ROTK = 0, 128, 256, 384, 512
C_COS, C_SIN, C_SUM4, C_TRI, C_IOTA, C_LOW, C_HALF = 640, 896, 1152, 1184, 1312, 1376, 1392
NCONST = 1393

V_AN, V_QN, V_KN, V_CW, V_OM, V_OC, V_FN = 0, 16, 20, 22, 46, 54, 62
NVEC = 78


def constants():
    c = np.zeros((P, NCONST), np.float32)
    c[:, C_ID:C_ID + P] = np.eye(P)
    c[:, C_ONE:C_ONE + P] = 1.0
    for j in range(P):
        w = j % 32
        source, sign = (j + 16, -1.0) if w < 16 else (j - 16, 1.0)
        c[source, C_ROTQ + j] = sign
        for half in range(2):
            c[64 * half + j % 64, C_DUP + j] = 1.0
            c[64 * half + source % 64, C_ROTK + j] = sign
    inv = (np.float32(10000.0) ** (-np.arange(16, dtype=np.float32) / np.float32(16))).astype(np.float32)
    token = np.arange(T)
    for j in range(P):
        place = (token // GRID_W if j % 64 < 32 else token % GRID_W).astype(np.float32)
        angle = (place * inv[j % 16]).astype(np.float32)
        c[j, C_COS:C_COS + T] = np.cos(angle)
        c[j, C_SIN:C_SIN + T] = np.sin(angle)
    for q in range(4):
        for e in range(32):
            c[32 * q + e, C_SUM4 + e] = 1.0
    c[:, C_TRI:C_TRI + P] = np.triu(np.ones((P, P)), 1)
    c[:, C_IOTA:C_IOTA + SLOTS] = np.arange(SLOTS)
    c[:, C_LOW:C_LOW + NG * NG] = np.tril(np.ones((NG, NG)), -1).ravel()
    c[:, C_HALF] = -0.5
    return c


def block_kernel(nc, x, c, ctx_in, c_ctx, w_mod, b_mod, attn_norm, w_in, q_a_norm, w_q_b, kv_a_norm, w_kv_b,
                 conv_w, o_norm_mla, o_norm_conv, w_out, ffn_norm, w_router, router_bias,
                 w_exp_gate, w_exp_up, w_exp_down, w_sh_gate, w_sh_up, w_sh_down, final_norm, consts, out):
    with ExitStack() as stack:
        def sb(name, shape, dt=F32):
            return stack.enter_context(nc.sbuf_tensor(name, shape, dt))

        def sem(name):
            return stack.enter_context(nc.semaphore(name))

        xres = sb("xres", [P, 2, D])
        ring = sb("ring", [P, 6 * 4096])
        nreg = sb("nreg", [P, 8192])
        qkv = sb("qkv", [P, 2048])
        krT = sb("krT", [P, 2 * T])
        krs = sb("krs", [P, 2 * T])
        qnT = sb("qnT", [P, HEADS, T])
        part = sb("part", [P, 2, 512])
        modT = sb("modT", [P, 96, 2])
        csT = sb("csT", [P, KC, 32])
        cst = sb("cst", [P, NCONST])
        kq = sb("kq", [P, 2048])
        conv = sb("conv", [P, 1540])
        hb = sb("hb", [P, 2, D], BF16)
        vrow = sb("vrow", [P, P])
        brow = sb("brow", [P, P])
        crow = sb("crow", [32, P])
        csil = sb("csil", [32, P])
        vecT = sb("vecT", [P, NVEC])
        bT = sb("bT", [P, 96])
        amul = sb("amul", [P, KC, 2])
        amul2 = sb("amul2", [P, KC])
        stat = sb("stat", [P, 16])
        wr = sb("wr", [P, KC, NE])
        rb = sb("rb", [P, NE])
        sig = sb("sig", [P, 2, NE])
        sel = sb("sel", [P, 2, NE])
        mask = sb("mask", [P, 2, NE])
        scan = sb("scan", [P, 2, 2, NE])
        comb = sb("comb", [P, 2, NE])
        rank = sb("rank", [P, PASSES, 2, NE])
        top8 = sb("top8", [P, 10, 8])
        tiny = sb("tiny", [P, 160])
        more = sb("more", [P, NE // 2], I32)
        pick = sb("pick", [P, 2, 2 * SLOTS], BF16)

        slot = [ring[:, 4096 * s:4096 * (s + 1)] for s in range(6)]
        ctxs = slot[3].rearrange("p (t d) -> p t d", t=2)
        xs = slot[4].rearrange("p (t d) -> p t d", t=2)
        mslot = [ring[:, 3 * 4096 + 2048 * s:3 * 4096 + 2048 * (s + 1)].rearrange("p (k n) -> p k n", k=4)
                 for s in range(4)]
        aslot = [ring[:, 2048 * s:2048 * (s + 1)].rearrange("p (k n) -> p k n", k=4) for s in range(4)]
        oT = slot[5].rearrange("p (c t) -> p c t", c=KC)
        squ = slot[5][:, 0:2048]
        knT = slot[3].rearrange("p (h t) -> p h t", h=HEADS)
        vtok = slot[4].rearrange("p (k n) -> p k n", k=4)
        xh = slot[3].rearrange("p (t d) -> p t d", t=2)
        gu = ring[:, 0:16384].rearrange("p (q u g k n) -> p q u g k n", q=4, u=2, g=2, k=4)
        down = [slot[4 + u].rearrange("p (k n) -> p k n", k=2) for u in range(2)]

        wkr = kq[:, 0:1024].rearrange("p (k n) -> p k n", k=KC)
        rowq, rowkv = kq[:, 0:T], kq[:, T:3 * T]
        qrT = kq[:, 1024:2048].rearrange("p (h t) -> p h t", h=HEADS // 2)
        gcs = conv[:, 0:512].rearrange("p (m t) -> p m t", m=2)
        upad = conv[:, 512:1028].rearrange("p (m t) -> p m t", m=2)
        ycv = conv[:, 1028:1540].rearrange("p (m t) -> p m t", m=2)
        pickw = conv[:, 0:256].rearrange("p (t s) -> p t s", t=2)
        pickT = conv[:, 256:512]
        act = conv[:, 512:1024].rearrange("p (a f) -> p a f", a=2)
        actT = conv[:, 1024:1280].rearrange("p (k s) -> p k s", k=2)
        qaT = qkv[:, 0:1024].rearrange("p (c t) -> p c t", c=4)
        kvT = qkv[:, 1024:2048].rearrange("p (c t) -> p c t", c=2)
        gfB = qkv[:, :]
        nT = nreg[:, :].rearrange("p (c t) -> p c t", c=KC)
        prob = [nreg[:, 0:512], nreg[:, 512:1024], nreg[:, 7680:8192]]
        pT = nreg[:, 1024:3072].rearrange("p (b k q) -> p b k q", b=2, k=4)
        gaB = nreg[:, 3072:5120]
        sqr = nreg[:, 5120:6144].rearrange("p (b t) -> p b t", b=4)
        rconv = nreg[:, 7168:7424]
        rmla = nreg[:, 7424:7680]
        qraw = nreg[:, 7680:8192].rearrange("p (b t) -> p b t", b=2)
        hT = nreg[:, 0:4096].rearrange("p (c t) -> p c t", c=KC)
        yacc = nreg[:, 4096:8192].rearrange("p (t d) -> p t d", t=2)
        shT = krT[:, :].rearrange("p (k t) -> p k t", k=2)
        shS = krs[:, :].rearrange("p (k t) -> p k t", k=2)
        gainB = slot[0][:, 0:D]
        xg = nreg[:, 0:2048].rearrange("p (c s) -> p c s", c=KC)
        ye = nreg[:, 2048:4096]
        parts = [qnT[:, :, :].rearrange("p h t -> p (h t)").bitcast(BF16).rearrange("p (t d) -> p t d", t=2),
                 hb[:, :, :], kq[:, :].bitcast(BF16).rearrange("p (t d) -> p t d", t=2)]

        ident, ones = cst[:, C_ID:C_ID + P], cst[:, C_ONE:C_ONE + P]
        cosT, sinT = cst[:, C_COS:C_COS + T], cst[:, C_SIN:C_SIN + T]
        sum4 = cst[:, C_SUM4:C_SUM4 + 32]
        before, iota = cst[:, C_TRI:C_TRI + P], cst[:, C_IOTA:C_IOTA + SLOTS]
        low = cst[:, C_LOW:C_LOW + NG * NG].rearrange("p (a b) -> p a b", a=NG)

        ps = stack.enter_context(nc.psum_tensor("ps", [P, 8, 512], F32))

        BANKS_C, BANKS_H, BANKS_B = (1, 0), (2, 3), (4, 0)
        SCORE_BANK = (0, 1, 6)
        hsum = tiny[:, 140:148].rearrange("p (t n) -> p t n", t=2)
        finsum = tiny[:, 148:156].rearrange("p (t n) -> p t n", t=2)
        negmax, rowsum, rowmax, inverse = (tiny[:, 128:131], tiny[:, 131:134], tiny[:, 134:137], tiny[:, 137:140])

        small_in, x_in, ctx_ld, wkr_in, router_in, gain_in = (sem("small_in"), sem("x_in"), sem("ctx_ld"), sem("wkr_in"),
                                                     sem("router_in"), sem("gain_in"))
        w_full = [sem(f"w_full{s}") for s in range(6)]
        m_full = [sem(f"m_full{s}") for s in range(4)]
        m_used = [sem(f"m_used{s}") for s in range(4)]
        zeroed, silu_c, small_T, small_done = sem("zeroed"), sem("silu_c"), sem("small_T"), sem("small_done")
        mod_rows, part_full, mod_cols, modT_done = (sem("mod_rows"), sem("part_full"), sem("mod_cols"),
                                                    sem("modT_done"))
        ctxs_ready = sem("ctxs_ready")
        xT_lat, xT_ctx = sem("xT_lat"), sem("xT_ctx")
        squares, xs_ready, amul_ready, xT_full, nT_lat, nT_ctx = (sem("squares"), sem("xs_ready"), sem("amul_ready"),
                                                                  sem("xT_full"), sem("nT_lat"), sem("nT_ctx"))
        q_full, q_out, q_sq = sem("q_full"), sem("q_out"), sem("q_sq")
        kv_full, kv_out, kv_sq = sem("kv_full"), sem("kv_out"), sem("kv_sq")
        kr_full, kr_sum, kr_mm, kr_done = (sem("kr_full"), sem("kr_sum"), sem("kr_mm"),
                                                   sem("kr_done"))
        stat_q, stat_kv, q_ready, kv_ready = (sem("stat_q"), sem("stat_kv"),
                                                        sem("q_ready"), sem("kv_ready"))
        conv_full, gc_out, u_out, y_out = sem("conv_full"), sem("gc_out"), sem("u_out"), sem("y_out")
        mods_ready, acc_done, bias_in = sem("mods_ready"), sem("acc_done"), sem("bias_in")
        proj_full, proj_act, proj_dve = sem("proj_full"), sem("proj_act"), sem("proj_dve")
        rot_full, qr_ready = sem("rot_full"), sem("qr_ready")
        csq, csq_used, msq, msq_used = sem("csq"), sem("csq_used"), sem("msq"), sem("msq_used")
        oc_ready, om_ready = sem("oc_ready"), sem("om_ready")
        score_full, neg_max, exp_done, p_ready = sem("score_full"), sem("neg_max"), sem("exp_done"), sem("p_ready")
        inv_ready = sem("inv_ready")
        pT_full, pT_out, o_full, o_out = sem("pT_full"), sem("pT_out"), sem("o_full"), sem("o_out")
        wo_half, wo_full, h_part = sem("wo_half"), sem("wo_full"), sem("h_part")
        hsq, xh_ready, xh_act, hT_full, hT_act, hT_dve = (sem("hsq"), sem("xh_ready"), sem("xh_act"), sem("hT_full"), sem("hT_act"),
                                                  sem("hT_dve"))
        split_act, split_ready = sem("split_act"), sem("split_ready")
        rt_rows, rt_copied, rt_full, rt_sig, mask_ready, rank_full, rank_ready = (
            sem("rt_rows"), sem("rt_copied"), sem("rt_full"), sem("rt_sig"), sem("mask_ready"), sem("rank_full"),
            sem("rank_ready"))
        sh_gate, sh_up, sh_silu, sh_act, sh_down = (sem("sh_gate"), sem("sh_up"), sem("sh_silu"), sem("sh_act"),
                                                          sem("sh_down"))
        gu_in = [sem(f"gu_in{q}") for q in range(4)]
        gu_used = [sem(f"gu_used{q}") for q in range(4)]
        down_in = [sem(f"down_in{n}") for n in range(4)]
        down_used = [sem(f"down_used{n}") for n in range(4)]
        pick_ready, pickw_ready, gx_full, gx_act, gx_dve, pickT_full, pickT_out = (
            sem("pick_ready"), sem("pickw_ready"), sem("gx_full"), sem("gx_act"), sem("gx_dve"), sem("pickT_full"),
            sem("pickT_out"))
        gu_full, silu_done, act_ready, actT_full, actT_out, dn_full, ye_out, sc_full, y_add = (
            sem("gu_full"), sem("silu_done"), sem("act_ready"), sem("actT_full"), sem("actT_out"), sem("dn_full"),
            sem("ye_out"), sem("sc_full"), sem("y_add"))
        mean_sq, root, mean_wide, root_wide = sem("mean_sq"), sem("root"), sem("mean_wide"), sem("root_wide")
        fin_h, fin_sq, fin_gain, fin_dve, fin_act, stored = (sem("fin_h"), sem("fin_sq"), sem("fin_gain"),
                                                             sem("fin_dve"), sem("fin_act"), sem("stored"))
        v_step = sem("v_step")

        wm = w_mod[0].rearrange("(c p) n -> p c n", p=P)
        wi = w_in[0].rearrange("(c p) n -> p c n", p=P)
        wq = w_q_b[0].rearrange("(c p) n -> p c n", p=P)
        wkv = w_kv_b[0].rearrange("(c p) n -> p c n", p=P)
        wo = w_out[0].rearrange("(c p) n -> p c n", p=P)
        wg = w_exp_gate[0].rearrange("e (c p) n -> p e c n", p=P)
        wu = w_exp_up[0].rearrange("e (c p) n -> p e c n", p=P)
        wd = w_exp_down[0].rearrange("e (c p) n -> p e c n", p=P)
        sg = w_sh_gate[0].rearrange("(c p) n -> p c n", p=P)
        su = w_sh_up[0].rearrange("(c p) n -> p c n", p=P)
        sd = w_sh_down[0].rearrange("(c p) n -> p c n", p=P)

        def k_of(s, k):
            return slot[s].rearrange("p (k n) -> p k n", k=k)

        FIRST = 0
        MOD_ORDER = [g for s in range(4) for g in (s, s + 4)]
        MOD_SLOTS = [(0, 1), (2, 5)]
        SETS = 4
        W_OUT = [(n, half) for n in range(4) for half in (1, 0)]
        USES = 7
        WO_USE = [((2, 0, 1)[j % 3], USES + j // 3 + 1) for j in range(len(W_OUT))]
        ATT_GROUP, OUT_GROUP = 16, 20
        QUARTER_AT = {n: (17 + j // 4, j % 4) for j, n in enumerate((0, 2, 3, 5, 6, 8, 9, 11))}
        SUM_AT = {7: 17, 14: 18}
        OUT_SUM_AT = {1: 19, 2: 20, 3: 21, 5: 22, 7: 23}

        SH_SLOT = (0, 1, 2, 0, 4, 5)
        SH_USE = (11, 10, 11, 12, 1, 2)

        block = stack.enter_context(nc.Block())

        @block.sync
        def _(sp):
            sp.dma_start(crow[0:KC, :], c.rearrange("b (c p) -> (b c) p", p=P)).then_inc(small_in, 16)
            sp.dma_start(crow[KC:2 * KC, :], c_ctx.rearrange("(c p) -> c p", p=P)).then_inc(small_in, 16)
            sp.dma_start(cst[:, :], consts).then_inc(small_in, 16)
            for at, src in ((V_AN, attn_norm[0]), (V_QN, q_a_norm[0]), (V_KN, kv_a_norm[0]), (V_OM, o_norm_mla[0]),
                            (V_OC, o_norm_conv[0]), (V_FN, ffn_norm[0])):
                n = src.shape[0] // P
                sp.dma_start(vrow[at:at + n, :], src.rearrange("(c p) -> c p", p=P)).then_inc(small_in, 16)
            sp.dma_start(vrow[V_CW:V_CW + 24, :], conv_w[0].rearrange("k (c p) -> (k c) p", p=P)).then_inc(small_in, 16)
            sp.dma_start(brow[0:96, :], b_mod[0].rearrange("(c p) -> c p", p=P)).then_inc(small_in, 16)

            sp.dma_start(xres[:, :, :], x[0].rearrange("(t p) d -> p t d", p=P)).then_inc(x_in, 16)
            sp.dma_start(ctxs, ctx_in[0].rearrange("(t p) d -> p t d", p=P)).then_inc(ctx_ld, 16)
            for n in range(2):
                for half, s in enumerate(MOD_SLOTS[n]):
                    g = MOD_ORDER[n]
                    sp.dma_start(k_of(s, 8), wm[:, 8 * half:8 * half + 8, g * 512:g * 512 + 512]).then_inc(w_full[s], 16)

            sp.wait_ge(mod_rows, 1)
            for s in range(2):
                sp.dma_start(k_of(s, KC), wi[:, :, 256 * s:256 * s + 256]).then_inc(w_full[s], 16)
            sp.wait_ge(mod_rows, 2)
            sp.dma_start(k_of(2, KC), wi[:, :, 512:768]).then_inc(w_full[2], 16)
            sp.dma_start(wkr[:, :, :], wi[:, :, KR0:CONV0]).then_inc(wkr_in, 16)

            def load_group(n, g, slots_, freed=None):
                for q in range(4):
                    if freed:
                        freed(n, q)
                    sp.dma_start(slots_[q], wm[:, 4 * q:4 * q + 4, bass.ds(g * 512, 512)]).then_inc(m_full[q], 16)

            def freed_by_pe(n, q):
                if q == 3:
                    sp.wait_ge(mod_rows, n)
                elif n != 2:
                    sp.wait_ge(m_used[q], n - 2)

            def freed_by_dve(n, q):
                sp.wait_ge(acc_done, 16 * (n - 9) + (4 * q + 4))

            sp.wait_ge(xT_full, KC)
            for n in range(2, 8):
                load_group(n, MOD_ORDER[n], mslot, freed_by_pe)

            def load_conv(i, s, col):
                sp.dma_start(k_of(s, KC), wi[:, :, bass.ds(col + i * 256, 256)]).then_inc(w_full[s], 16)

            load_group(8, 12, mslot, freed_by_pe)
            sp.wait_ge(q_full, 2)
            load_conv(0, 0, CONV0 + CW)
            sp.wait_ge(q_full, 4)
            load_conv(0, 1, CONV0 + 2 * CW)
            sp.wait_ge(kv_full, 2)
            load_conv(0, 2, CONV0)
            load_group(9, 13, mslot, freed_by_dve)
            with sp.Fori(1, 4) as i:
                sp.wait_ge(conv_full, 6 * i - 4)
                load_conv(i, 0, CONV0 + CW)
                load_group(2 * i + 8, 2 * i + 12, mslot, freed_by_dve)
                sp.wait_ge(conv_full, 6 * i - 2)
                load_conv(i, 1, CONV0 + 2 * CW)
                sp.wait_ge(conv_full, 6 * i)
                load_conv(i, 2, CONV0)
                load_group(2 * i + 9, 2 * i + 13, mslot, freed_by_dve)

            for s in range(2):
                sp.wait_ge(conv_full, 20 + 2 * s)
                sp.dma_start(slot[s][:, 0:3072].rearrange("p (k n) -> p k n", k=4), wq[:, :, 768 * s:768 * s + 768])\
                  .then_inc(w_full[s], 16)
            sp.wait_ge(conv_full, 24)
            sp.dma_start(k_of(2, 2), wkv).then_inc(w_full[2], 16)
            sp.dma_start(wr[:, :, :], w_router[0].rearrange("(c p) n -> p c n", p=P)).then_inc(router_in, 16)
            sp.dma_start(rb[:, :], router_bias.to_broadcast([P, NE])).then_inc(router_in, 16)

            def load_out(j):
                (n, half), (s, use) = W_OUT[j], WO_USE[j]
                if j >= 3:
                    sp.wait_ge(wo_full if j % 2 == 0 else wo_half, (j - 3) // 2 + 1)
                sp.dma_start(k_of(s, 8), wo[:, 8 * half:8 * half + 8, 512 * n:512 * n + 512]).then_inc(w_full[s], 16)

            sp.wait_ge(conv_full, 24)
            sp.dma_start(gaB, b_mod[:, 2 * D:3 * D].to_broadcast([P, D])).then_inc(bias_in, 16)
            sp.wait_ge(proj_full, 12)
            load_group(16, 8, aslot)
            load_group(17, 9, aslot, freed_by_dve)
            sp.wait_ge(proj_full, 28)
            sp.dma_start(gfB, b_mod[:, 5 * D:6 * D].to_broadcast([P, D])).then_inc(bias_in, 16)
            load_out(0)
            load_group(18, 10, aslot, freed_by_dve)
            sp.wait_ge(acc_done, 16 * 11)
            load_out(1)
            load_out(2)
            sp.wait_ge(score_full, 2 * HEADS)
            sp.wait_ge(o_full, HEADS)
            load_group(19, 11, mslot)
            load_out(3)
            load_group(20, 20, mslot, freed_by_dve)
            load_out(4)
            load_group(21, 21, mslot, freed_by_dve)
            load_out(5)
            load_group(22, 22, mslot, freed_by_dve)
            load_out(6)
            load_out(7)
            load_group(23, 23, mslot, freed_by_dve)

            sp.wait_ge(wo_full, 3)
            sp.dma_start(k_of(1, KC), su[:, :, 0:FF]).then_inc(w_full[1], 16)
            sp.wait_ge(wo_half, 4)
            sp.dma_start(k_of(2, KC), sg[:, :, FF:2 * FF]).then_inc(w_full[2], 16)
            sp.wait_ge(acc_done, 16 * 16)
            sp.dma_start(k_of(4, 2), sd[:, 0:2, :]).then_inc(w_full[4], 16)
            sp.wait_ge(wo_full, 4)
            sp.dma_start(k_of(0, KC), sg[:, :, 0:FF]).then_inc(w_full[0], 16)
            sp.dma_start(k_of(5, 2), sd[:, 2:4, :]).then_inc(w_full[5], 16)
            sp.wait_ge(sh_gate, 2)
            sp.dma_start(k_of(0, KC), su[:, :, FF:2 * FF]).then_inc(w_full[0], 16)

            def load_quarter(i, q):
                for u in range(2):
                    for g, src in ((0, wg), (1, wu)):
                        sp.dma_start(gu[:, q, u, g, :, :].rearrange("p k n -> p (k n)").rearrange("p (k n) -> p k n", k=4),
                                     src[:, bass.ds(2 * i + u, 1), 4 * q:4 * q + 4, :]
                                     .rearrange("p a c n -> p (a c) n")).then_inc(gu_in[q], 16)

            def load_down(i, n, u):
                sp.dma_start(down[u][:, :, 512 * n:512 * n + 512],
                             wd[:, bass.ds(2 * i + u, 1), :, 512 * n:512 * n + 512]
                             .rearrange("p a c n -> p (a c) n")).then_inc(down_in[n], 16)

            sp.wait_ge(sh_up, 2)
            load_quarter(0, 1)
            sp.wait_ge(hT_full, 8)
            sp.wait_ge(split_ready, 2)
            load_quarter(0, 3)
            sp.wait_ge(sh_gate, 4)
            load_quarter(0, 2)
            sp.wait_ge(sh_down, 8)
            for n in range(4):
                load_down(0, n, 0)
            sp.wait_ge(sh_up, 4)
            load_quarter(0, 0)
            sp.wait_ge(sh_down, 16)
            for n in range(4):
                load_down(0, n, 1)
            with sp.Fori(1, NE // 2) as i:
                for q in range(4):
                    sp.wait_ge(gu_used[q], i)
                    load_quarter(i, q)
                for n in range(4):
                    sp.wait_ge(down_used[n], i)
                    for u in range(2):
                        load_down(i, n, u)

            sp.wait_ge(gu_used[0], NE // 2)
            sp.dma_start(gainB, final_norm.rearrange("(a d) -> a d", a=1).to_broadcast([P, D])).then_inc(gain_in, 16)

            for half in range(2):
                for t, done in ((0, fin_dve), (1, fin_act)):
                    sp.wait_ge(done, 2 * half + 2)
                    cols = slice(1024 * half, 1024 * half + 1024)
                    sp.dma_start(out[0].rearrange("(t p) d -> p t d", p=P)[:, t, cols], xres[:, t, cols])\
                      .then_inc(stored, 16)
            sp.wait_ge(stored, 64)

        @block.gpsimd
        def _(pool):
            nc.gpsimd.memset(csT[:, :, :], 0.0).then_inc(zeroed, 1)
            nc.gpsimd.memset(upad[:, :, :], 0.0).then_inc(zeroed, 1)

            roots = [0]

            def power(v):
                roots[0] += 1
                pool.wait_ge(mean_sq, roots[0])
                nc.gpsimd.tensor_tensor(v, v, cst[:, C_HALF:C_HALF + 1].to_broadcast(list(v.shape)), ALU.pow)\
                    .then_inc(root, 1)

            power(tiny[:, 8:12])

            power(stat[:, 10:12])
            pool.wait_ge(gain_in, 16)
            for n in range(4):
                pool.wait_ge(fin_h, 2 * n + 2)
                nc.gpsimd.tensor_tensor(yacc[:, 1, 512 * n:512 * n + 512], xres[:, 1, 512 * n:512 * n + 512],
                                        gainB[:, 512 * n:512 * n + 512], ALU.mult).then_inc(fin_gain, 1)
            power(stat[:, 14:16])

        @block.tensor
        def _(pe):
            def mm(o, l, r, start, stop):
                return nc.tensor.matmul(o, l, r, start=start, stop=stop)

            pe.wait_ge(silu_c, 1)
            nc.tensor.transpose(ps[:, 7, 0:32], csil[:, :], ident[0:32, 0:32])
            nc.tensor.transpose(ps[:, 7, 64:64 + NVEC], vrow[0:NVEC, :], ident[0:NVEC, 0:NVEC])
            nc.tensor.transpose(ps[:, 7, 256:352], brow[0:96, :], ident[0:96, 0:96]).then_inc(small_T, 1)
            pe.wait_ge(small_done, 1)

            def mod_cols_of(n, b, bank=5):
                pe.wait_ge(part_full, n + 1)
                if n is not FIRST:
                    pe.wait_ge(modT_done, n)
                for j in range(4):
                    ins = nc.tensor.transpose(ps[:, bank, 128 * j:128 * j + 128], part[:, b, 128 * j:128 * j + 128], ident)
                ins.then_inc(mod_cols, 1)

            def mod_sum(n):
                pe.wait_ge(acc_done, 16 * (n - 8) + 16)
                pe.wait_ge(modT_done, n)

            def mod_sum_cols(n, b):
                mod_sum(n)
                for j in range(4):
                    ins = mm(ps[:, 5, j:j + 1], part[:, b, 128 * j:128 * j + 128], ones[:, 0:1], True, True)
                ins.then_inc(mod_cols, 1)

            def mod_sum_wide(n):
                mod_sum(n)
                mm(ps[:, 5, :], ones, part[:, n % 2, :], True, True).then_inc(mod_cols, 1)

            def group_rows(n, slots_, bank):
                for k in range(KC):
                    q = k // 4
                    if k % 4 == 0:
                        pe.wait_ge(m_full[q], 16 * (n - 1))
                    ins = mm(ps[32 * (k % 4):32 * (k % 4) + 32, bank, :], csT[:, k, :], slots_[q][:, k % 4, :],
                             k < 4, k >= 12)
                    if k % 4 == 3:
                        ins.then_inc(m_used[q] if q < 3 else mod_rows, 1)

            def first_group(n):
                if n:
                    pe.wait_ge(modT_done, n)
                for k in range(KC):
                    half, q = k // 8, k % 4
                    s = MOD_SLOTS[n][half]
                    if k % 8 == 0:
                        pe.wait_ge(w_full[s], 16)
                    ins = mm(ps[32 * q:32 * q + 32, 7, :], csT[:, k, :], k_of(s, 8)[:, k % 8, :], k < 4, k >= 12)
                ins.then_inc(mod_rows, 1)
                mod_cols_of(FIRST if n == 0 else n, n, 7)

            first_group(0)

            pe.wait_ge(xs_ready, 2)
            pe.wait_ge(ctxs_ready, 2)
            for k in range(KC):
                if k >= 2:
                    pe.wait_ge(xT_lat, k - 1)
                    pe.wait_ge(xT_ctx, k - 1)
                for t in range(4):
                    src = (xs if t < 2 else ctxs)[:, t % 2, 128 * k:128 * k + 128]
                    ins = nc.tensor.transpose(ps[:, 2 * (k % 2) + t // 2, 128 * (t % 2):128 * (t % 2) + 128], src, ident)
                ins.then_inc(xT_full, 1)
            first_group(1)
            pe.wait_ge(xT_lat, KC)
            pe.wait_ge(xT_ctx, KC)

            def query_set(s, ms):
                pe.wait_ge(nT_lat, 4 * s + 4)
                for m in ms:
                    w = k_of(m // 2, KC)
                    pe.wait_ge(w_full[m // 2], 16 * 2)
                    for k in range(4 * s, 4 * s + 4):
                        ins = mm(ps[:, m, 0:T], w[:, k, 128 * (m % 2):128 * (m % 2) + 128], nT[:, k, 0:T],
                                 k == 0, k == KC - 1)
                    if s == SETS - 1:
                        ins.then_inc(q_full, 1)

            def rotary_set(s):
                pe.wait_ge(wkr_in, 16)
                for k in range(4 * s, 4 * s + 4):
                    r = 64 * (k % 2)
                    ins = mm(ps[r:r + 64, 6, :], wkr[:, k, :], nT[:, k, :], k < 2, k >= 14)
                if s == SETS - 1:
                    ins.then_inc(kr_full, 1)

            def kv_set(s, m):
                pe.wait_ge(nT_ctx, 4 * s + 4)
                pe.wait_ge(w_full[2], 16 * 2)
                w = k_of(2, KC)
                for k in range(4 * s, 4 * s + 4):
                    ins = mm(ps[:, 4 + m, :], w[:, k, 128 * m:128 * m + 128], nT[:, k, :], k == 0, k == KC - 1)
                if s == SETS - 1:
                    ins.then_inc(kv_full, 1)

            def step_group(n):
                pe.wait_ge(modT_done, n)
                group_rows(n, mslot, 7)

            for s in range(SETS - 1):
                query_set(s, range(4) if s == 0 else (0, 1))
                if s == 0:
                    kv_set(s, 0)
                step_group(2 * s + 2)
                if s:
                    kv_set(s, 0)
                mod_cols_of(2 * s + 2, 0, 7)
                rotary_set(s)
                if s:
                    query_set(s, (2, 3))
                step_group(2 * s + 3)
                mod_cols_of(2 * s + 3, 1, 7)
                kv_set(s, 1)
            query_set(SETS - 1, range(4))
            kv_set(SETS - 1, 0)
            rotary_set(SETS - 1)
            pe.wait_ge(modT_done, 8)
            pe.wait_ge(q_sq, 4)
            for m in range(4):
                ins = mm(ps[:, 7, 0:T], ones, squ[:, T * m:T * m + T], m == 0, m == 3)
            ins.then_inc(stat_q, 1)
            pe.wait_ge(q_out, 4)
            pe.wait_ge(kr_sum, 1)
            mm(ps[:, 2, :], cst[:, C_DUP:C_DUP + P], krs[:, :], True, True)
            mm(ps[:, 3, 0:T], cst[:, C_ROTK:C_ROTK + P], krs[:, 0:T], True, True).then_inc(kr_mm, 1)
            kv_set(SETS - 1, 1)
            pe.wait_ge(kv_out, 1)
            pe.wait_ge(kv_sq, 2)
            for m in range(2):
                ins = mm(ps[:, 4, :], ones, squ[:, 1024 + 512 * m:1536 + 512 * m], m == 0, m == 1)
            ins.then_inc(stat_kv, 1)

            def conv_blocks(i, s, banks, ms=(0, 1)):
                pe.wait_ge(w_full[s], 16 * i + 16 * 3)
                w = k_of(s, KC)
                for m in ms:
                    for k in range(KC):
                        ins = mm(ps[:, banks[m], 0:T], w[:, k, 128 * m:128 * m + 128], nT[:, k, 0:T],
                                 k == 0, k == KC - 1)
                    ins.then_inc(conv_full, 1)

            with pe.Fori(0, 4) as i:
                conv_blocks(i, 0, BANKS_C, (0,))
                pe.wait_ge(modT_done, 2 * i + 8)
                conv_blocks(i, 0, BANKS_C, (1,))
                pe.wait_ge(kr_done, 1)
                conv_blocks(i, 1, BANKS_H)
                pe.wait_ge(kv_out, 2)
                mod_sum_cols(2 * i + 8, 0)
                pe.wait_ge(gc_out, 2 * i + 2)
                pe.wait_ge(mean_wide, 2)
                conv_blocks(i, 2, BANKS_B)
                mod_sum_cols(2 * i + 9, 1)
            pe.wait_ge(y_out, 8)

            def project(j, width, steps):
                if j >= 4:
                    pe.wait_ge(proj_dve if j % 2 else proj_act, (j - 4) // 2 + 1)
                for n, (ls, r) in enumerate(steps):
                    for u, l in enumerate(ls):
                        rows_ = slice(P // len(ls) * u, P // len(ls) * (u + 1))
                        ins = mm(ps[rows_, j % 4, 0:width], l, r, n == 0, n == len(steps) - 1)
                ins.then_inc(proj_full, 1)

            def rotate(p):
                pe.wait_ge(proj_act, 3 * (p // 2) + p % 2 + 1)
                if p >= 2:
                    pe.wait_ge(qr_ready, p - 1)
                mm(ps[:, 6 + p % 2, 0:T], cst[:, C_ROTQ:C_ROTQ + P], qraw[:, p % 2, :], True, True).then_inc(rot_full, 1)

            pe.wait_ge(q_ready, 1)
            for s in range(2):
                w = slot[s][:, 0:3072].rearrange("p (k h n) -> p k h n", k=4, h=4)
                pe.wait_ge(w_full[s], 16 * USES)
                for n, (rope, h) in enumerate(((True, 0), (False, 0), (True, 2), (False, 1), (False, 2), (False, 3))):
                    lhs = [[w[:, k, h + u, NOPE:NOPE + ROPE] for u in range(2)] if rope else [w[:, k, h, 0:NOPE]]
                           for k in range(4)]
                    project(6 * s + n, T, [(lhs[k], qaT[:, k, :]) for k in range(4)])
                    if n == 3:
                        rotate(2 * s)
                rotate(2 * s + 1)
            def conv_square(k):
                pe.wait_ge(csq, k + 1)
                mm(ps[:, 5, 0:T], ones, sqr[:, k % 4, :], k == 0, k == 7).then_inc(csq_used, 1)

            pe.wait_ge(kv_ready, 1)
            pe.wait_ge(w_full[2], 16 * USES)
            pe.wait_ge(modT_done, 16)
            w = slot[2].rearrange("p (k h n) -> p k h n", k=2, h=HEADS)
            for h in range(HEADS):
                project(12 + h, 2 * T, [([w[:, k, h, 0:NOPE]], kvT[:, k, :]) for k in range(2)])
                if h >= 2:
                    conv_square(h - 2)
            pe.wait_ge(qr_ready, 4)
            for t in range(4):
                for n in range(2):
                    project(20 + 2 * t + n, 512, [([kvT[:, k, 128 * t:128 * t + 128]],
                                                   w[:, k, 4 * n:4 * n + 4, NOPE:NOPE + VD]) for k in range(2)])
                if t < 2:
                    conv_square(6 + t)


            pe.wait_ge(proj_act, 14)
            pe.wait_ge(proj_dve, 14)

            def scores(n):
                h, t = n // 2, n % 2
                r = 64 * (h % 2)
                if n >= 3:
                    pe.wait_ge(exp_done, n - 2)
                bank = SCORE_BANK[n % 3]
                mm(ps[:, bank, :], qnT[:, h, 128 * t:128 * t + 128], knT[:, h, :], True, False)
                mm(ps[:, bank, :], qrT[r:r + 64, h // 2, 128 * t:128 * t + 128], krT[r:r + 64, :], False, True)\
                    .then_inc(score_full, 1)

            def head_square(h):
                pe.wait_ge(msq, h + 1)
                mm(ps[:, 7, 0:T], ones, sqr[:, h % 4, :], h == 0, h == 7).then_inc(msq_used, 1)

            scores(0)
            scores(1)
            scores(2)
            pe.wait_ge(mean_wide, 3)
            mod_sum_wide(ATT_GROUP)
            for n in range(2 * HEADS):
                h = n // 2
                pe.wait_ge(p_ready, n + 1)
                if n >= 2:
                    pe.wait_ge(pT_out, n - 1)
                for k in range(4):
                    ins = nc.tensor.transpose(ps[:, 2 + n % 2, 128 * k:128 * k + 128],
                                              prob[n % 3][:, 128 * k:128 * k + 128], ident)
                ins.then_inc(pT_full, 1)
                if n + 3 < 2 * HEADS:
                    scores(n + 3)
                if n in SUM_AT:
                    mod_sum_wide(SUM_AT[n])
                if n % 2:
                    pe.wait_ge(pT_out, n + 1)
                    if h:
                        pe.wait_ge(o_out, h)
                    for k in range(4):
                        ins = mm(ps[:, 4, 0:T], vtok[:, k, 128 * h:128 * h + 128], pT[:, h % 2, k, :],
                                 k == 0, k == 3)
                    ins.then_inc(o_full, 1)
                    if h:
                        head_square(h - 1)

            pe.wait_ge(oc_ready, 8)
            for (n, half), (s, use) in zip(W_OUT, WO_USE):
                pe.wait_ge(w_full[s], 16 * use)
                if n >= 2 and half == 1:
                    pe.wait_ge(h_part, 2 * (n - 1))
                w = k_of(s, 8)
                for k in range(8):
                    if n == 0 and half == 1 and k == 3:
                        head_square(HEADS - 1)
                    if half == 0:
                        pe.wait_ge(om_ready, k + 1)
                    for t in range(2):
                        ins = mm(ps[:, 2 * (n % 2) + t, :], oT[:, 8 * half + k, 128 * t:128 * t + 128], w[:, k, :],
                                 half == 1 and k == 0, half == 0 and k == 7)
                ins.then_inc(wo_full if half == 0 else wo_half, 1)
                tile = 2 * n + 1 - half
                if tile in OUT_SUM_AT:
                    mod_sum_wide(OUT_SUM_AT[tile])

            for b in range(8):
                if b % 2 == 0:
                    pe.wait_ge(xh_ready, b // 2 + 1)
                    pe.wait_ge(xh_act, b // 2 + 1)
                if b >= 4:
                    pe.wait_ge(hT_dve if b % 2 else hT_act, (b - 4) // 2 + 1)
                for j in range(2):
                    for t in range(2):
                        k = 2 * b + j
                        ins = nc.tensor.transpose(ps[:, b % 4, 256 * j + 128 * t:256 * j + 128 * t + 128],
                                                  xh[:, t, 128 * k:128 * k + 128], ident)
                ins.then_inc(hT_full, 1)

            pe.wait_ge(router_in, 32)
            for k in range(KC):
                if k % 2 == 0:
                    pe.wait_ge(hT_dve if k % 4 else hT_act, k // 4 + 1)
                q = k % 4
                ins = mm(ps[32 * q:32 * q + 32, 4, 0:T], wr[:, k, :], hT[:, k, :], k < 4, k >= 12)
            ins.then_inc(rt_rows, 1)
            pe.wait_ge(rt_copied, 1)
            pe.wait_ge(modT_done, 24)
            for t in range(2):
                ins = mm(ps[:, 5, 32 * t:32 * t + 32], part[:, 0, 128 * t:128 * t + 128], sum4, True, True)
            ins.then_inc(rt_full, 1)
            def gather(t, banks, last=False):
                for b in banks:
                    if b == 0:
                        pe.wait_ge(pick_ready, t + 1)
                    if b >= 2:
                        pe.wait_ge((gx_act, gx_dve)[b % 2], 2 * t + 1)
                    for j in range(4):
                        k = 4 * b + j
                        for n in range(6):
                            ins = mm(ps[:, b % 2, 128 * j:128 * j + 128], parts[n % 3][:, n // 3, 128 * k:128 * k + 128],
                                     pick[:, n // 3, :], n == 0, n == 5)
                            if last and b == j == n == 0:
                                ins.then_inc(gu_used[3], 1)
                    ins.then_inc(gx_full, 1)

            for u in range(2):
                if u:
                    pe.wait_ge(sh_act, 2)
                for i, base, full in ((2 * u, 0, sh_gate), (2 * u + 1, 2, sh_up)):
                    s = SH_SLOT[i]
                    w = k_of(s, KC)
                    pe.wait_ge(w_full[s], 16 * SH_USE[i])
                    for m in range(2):
                        for k in range(KC):
                            ins = mm(ps[:, base + m, 0:T], w[:, k, 128 * m:128 * m + 128], hT[:, k, :],
                                     k == 0, k == KC - 1)
                        ins.then_inc(full, 1)
                w = k_of(4 + u, 2)
                pe.wait_ge(w_full[4 + u], 16 * SH_USE[4 + u])
                pe.wait_ge(sh_act, 2 * u + 2)
                if u == 1:
                    gather(0, (0, 1))
                    pe.wait_ge(rank_ready, 1)
                for j in range(8):
                    t, m = j // 4, j % 4
                    if 8 * u + j >= 4:
                        pe.wait_ge(y_add, 8 * u + j - 3)
                    for k in range(2):
                        ins = mm(ps[:, 4 + m, :], shT[:, k, 128 * t:128 * t + 128], w[:, k, 512 * m:512 * m + 512],
                                 k == 0, k == 1)
                    ins.then_inc(sh_down, 1)
                if u == 0:
                    pe.wait_ge(mask_ready, 1)
                    pe.wait_ge(y_add, 6)
                    mm(ps[:, 5, 0:32], before, mask[:, 0, :], True, True)
                    mm(ps[:, 5, 32:64], ones, mask[:, 0, :], True, False)
                    mm(ps[:, 5, 32:64], before, mask[:, 1, :], False, True)
                    mm(ps[:, 5, 64:96], ones, mask[:, 0, :], True, False)
                    mm(ps[:, 5, 64:96], ones, mask[:, 1, :], False, True).then_inc(rank_full, 1)
            gather(0, (2, 3))

            def pair_pass(i, t, last, ahead=True):
                pe.wait_ge(pickw_ready, t + 1)
                for j in range(2):
                    ins = nc.tensor.transpose(ps[:, 3, 128 * j:128 * j + 128], pickw[:, j, :], ident)
                ins.then_inc(pickT_full, 1)
                for q in range(4):
                    pe.wait_ge(gu_in[q], 64 * i + 64)
                    pe.wait_ge((gx_act, gx_dve)[q % 2], 2 * t + (q // 2 + 1))
                    for k in range(4):
                        for u in range(2):
                            ins = mm(ps[64 * u:64 * u + 64, 2, :], xg[:, 4 * q + k, 64 * u:64 * u + 64],
                                     gu[:, q, u, :, k, :], q == 0 and k == 0, q == 3 and k == 3)
                    if q == 3:
                        ins.then_inc(gu_full, 1)
                    elif last:
                        ins.then_inc(gu_used[q], 1)
                if ahead:
                    gather(t + 1, (0, 1), last)
                pe.wait_ge(act_ready, t + 1)
                for k in range(2):
                    ins = nc.tensor.transpose(ps[:, 3, 256 + 128 * k:384 + 128 * k], act[:, 1, 128 * k:128 * k + 128], ident)
                ins.then_inc(actT_full, 1)
                if ahead:
                    gather(t + 1, (2, 3))
                pe.wait_ge(actT_out, t + 1)

                def scatter(n):
                    pe.wait_ge(ye_out, 4 * t + (n + 1))
                    for h in range(2):
                        m = 2 * n + h
                        pe.wait_ge(y_add, 8 * t + (16 + max(m - 1, 0)))
                        ins = mm(ps[:, 6 + h, :], pickT[:, 128 * h:128 * h + 128], ye[:, 512 * n:512 * n + 512], True, True)
                        if n < 3 and h == 0 and last:
                            ins.then_inc(down_used[n + 1], 1)
                    ins.then_inc(sc_full, 1)

                for n in range(4):
                    pe.wait_ge(down_in[n], 32 * i + 32)
                    if n >= 2:
                        pe.wait_ge(ye_out, 4 * t + (n - 1))
                    for k in range(2):
                        for u in range(2):
                            ins = mm(ps[64 * u:64 * u + 64, 4 + n % 2, :], actT[:, k, 64 * u:64 * u + 64],
                                     down[u][:, k, 512 * n:512 * n + 512], k == 0, k == 1)
                            if n == 1 and k == u == 0 and last:
                                ins.then_inc(down_used[0], 1)
                    ins.then_inc(dn_full, 1)
                    if n == 0:
                        pe.wait_ge(pickT_out, t + 1)
                    else:
                        scatter(n - 1)
                scatter(3)

            passes = pe.alloc_register("pe_passes")
            pe.reg_mov(passes, 0)
            pe.wait_ge(rank_ready, 1)
            pe.wait_ge(y_add, 16)

            def extra_passes(i):
                extra = pe.value_load(more[0:1, bass.ds(i, 1)], min_val=0, max_val=PASSES - 1)
                with pe.If(extra > 0):
                    with pe.Fori(0, extra):
                        pair_pass(i, pe.snap(passes, min_val=0, max_val=64), False)
                        pe.reg_add(passes, passes, 1)

            with pe.Fori(0, NE // 2 - 1) as i:
                extra_passes(i)
                pair_pass(i, pe.snap(passes, min_val=0, max_val=64), True)
                pe.reg_add(passes, passes, 1)
            extra_passes(NE // 2 - 1)
            pair_pass(NE // 2 - 1, pe.snap(passes, min_val=0, max_val=64), True, ahead=False)

        @block.scalar
        def _(sc):
            def copy(o, i_):
                return nc.scalar.activation(o, i_, ACT.Copy)

            sc.wait_ge(small_in, 16 * 11)
            nc.scalar.activation(csil[:, :], crow[:, :], ACT.Silu).then_inc(silu_c, 1)

            sc.wait_ge(x_in, 16)
            for t in range(2):
                nc.scalar.activation(nreg[:, 2048 * t:2048 * t + 2048], xres[:, t, :], ACT.Square,
                                     accum_out=stat[:, t:t + 1]).then_inc(squares, 1)
            sc.wait_ge(ctx_ld, 16)
            for t in range(2):
                nc.scalar.activation(nreg[:, 2048 * t + 4096:2048 * t + 6144], ctxs[:, t, :], ACT.Square,
                                     accum_out=stat[:, t + 2:t + 3]).then_inc(squares, 1)

            def rows_out(n, bank, b, first):
                sc.wait_ge(mod_rows, n + 1)
                if not first:
                    sc.wait_ge(mod_cols, n - 1)
                copy(part[:, b, :], ps[:, bank, :]).then_inc(part_full, 1)

            sc.wait_ge(root, 1)
            for t in range(2):
                nc.scalar.activation(ctxs[:, t, :], ctxs[:, t, :], ACT.Identity, scale=tiny[:, 10 + t:11 + t])\
                    .then_inc(ctxs_ready, 1)
            rows_out(0, 7, 0, True)
            for k in range(KC):
                sc.wait_ge(xT_full, k + 1)
                copy(nT[:, k, T:2 * T], ps[:, 2 * (k % 2) + 1, 0:T]).then_inc(xT_ctx, 1)
            rows_out(1, 7, 1, True)
            sc.wait_ge(xT_ctx, KC)
            for s in range(SETS):
                if s:
                    rows_out(2 * s, 7, 0, False)
                    rows_out(2 * s + 1, 7, 1, False)
                sc.wait_ge(amul_ready, s + 1)
                for k in range(4 * s, 4 * s + 4):
                    nc.scalar.activation(nT[:, k, T:2 * T], nT[:, k, T:2 * T], ACT.Identity, bias=modT[:, k, 1:2],
                                         scale=amul[:, k, 1:2]).then_inc(nT_ctx, 1)

            for m in range(4):
                sc.wait_ge(q_full, m + 1)
                nc.scalar.activation(squ[:, T * m:T * m + T], ps[:, m, 0:T], ACT.Square).then_inc(q_sq, 1)
            sc.wait_ge(kr_full, 1)
            copy(krs[:, :], ps[:, 6, :]).then_inc(kr_sum, 1)

            def kv_square(m):
                sc.wait_ge(kv_full, m + 1)
                nc.scalar.activation(squ[:, 1024 + 512 * m:1536 + 512 * m], ps[:, 4 + m, :], ACT.Square).then_inc(kv_sq, 1)

            wide = [0]

            def square_root(v):
                wide[0] += 1
                sc.wait_ge(mean_wide, wide[0])
                nc.scalar.activation(v, v, ACT.Sqrt).then_inc(root_wide, 1)

            kv_square(0)
            square_root(rowq)
            kv_square(1)
            square_root(rowkv)

            with sc.Fori(0, 4) as i:
                sc.wait_ge(modT_done, 2 * i + 8)
                for m in range(2):
                    sc.wait_ge(conv_full, 6 * i + m + 1)
                    copy(gcs[:, m, :], ps[:, BANKS_C[m], 0:T]).then_inc(gc_out, 1)

            for j in range(0, 28, 2):
                sc.wait_ge(proj_full, j + 1)
                bank = ps[:, j % 4, :]
                if j < 12:
                    s, n = j // 6, j % 6
                    if n == 4:
                        dst, src = qnT[:, 4 * s + 2, :], bank[:, 0:T]
                    else:
                        p = 2 * s + n // 2
                        if p >= 2:
                            sc.wait_ge(qr_ready, p - 1)
                        dst, src = qraw[:, p % 2, :], bank[:, 0:T]
                elif j < 20:
                    dst, src = knT[:, j - 12, :], bank
                else:
                    t, n = (j - 20) // 2, j % 2
                    dst, src = vtok[:, t, 512 * n:512 * n + 512], bank
                copy(dst, src).then_inc(proj_act, 1)
                for k in {10: (0, 1), 12: (2, 3), 14: (4,), 16: (5,), 18: (6, 7)}.get(j, ()):
                    if k == 0:
                        sc.wait_ge(y_out, 8)
                    if k >= 4:
                        sc.wait_ge(csq_used, k - 3)
                    nc.scalar.activation(sqr[:, k % 4, :], oT[:, 8 + k, :], ACT.Square).then_inc(csq, 1)
                if j == 26:
                    square_root(rconv)

            def exponentials(n):
                sc.wait_ge(neg_max, n + 1)
                b = n % 3
                if n >= 3:
                    sc.wait_ge(pT_full, n - 2)
                nc.scalar.activation(prob[b], ps[:, SCORE_BANK[b], :], ACT.Exp, bias=negmax[:, b:b + 1],
                                     scale=SCALE, accum_out=rowsum[:, b:b + 1]).then_inc(exp_done, 1)

            def head_square(h):
                sc.wait_ge(o_out, h + 1)
                if h >= 4:
                    sc.wait_ge(msq_used, h - 3)
                nc.scalar.activation(sqr[:, h % 4, :], oT[:, h, :], ACT.Square).then_inc(msq, 1)

            sc.wait_ge(csq_used, 8)
            def scale(n):
                b = n % 3
                sc.wait_ge(inv_ready, n + 1)
                nc.scalar.activation(prob[b], prob[b], ACT.Identity, scale=inverse[:, b:b + 1]).then_inc(p_ready, 1)

            exponentials(0)
            exponentials(1)
            scale(0)
            for n in range(2 * HEADS):
                h = n // 2
                if n + 2 < 2 * HEADS:
                    exponentials(n + 2)
                if n + 1 < 2 * HEADS:
                    scale(n + 1)
                sc.wait_ge(pT_full, n + 1)
                if h >= 2:
                    sc.wait_ge(o_full, h - 1)
                copy(pT[:, h % 2, :, 128 * (n % 2):128 * (n % 2) + 128],
                     ps[:, 2 + n % 2, :].rearrange("p (k q) -> p k q", k=4)).then_inc(pT_out, 1)
                if n % 2 and h:
                    head_square(h - 1)
            head_square(HEADS - 1)
            square_root(rmla)
            for n in range(4):
                for t in range(2):
                    sc.wait_ge(h_part, 2 * n + t + 1)
                    if n:
                        sc.wait_ge(hsq, 2 * n + t - 1)
                    nc.scalar.activation(nreg[:, 1024 + 512 * t:1536 + 512 * t], xres[:, t, 512 * n:512 * n + 512],
                                         ACT.Square, accum_out=hsum[:, t, n:n + 1]).then_inc(hsq, 1)

            sc.wait_ge(root, 2)
            sc.wait_ge(mods_ready, 1)
            for n in range(4):
                nc.scalar.activation(xh[:, 1, 512 * n:512 * n + 512], xres[:, 1, 512 * n:512 * n + 512], ACT.Identity,
                                     scale=stat[:, 11:12]).then_inc(xh_act, 1)

            for b in range(0, 8, 2):
                sc.wait_ge(hT_full, b + 1)
                for k in (2 * b, 2 * b + 1):
                    ins = nc.scalar.activation(hT[:, k, :], ps[:, b % 4, T * (k % 2):T * (k % 2) + T], ACT.Identity,
                                               bias=modT[:, 3 * KC + k, 0:1], scale=amul2[:, k:k + 1])
                ins.then_inc(hT_act, 1)
            sc.wait_ge(hT_full, 8)
            sc.wait_ge(rt_rows, 1)
            copy(part[:, 0, 0:T], ps[:, 4, 0:T]).then_inc(rt_copied, 1)
            sc.wait_ge(rt_full, 1)
            nc.scalar.activation(sig[:, :, :], ps[:, 5, 0:64].rearrange("p (t e) -> p t e", t=2), ACT.Sigmoid)\
                .then_inc(rt_sig, 1)

            for t in range(2):
                copy(parts[0][:, t, :], xh[:, t, :]).then_inc(split_act, 1)

            for n in range(4):
                sc.wait_ge(sh_gate, n + 1)
                if n >= 2:
                    sc.wait_ge(sh_act, n - 1)
                nc.scalar.activation(shS[:, n % 2, :], ps[:, n % 2, 0:T], ACT.Silu).then_inc(sh_silu, 1)

            def tokens_out(t, b):
                sc.wait_ge(gx_full, 4 * t + (b + 1))
                for j in range(4):
                    k = 4 * b + j
                    ins = nc.scalar.activation(xg[:, k, :], ps[:, b % 2, 128 * j:128 * j + 128], ACT.Identity,
                                               bias=modT[:, 3 * KC + k, 0:1], scale=amul2[:, k:k + 1])
                ins.then_inc(gx_act, 1)

            def pair_pass(t, ahead=True):
                sc.wait_ge(pickT_full, t + 1)
                copy(pickT[:, :], ps[:, 3, 0:256]).then_inc(pickT_out, 1)
                sc.wait_ge(gu_full, t + 1)
                nc.scalar.activation(act[:, 0, :], ps[:, 2, 0:FF], ACT.Silu).then_inc(silu_done, 1)
                if ahead:
                    tokens_out(t + 1, 0)
                sc.wait_ge(actT_full, t + 1)
                copy(actT[:, :, :].rearrange("p k s -> p (k s)"), ps[:, 3, 256:512]).then_inc(actT_out, 1)
                if ahead:
                    tokens_out(t + 1, 2)
                for n in range(4):
                    sc.wait_ge(dn_full, 4 * t + (n + 1))
                    copy(ye[:, 512 * n:512 * n + 512], ps[:, 4 + n % 2, :]).then_inc(ye_out, 1)
                    if not ahead and n == 2:
                        final_squares(0)

            def final_squares(n):
                for t in range(2):
                    m = 2 * n + t
                    sc.wait_ge(fin_h, m + 1)
                    if m >= 4:
                        sc.wait_ge(fin_sq, m - 3)
                    nc.scalar.activation(nreg[:, 512 * (m % 4):512 * (m % 4) + 512], xres[:, t, 512 * n:512 * n + 512],
                                         ACT.Square, accum_out=finsum[:, t, n:n + 1]).then_inc(fin_sq, 1)

            passes = sc.alloc_register("act_passes")
            sc.reg_mov(passes, 0)
            sc.wait_ge(rank_ready, 1)
            tokens_out(0, 0)
            tokens_out(0, 2)

            def extra_passes(i):
                extra = sc.value_load(more[0:1, bass.ds(i, 1)], min_val=0, max_val=PASSES - 1)
                with sc.If(extra > 0):
                    with sc.Fori(0, extra):
                        pair_pass(sc.snap(passes, min_val=0, max_val=64))
                        sc.reg_add(passes, passes, 1)

            with sc.Fori(0, NE // 2 - 1) as i:
                extra_passes(i)
                pair_pass(sc.snap(passes, min_val=0, max_val=64))
                sc.reg_add(passes, passes, 1)
            extra_passes(NE // 2 - 1)
            pair_pass(sc.snap(passes, min_val=0, max_val=64), ahead=False)

            for n in range(1, 4):
                final_squares(n)
            sc.wait_ge(root, 3)
            for n in range(4):
                sc.wait_ge(fin_gain, n + 1)
                nc.scalar.activation(xres[:, 1, 512 * n:512 * n + 512], yacc[:, 1, 512 * n:512 * n + 512], ACT.Identity,
                                     scale=stat[:, 15:16]).then_inc(fin_act, 1)

        @block.vector
        def _(ve):
            V = nc.vector
            steps = [0]

            def link(ins):
                steps[0] += 1
                ins.then_inc(v_step, 1)
                ve.wait_ge(v_step, steps[0])

            roots = [0]
            wide = [0]

            def mean_square_wide(o, i_, n):
                V.tensor_scalar(o, i_, 1.0 / n, EPS, ALU.mult, ALU.add).then_inc(mean_wide, 1)
                wide[0] += 1

            def root_inverse_wide(o):
                ve.wait_ge(root_wide, wide[0])
                link(V.reciprocal(o, o))

            def rsqrt_wide(o, i_, n):
                mean_square_wide(o, i_, n)
                root_inverse_wide(o)

            def rsqrt(o, i_, n):
                V.tensor_scalar(o, i_, 1.0 / n, EPS, ALU.mult, ALU.add).then_inc(mean_sq, 1)
                roots[0] += 1
                ve.wait_ge(root, roots[0])

            ve.wait_ge(zeroed, 2)
            ve.wait_ge(small_T, 1)
            for v in range(2):
                V.tensor_copy(csT[:, :, v:v + 1], ps[:, 7, 16 * v:16 * v + 16].rearrange("p (c a) -> p c a", a=1))
            V.tensor_copy(vecT[:, :], ps[:, 7, 64:64 + NVEC])
            V.tensor_copy(bT[:, :], ps[:, 7, 256:352]).then_inc(small_done, 1)
            ve.wait_ge(small_done, 1)

            def cols_out(n, g, bank=5):
                ve.wait_ge(mod_cols, n + 1)
                V.tensor_reduce(modT[:, bass.ds(4 * g, 4), :],
                                ps[:, bank, :].rearrange("p (c q r) -> p c r q", c=4, q=4)[:, :, 0:2, :], AX.X, ALU.add)\
                    .then_inc(modT_done, 1)

            def accumulate(n, b, slots_=mslot, quarters=range(4)):
                acc = part[:, b, :]
                for q in quarters:
                    if q == 0:
                        ve.wait_ge(mod_cols, n - 1)
                    ve.wait_ge(m_full[q], 16 * (n - 1))
                    for k in range(4):
                        w, scale = slots_[q][:, k, :], csT[:, 4 * q + k, 0:1]
                        if q == k == 0:
                            ins = V.tensor_scalar(acc, w, scale, None, ALU.mult)
                        else:
                            ve.wait_ge(acc_done, 16 * (n - 8) + (4 * q + k))
                            ins = V.scalar_tensor_tensor(out=acc, in0=w, scalar=scale, in1=acc, op0=ALU.mult,
                                                         op1=ALU.add)
                        ins.then_inc(acc_done, 1)

            def sum_out(n, g):
                ve.wait_ge(mod_cols, n + 1)
                V.tensor_copy(modT[:, bass.ds(4 * g, 4), 0:1], ps[:, 5, 0:4].unsqueeze(2)).then_inc(modT_done, 1)

            def gate_out(n):
                gate, m = (gaB, n - ATT_GROUP) if n < OUT_GROUP else (gfB, n - OUT_GROUP)
                chunk = gate[:, 512 * m:512 * m + 512]
                ve.wait_ge(bias_in, 32)
                ve.wait_ge(mod_cols, n + 1)
                V.tensor_tensor(chunk, chunk, ps[:, 5, :], ALU.add).then_inc(modT_done, 1)

            ve.wait_ge(squares, 4)
            rsqrt(tiny[:, 8:12], stat[:, 0:4], D)
            for t in range(2):
                V.tensor_scalar(xs[:, t, :], xres[:, t, :], tiny[:, 8 + t:9 + t], None, ALU.mult).then_inc(xs_ready, 1)
            cols_out(0, MOD_ORDER[0], 7)

            for k in range(KC):
                ve.wait_ge(xT_full, k + 1)
                V.tensor_copy(nT[:, k, 0:T], ps[:, 2 * (k % 2), 0:T]).then_inc(xT_lat, 1)
            cols_out(1, MOD_ORDER[1], 7)
            ve.wait_ge(xT_lat, KC)
            for s in range(SETS):
                if s:
                    for n in (2 * s, 2 * s + 1):
                        cols_out(n, MOD_ORDER[n], 7)
                ve.wait_ge(modT_done, 2 * s + 2)
                for at in (4 * s, 4 * (s + 4)):
                    ins = V.tensor_tensor(modT[:, at:at + 4, :], modT[:, at:at + 4, :],
                                          bT[:, at:at + 4].unsqueeze(2).to_broadcast([P, 4, 2]), ALU.add)
                link(ins)
                V.scalar_tensor_tensor(out=amul[:, 4 * s:4 * s + 4, :], in0=modT[:, 16 + 4 * s:20 + 4 * s, :], scalar=1.0,
                                       in1=vecT[:, V_AN + 4 * s:V_AN + 4 * s + 4].unsqueeze(2).to_broadcast([P, 4, 2]),
                                       op0=ALU.add, op1=ALU.mult).then_inc(amul_ready, 1)
                ve.wait_ge(amul_ready, s + 1)
                for k in range(4 * s, 4 * s + 4):
                    V.tensor_scalar(nT[:, k, 0:T], nT[:, k, 0:T], amul[:, k, 0:1], modT[:, k, 0:1], ALU.mult, ALU.add)\
                        .then_inc(nT_lat, 1)

            for m in range(4):
                ve.wait_ge(q_sq, m + 1)
                V.tensor_scalar(qaT[:, m, :], ps[:, m, 0:T], vecT[:, V_QN + m:V_QN + m + 1], None, ALU.mult)\
                    .then_inc(q_out, 1)

            def kv_gain(m):
                ve.wait_ge(kv_sq, m + 1)
                V.tensor_scalar(kvT[:, m, :], ps[:, 4 + m, :], vecT[:, V_KN + m:V_KN + m + 1], None, ALU.mult)\
                    .then_inc(kv_out, 1)

            kv_gain(0)
            ve.wait_ge(stat_q, 1)
            mean_square_wide(rowq, ps[:, 7, 0:T], QL)
            ve.wait_ge(kr_mm, 1)
            V.tensor_copy(krT[:, T:2 * T], ps[:, 2, T:2 * T])
            link(V.tensor_tensor(krT[:, 0:T], ps[:, 2, 0:T], cosT, ALU.mult))
            link(V.tensor_tensor(krs[:, 0:T], ps[:, 3, 0:T], sinT, ALU.mult))
            V.tensor_tensor(krT[:, 0:T], krT[:, 0:T], krs[:, 0:T], ALU.add).then_inc(kr_done, 1)
            root_inverse_wide(rowq)
            kv_gain(1)
            ve.wait_ge(q_out, 4)
            for m in range(4):
                ins = V.tensor_tensor(qaT[:, m, :], qaT[:, m, :], rowq, ALU.mult)
            ins.then_inc(q_ready, 1)
            ve.wait_ge(stat_kv, 1)
            rsqrt_wide(rowkv, ps[:, 4, :], KVL)
            ve.wait_ge(kv_out, 2)
            for m in range(2):
                ins = V.tensor_tensor(kvT[:, m, :], kvT[:, m, :], rowkv, ALU.mult)
            ins.then_inc(kv_ready, 1)

            base, LINKS = steps[0], 3
            with ve.Fori(0, 4) as i:
                def tap(j, m):
                    return vecT[:, bass.ds(V_CW + 8 * j + m + 2 * i, 1)]

                accumulate(2 * i + 8, 0)
                accumulate(2 * i + 9, 1)
                for m in range(2):
                    ve.wait_ge(conv_full, 6 * i + 3 + m)
                    ve.wait_ge(gc_out, 2 * i + m + 1)
                    V.tensor_tensor(upad[:, m, 1:T + 1], ps[:, 2 + m, 0:T], gcs[:, m, :], ALU.mult).then_inc(u_out, 1)
                ve.wait_ge(u_out, 2 * i + 2)
                for m in range(2):
                    ins = V.tensor_scalar(ycv[:, m, :], upad[:, m, 1:T + 1], tap(1, m), None, ALU.mult)
                ins.then_inc(v_step, 1)
                ve.wait_ge(v_step, 3 * i + base + 1)
                for j in (0, 2):
                    for m in range(2):
                        ins = V.scalar_tensor_tensor(out=ycv[:, m, :], in0=upad[:, m, j:j + T], scalar=tap(j, m),
                                                     in1=ycv[:, m, :], op0=ALU.mult, op1=ALU.add)
                    ins.then_inc(v_step, 1)
                    ve.wait_ge(v_step, 3 * i + base + 2 + j // 2)
                sum_out(2 * i + 8, 2 * i + 12)
                for m in range(2):
                    ve.wait_ge(conv_full, 6 * i + 5 + m)
                    V.tensor_tensor(oT[:, bass.ds(8 + m + 2 * i, 1), :].rearrange("p a t -> p (a t)"), ps[:, BANKS_B[m], 0:T],
                                    ycv[:, m, :], ALU.mult).then_inc(y_out, 1)
                sum_out(2 * i + 9, 2 * i + 13)
            steps[0] += 4 * LINKS

            ve.wait_ge(modT_done, 16)
            link(V.tensor_tensor(modT[:, 48:80, 0:1], modT[:, 48:80, 0:1], bT[:, 48:80].unsqueeze(2), ALU.add))
            V.scalar_tensor_tensor(out=amul2[:, :].rearrange("p (c a) -> p c a", a=1), in0=modT[:, 64:80, 0:1], scalar=1.0,
                                   in1=vecT[:, V_FN:V_FN + KC].rearrange("p (c a) -> p c a", a=1),
                                   op0=ALU.add, op1=ALU.mult).then_inc(mods_ready, 1)

            def rope(p):
                ve.wait_ge(rot_full, p + 1)
                ve.wait_ge(proj_act, 3 * (p // 2) + p % 2 + 1)
                link(V.tensor_tensor(ycv[:, p % 2, :], ps[:, 6 + p % 2, 0:T], sinT, ALU.mult))
                link(V.tensor_tensor(qrT[:, p, :], qraw[:, p % 2, :], cosT, ALU.mult))
                V.tensor_tensor(qrT[:, p, :], qrT[:, p, :], ycv[:, p % 2, :], ALU.add).then_inc(qr_ready, 1)

            for j in range(1, 28, 2):
                ve.wait_ge(proj_full, j + 1)
                bank = ps[:, j % 4, :]
                if j < 12:
                    s, n = j // 6, j % 6
                    dst, src = qnT[:, 4 * s + {1: 0, 3: 1, 5: 3}[n], :], bank[:, 0:T]
                elif j < 20:
                    dst, src = knT[:, j - 12, :], bank
                else:
                    dst, src = vtok[:, (j - 20) // 2, 512:1024], bank
                V.tensor_copy(dst, src).then_inc(proj_dve, 1)
                if j in (5, 7, 11, 13):
                    rope({5: 0, 7: 1, 11: 2, 13: 3}[j])
                if j in (17, 19, 21, 23):
                    accumulate(ATT_GROUP, 0, aslot, ((j - 17) // 2,))
                if j == 25:
                    ve.wait_ge(csq_used, 8)
                    mean_square_wide(rconv, ps[:, 5, 0:T], CW)

            def maximum(n):
                ve.wait_ge(score_full, n + 1)
                b = n % 3
                link(V.tensor_reduce(rowmax[:, b:b + 1], ps[:, SCORE_BANK[b], :], AX.X, ALU.max))
                V.tensor_scalar(negmax[:, b:b + 1], rowmax[:, b:b + 1], -SCALE, None, ALU.mult).then_inc(neg_max, 1)

            def head_out(h):
                ve.wait_ge(o_full, h + 1)
                V.tensor_copy(oT[:, h, :], ps[:, 4, 0:T]).then_inc(o_out, 1)

            def invert(n):
                b = n % 3
                ve.wait_ge(exp_done, n + 1)
                if n >= 3:
                    ve.wait_ge(p_ready, n - 2)
                V.reciprocal(inverse[:, b:b + 1], rowsum[:, b:b + 1]).then_inc(inv_ready, 1)

            SCALED_AT = (1, 4, 7, 10, 12, 13, 14, 15)
            maximum(0)
            maximum(1)
            invert(0)
            root_inverse_wide(rconv)
            for n in range(2 * HEADS):
                if n + 1 < 2 * HEADS:
                    invert(n + 1)
                if n + 2 < 2 * HEADS:
                    maximum(n + 2)
                if n % 2 and n > 1:
                    head_out(n // 2 - 1)
                if n == 1:
                    gate_out(ATT_GROUP)
                elif n - 1 in SUM_AT:
                    gate_out(SUM_AT[n - 1])
                if n in SCALED_AT:
                    k = SCALED_AT.index(n)
                    V.scalar_tensor_tensor(out=oT[:, 8 + k, :], in0=oT[:, 8 + k, :], scalar=vecT[:, V_OC + k:V_OC + k + 1],
                                           in1=rconv, op0=ALU.mult, op1=ALU.mult).then_inc(oc_ready, 1)
                if n in QUARTER_AT:
                    g, q = QUARTER_AT[n]
                    accumulate(g, g % 2, aslot, (q,))
            head_out(HEADS - 1)

            ve.wait_ge(msq_used, 8)
            rsqrt_wide(rmla, ps[:, 7, 0:T], HEADS * VD)
            for k in range(8):
                V.scalar_tensor_tensor(out=oT[:, k, :], in0=oT[:, k, :], scalar=vecT[:, V_OM + k:V_OM + k + 1],
                                       in1=rmla, op0=ALU.mult, op1=ALU.mult).then_inc(om_ready, 1)

            ve.wait_ge(modT_done, ATT_GROUP + 3)
            for n in range(4):
                for g in ((19, 20), (21,), (22,), (23,))[n]:
                    accumulate(g, g % 2)
                if n == 3:
                    ve.wait_ge(modT_done, OUT_GROUP)
                ve.wait_ge(wo_full, n + 1)
                for t in range(2):
                    tmp = nreg[:, 512 * t:512 * t + 512]
                    link(V.tensor_tensor(tmp, ps[:, 2 * (n % 2) + t, :], gaB[:, 512 * n:512 * n + 512], ALU.mult))
                    V.tensor_tensor(xres[:, t, 512 * n:512 * n + 512], xres[:, t, 512 * n:512 * n + 512], tmp, ALU.add)\
                        .then_inc(h_part, 1)
                for g in ((19, 20), (21,), (22,), ())[n]:
                    gate_out(g)

            ve.wait_ge(hsq, 8)
            link(V.tensor_reduce(stat[:, 8:10], hsum, AX.X, ALU.add))
            V.tensor_scalar(stat[:, 10:12], stat[:, 8:10], 1.0 / D, EPS, ALU.mult, ALU.add).then_inc(mean_sq, 1)
            roots[0] += 1
            ve.wait_ge(root, roots[0])
            ve.wait_ge(mods_ready, 1)
            for n in range(4):
                V.tensor_scalar(xh[:, 0, 512 * n:512 * n + 512], xres[:, 0, 512 * n:512 * n + 512], stat[:, 10:11], None,
                                ALU.mult).then_inc(xh_ready, 1)
            gate_out(OUT_GROUP + 3)
            for b in range(1, 8, 2):
                ve.wait_ge(hT_full, b + 1)
                for k in (2 * b, 2 * b + 1):
                    ins = V.tensor_scalar(hT[:, k, :], ps[:, b % 4, T * (k % 2):T * (k % 2) + T], amul2[:, k:k + 1],
                                          modT[:, 3 * KC + k, 0:1], ALU.mult, ALU.add)
                ins.then_inc(hT_dve, 1)

            ve.wait_ge(rt_sig, 1)
            link(V.tensor_tensor(sel[:, :, :], sig[:, :, :], rb[:, :].unsqueeze(1).to_broadcast([P, 2, NE]), ALU.add))
            for t in range(2):
                for g in range(NG):
                    ins = V.max(top8[:, 4 * t + g, :], sel[:, t, 8 * g:8 * g + 8])
            link(ins)
            gs = tiny[:, 32:40].rearrange("p (t g) -> p t g", t=2)
            link(V.tensor_tensor(gs.unsqueeze(3), top8[:, 0:8, 0:1].rearrange("p (t g) a -> p t g a", t=2),
                                 top8[:, 0:8, 1:2].rearrange("p (t g) a -> p t g a", t=2), ALU.add))
            above = tiny[:, 40:72].rearrange("p (t g a) -> p t g a", t=2, g=NG)
            same = tiny[:, 72:104].rearrange("p (t g a) -> p t g a", t=2, g=NG)
            other = gs.unsqueeze(2).to_broadcast([P, 2, NG, NG])
            own = gs.unsqueeze(3).to_broadcast([P, 2, NG, NG])
            V.tensor_tensor(above, other, own, ALU.is_gt)
            link(V.tensor_tensor(same, other, own, ALU.is_equal))
            link(V.tensor_tensor(same, same, low.unsqueeze(1).to_broadcast([P, 2, NG, NG]), ALU.mult))
            link(V.tensor_tensor(above, above, same, ALU.add))
            link(V.tensor_reduce(tiny[:, 104:112].rearrange("p (t g) -> p t g", t=2), above, AX.X, ALU.add))
            link(V.tensor_scalar(tiny[:, 112:120], tiny[:, 104:112], 1.5, -BIG, ALU.is_gt, ALU.mult))
            gm = tiny[:, 104:112]
            link(V.tensor_scalar(gm, tiny[:, 104:112], 1.5, None, ALU.is_lt))
            link(V.tensor_tensor(sel[:, :, :].rearrange("p t (g e) -> p t g e", g=NG),
                                 sel[:, :, :].rearrange("p t (g e) -> p t g e", g=NG),
                                 gm.rearrange("p (t g) -> p t g", t=2).unsqueeze(3).to_broadcast([P, 2, NG, 8]), ALU.mult))
            link(V.tensor_tensor(sel[:, :, :].rearrange("p t (g e) -> p t g e", g=NG),
                                 sel[:, :, :].rearrange("p t (g e) -> p t g e", g=NG),
                                 tiny[:, 112:120].rearrange("p (t g) -> p t g", t=2).unsqueeze(3)
                                 .to_broadcast([P, 2, NG, 8]), ALU.add))
            for t in range(2):
                ins = V.max(top8[:, 8 + t, :], sel[:, t, :])
            link(ins)
            for t in range(2):
                last_ = top8[:, 8 + t, TOP_K - 1:TOP_K]
                V.tensor_scalar(mask[:, t, :], sel[:, t, :], last_, None, ALU.is_gt)
                ins = V.tensor_scalar(scan[:, 0, t, :], sel[:, t, :], last_, None, ALU.is_equal)
            link(ins)
            V.tensor_copy(sel[:, :, :], scan[:, 0, :, :])
            link(V.tensor_reduce(tiny[:, 120:122], mask[:, :, :], AX.X, ALU.add))
            for n, d in enumerate((1, 2, 4, 8, 16)):
                a, b = scan[:, n % 2, :, :], scan[:, (n + 1) % 2, :, :]
                V.tensor_copy(b[:, :, 0:d], a[:, :, 0:d])
                link(V.tensor_tensor(b[:, :, d:NE], a[:, :, d:NE], a[:, :, 0:NE - d], ALU.add))
            link(V.tensor_tensor(scan[:, 1, :, :], scan[:, 1, :, :], tiny[:, 120:122].unsqueeze(2).to_broadcast([P, 2, NE]),
                                 ALU.add))
            link(V.tensor_scalar(scan[:, 1, :, :], scan[:, 1, :, :], TOP_K + 0.5, None, ALU.is_lt))
            link(V.tensor_tensor(sel[:, :, :], sel[:, :, :], scan[:, 1, :, :], ALU.mult))
            V.tensor_tensor(mask[:, :, :], mask[:, :, :], sel[:, :, :], ALU.add).then_inc(mask_ready, 1)
            ve.wait_ge(mask_ready, 1)
            link(V.tensor_tensor(comb[:, :, :], sig[:, :, :], mask[:, :, :], ALU.mult))
            link(V.tensor_reduce(tiny[:, 124:126], comb[:, :, :], AX.X, ALU.add))
            link(V.reciprocal(tiny[:, 126:128], tiny[:, 124:126]))
            for t in range(2):
                ins = V.tensor_scalar(comb[:, t, :], comb[:, t, :], tiny[:, 126 + t:127 + t], ROUTED_SCALE, ALU.mult, ALU.mult)
            link(ins)
            def shared_act(u):
                for m in range(2):
                    n = 2 * u + m
                    ve.wait_ge(sh_up, n + 1)
                    ve.wait_ge(sh_silu, n + 1)
                    if u:
                        ve.wait_ge(sh_down, 8)
                    V.tensor_tensor(shT[:, m, :], ps[:, 2 + m, 0:T], shS[:, m, :], ALU.mult).then_inc(sh_act, 1)

            def shared_out(u):
                for j in range(8):
                    t, m = j // 4, j % 4
                    ve.wait_ge(sh_down, 8 * u + j + 1)
                    y = yacc[:, t, 512 * m:512 * m + 512]
                    if u == 0:
                        V.tensor_copy(y, ps[:, 4 + m, :]).then_inc(y_add, 1)
                    else:
                        ve.wait_ge(y_add, j + 1)
                        V.tensor_tensor(y, y, ps[:, 4 + m, :], ALU.add).then_inc(y_add, 1)

            shared_act(0)
            shared_out(0)

            for t in range(2):
                ve.wait_ge(split_act, t + 1)
                link(V.tensor_tensor(xh[:, t, :], xh[:, t, :], parts[0][:, t, :], ALU.subtract))
                link(V.tensor_copy(parts[1][:, t, :], xh[:, t, :]))
                V.tensor_tensor(parts[2][:, t, :], xh[:, t, :], parts[1][:, t, :], ALU.subtract).then_inc(split_ready, 1)

            ve.wait_ge(rank_full, 1)
            cnt = scan[:, 0, 0, :]
            V.tensor_copy(cnt, ps[:, 5, 64:96])
            link(V.scalar_tensor_tensor(out=rank[:, 0, :, :], in0=ps[:, 5, 0:64].rearrange("p (t e) -> p t e", t=2),
                                        scalar=1.0, in1=mask[:, :, :], op0=ALU.add, op1=ALU.mult))
            link(V.tensor_scalar(rank[:, 0, :, :], rank[:, 0, :, :], -1.0, None, ALU.add))
            for n in range(1, PASSES):
                V.tensor_scalar(rank[:, n, :, :], rank[:, 0, :, :], -float(SLOTS * n), None, ALU.add)
            pairs = cnt.rearrange("p (i u) -> p i u", u=2)
            big = scan[:, 0, 1, 0:16]
            link(V.tensor_tensor(big.unsqueeze(2), pairs[:, :, 0:1], pairs[:, :, 1:2], ALU.max))
            acc, one = scan[:, 1, 0, 0:16], scan[:, 1, 1, 0:16]
            link(V.tensor_scalar(acc, big, SLOTS + 0.5, None, ALU.is_gt))
            for n in range(2, PASSES):
                link(V.tensor_scalar(one, big, SLOTS * n + 0.5, None, ALU.is_gt))
                link(V.tensor_tensor(acc, acc, one, ALU.add))
            V.tensor_copy(more[:, :], acc).then_inc(rank_ready, 1)

            slots = rank[:, :, :, :].rearrange("p n t e -> p (n t e)")
            weights = comb[:, :, :].rearrange("p t e -> p (t e)")

            def picks(i, n):
                for j in range(2):
                    for u in range(2):
                        ins = V.tensor_scalar(pick[:, j, 64 * u:64 * u + 64], iota,
                                              slots[:, bass.ds(n * (2 * NE) + j * NE + 2 * i + u, 1)], None, ALU.is_equal)
                ins.then_inc(pick_ready, 1)

            def weighted_picks(i, n):
                for j in range(2):
                    for u in range(2):
                        ins = V.tensor_scalar(pickw[:, j, 64 * u:64 * u + 64], iota,
                                              slots[:, bass.ds(n * (2 * NE) + j * NE + 2 * i + u, 1)],
                                              weights[:, bass.ds(j * NE + 2 * i + u, 1)], ALU.is_equal, ALU.mult)
                ins.then_inc(pickw_ready, 1)

            def tokens_out(t, b):
                ve.wait_ge(gx_full, 4 * t + (b + 1))
                for j in range(4):
                    k = 4 * b + j
                    ins = V.tensor_scalar(xg[:, k, :], ps[:, b % 2, 128 * j:128 * j + 128], amul2[:, k:k + 1],
                                          modT[:, 3 * KC + k, 0:1], ALU.mult, ALU.add)
                ins.then_inc(gx_dve, 1)

            def pair_pass(t, ahead):
                if ahead:
                    picks(*ahead)
                    ve.wait_ge(pickT_full, t + 1)
                    weighted_picks(*ahead)
                ve.wait_ge(silu_done, t + 1)
                V.tensor_tensor(act[:, 1, :], ps[:, 2, FF:2 * FF], act[:, 0, :], ALU.mult).then_inc(act_ready, 1)
                if ahead:
                    tokens_out(t + 1, 1)
                    tokens_out(t + 1, 3)
                for q in range(4):
                    cols = slice(512 * q, 512 * q + 512)
                    ve.wait_ge(sc_full, 4 * t + (q + 1))
                    for h in range(2):
                        V.tensor_tensor(yacc[:, h, cols], yacc[:, h, cols], ps[:, 6 + h, :], ALU.add).then_inc(y_add, 1)
                    if not ahead:
                        ve.wait_ge(y_add, 8 * t + (2 * q + 18))
                        for h in range(2):
                            ins = V.tensor_tensor(yacc[:, h, cols], yacc[:, h, cols], gfB[:, cols], ALU.mult)
                        link(ins)
                        for h in range(2):
                            V.tensor_tensor(xres[:, h, cols], xres[:, h, cols], yacc[:, h, cols], ALU.add)\
                                .then_inc(fin_h, 1)
                ve.wait_ge(y_add, 8 * t + 24)

            passes = ve.alloc_register("dve_passes")
            ve.reg_mov(passes, 0)
            left = ve.alloc_register("dve_left")
            ve.wait_ge(rank_ready, 1)

            def extra_of(i):
                return ve.value_load(more[0:1, bass.ds(i, 1)], min_val=0, max_val=PASSES - 1)

            first = extra_of(0)
            picks(0, first)
            weighted_picks(0, first)
            shared_act(1)
            tokens_out(0, 1)
            shared_out(1)
            tokens_out(0, 3)
            ve.wait_ge(y_add, 16)

            def extra_passes(i):
                extra = extra_of(i)
                with ve.If(extra > 0):
                    ve.reg_mov(left, extra)
                    with ve.Fori(0, extra):
                        ve.reg_add(left, left, -1)
                        pair_pass(ve.snap(passes, min_val=0, max_val=64), (i, ve.snap(left, min_val=0, max_val=PASSES - 2)))
                        ve.reg_add(passes, passes, 1)

            with ve.Fori(0, NE // 2 - 1) as i:
                extra_passes(i)
                pair_pass(ve.snap(passes, min_val=0, max_val=64), (i + 1, extra_of(i + 1)))
                ve.reg_add(passes, passes, 1)
            extra_passes(NE // 2 - 1)
            ve.wait_ge(modT_done, 24)
            pair_pass(ve.snap(passes, min_val=0, max_val=64), None)

            ve.wait_ge(fin_sq, 8)
            link(V.tensor_reduce(stat[:, 12:14], finsum, AX.X, ALU.add))
            rsqrt(stat[:, 14:16], stat[:, 12:14], D)
            ve.wait_ge(gain_in, 16)
            for n in range(4):
                cols = slice(512 * n, 512 * n + 512)
                V.scalar_tensor_tensor(out=xres[:, 0, cols], in0=xres[:, 0, cols], scalar=stat[:, 14:15],
                                       in1=gainB[:, cols], op0=ALU.mult, op1=ALU.mult).then_inc(fin_dve, 1)


_INS = ["x", "c", "ctx", "c_ctx", "w_mod", "b_mod", "attn_norm", "w_in", "q_a_norm", "w_q_b", "kv_a_norm", "w_kv_b",
        "conv_w", "o_norm_mla", "o_norm_conv", "w_out", "ffn_norm", "w_router", "router_bias",
        "w_exp_gate", "w_exp_up", "w_exp_down", "w_sh_gate", "w_sh_up", "w_sh_down", "final_norm"]


def kernel(**inputs):
    import concourse.bacc as _bacc
    from concourse.bass_utils import run_bass_kernel_spmd as _run

    nc = _bacc.Bacc("TRN2", target_bir_lowering=False, num_devices=1)
    arrays = {f"in_{name}": np.ascontiguousarray(inputs[name]) for name in _INS}
    arrays["in_consts"] = constants()
    args = [nc.dram_tensor(name, a.shape, F32, kind="ExternalInput").ap() for name, a in arrays.items()]
    args.append(nc.dram_tensor("out", (1, T, D), F32, kind="ExternalOutput").ap())
    block_kernel(nc, *args)
    r = _run(nc, [arrays], core_ids=[0])
    return r.results[0]["out"]
```
